# Optimizing a Trainium2 kernel written in Bass

```python
import jax, jax.numpy as jnp
from jax import lax
import numpy as np
import math

D_MODEL = 1024
BATCH = 1
SEQ = 2048
DEPTH = 1

D_MIX = D_MODEL
D_RET = D_MIX // 2
D_POOL = D_MIX - D_RET
RET_HEADS = 8
RET_HEAD_DIM = D_RET // RET_HEADS
RET_CHUNK = 128
ROPE_BASE = 10000.0
POOL_WINDOWS = (2, 4, 8, 16)
POOL_GROUPS = len(POOL_WINDOWS)
POOL_GROUP_DIM = D_POOL // POOL_GROUPS
D_IN_PROJ = 4 * D_RET + D_POOL
N_EXPERTS = 32
TOP_K = 4
D_EXPERT = D_MODEL
SWIGLU_LIMIT = 7.0
SWIGLU_ALPHA = 1.702
PLE_DIM = 256
NORM_EPS = 1e-5
GN_EPS = 1e-5


def rms_norm(x, g):
    xf = x.astype(jnp.float32)
    y = xf * lax.rsqrt(jnp.mean(xf * xf, axis=-1, keepdims=True) + NORM_EPS)
    return (y * g.astype(jnp.float32)).astype(x.dtype)

def rope(x, positions):
    half = x.shape[-1] // 2
    inv_freq = ROPE_BASE ** (-jnp.arange(half, dtype=jnp.float32) / half)
    ang = positions.astype(jnp.float32)[..., None] * inv_freq
    cos = jnp.cos(ang)[:, :, None, :]
    sin = jnp.sin(ang)[:, :, None, :]
    xf = x.astype(jnp.float32)
    x1, x2 = xf[..., :half], xf[..., half:]
    out = jnp.concatenate([x1 * cos - x2 * sin, x2 * cos + x1 * sin], axis=-1)
    return out.astype(x.dtype)

def retention(q, k, v, gn_w):
    B, S, H, d = q.shape
    C = RET_CHUNK
    N = S // C
    log_gamma = jnp.log1p(-jnp.power(2.0, -5.0 - jnp.arange(H, dtype=jnp.float32)))
    qc = q.reshape(B, N, C, H, d)
    kc = (k * (d ** -0.5)).reshape(B, N, C, H, d)
    vc = v.reshape(B, N, C, H, d)
    idx = jnp.arange(C, dtype=jnp.float32)
    rel = idx[:, None] - idx[None, :]
    causal = rel >= 0
    decay = jnp.where(causal[None], jnp.exp(jnp.where(causal, rel, 0.0)[None] * log_gamma[:, None, None]), 0.0)
    scores = jnp.einsum('bnchd,bnmhd->bnhcm', qc, kc) * decay
    intra = jnp.einsum('bnhcm,bnmhd->bnchd', scores, vc)
    zeta = jnp.exp((C - 1 - idx)[None, :] * log_gamma[:, None])
    kv = jnp.einsum('bnmhd,hm,bnmhe->bnhde', kc, zeta, vc)
    chunk_decay = jnp.exp(C * log_gamma)[:, None, None]

    def step(state, kv_i):
        return chunk_decay * state + kv_i, state

    init = jnp.zeros((B, H, d, d), dtype=kv.dtype)
    _, states = lax.scan(step, init, jnp.moveaxis(kv, 1, 0))
    states = jnp.moveaxis(states, 0, 1)
    xi = jnp.exp((idx + 1.0)[None, :] * log_gamma[:, None])
    cross = jnp.einsum('bnchd,bnhde,hc->bnche', qc, states, xi)
    y = (intra + cross).reshape(B, S, H, d).astype(jnp.float32)
    mu = jnp.mean(y, axis=-1, keepdims=True)
    var = jnp.mean(jnp.square(y - mu), axis=-1, keepdims=True)
    y = (y - mu) * lax.rsqrt(var + GN_EPS)
    y = y.reshape(B, S, H * d) * gn_w.astype(jnp.float32)
    return y.astype(q.dtype)

def pool_mixer(u, w_pool, pool_scale):
    B, S, _ = u.shape
    ug = u.reshape(B, S, POOL_GROUPS, POOL_GROUP_DIM).astype(jnp.float32)
    P = jnp.pad(jnp.cumsum(ug, axis=1), ((0, 0), (1, 0), (0, 0), (0, 0)))
    t = jnp.arange(S, dtype=jnp.float32)
    outs = []
    for gi, w in enumerate(POOL_WINDOWS):
        Pg = P[:, :, gi]
        lag = jnp.pad(Pg, ((0, 0), (w, 0), (0, 0)))[:, :S + 1]
        window_sum = Pg[:, 1:] - lag[:, 1:]
        count = jnp.minimum(t + 1.0, float(w))
        outs.append(window_sum / count[None, :, None] - ug[:, :, gi])
    pooled = jnp.stack(outs, axis=2).astype(u.dtype)
    mixed = jnp.einsum('bsgc,gcd->bsgd', pooled, w_pool)
    return mixed.reshape(B, S, D_POOL) * pool_scale

def moe(hn, router_w, router_b, w_gu, b_gu, w_down, b_down):
    B, S, D = hn.shape
    xt = hn.reshape(-1, D)
    logits = xt.astype(jnp.float32) @ router_w.astype(jnp.float32) + router_b.astype(jnp.float32)
    top_vals, top_idx = lax.top_k(logits, TOP_K)
    gates = jax.nn.softmax(top_vals, axis=-1)
    flat_e = top_idx.reshape(-1)
    order = jnp.argsort(flat_e)
    sorted_e = flat_e[order]
    tok = order // TOP_K
    xs = xt[tok]
    group_sizes = jnp.bincount(flat_e, length=N_EXPERTS).astype(jnp.int32)
    gu = lax.ragged_dot(xs, w_gu, group_sizes) + b_gu[sorted_e]
    gate = jnp.minimum(gu[:, ::2], SWIGLU_LIMIT)
    up = jnp.clip(gu[:, 1::2], -SWIGLU_LIMIT, SWIGLU_LIMIT)
    act = (up + 1.0) * (gate * jax.nn.sigmoid(SWIGLU_ALPHA * gate))
    y = lax.ragged_dot(act.astype(w_down.dtype), w_down, group_sizes) + b_down[sorted_e]
    y = y * gates.reshape(-1)[order][:, None].astype(y.dtype)
    out = jnp.zeros_like(xt).at[tok].add(y.astype(xt.dtype))
    return out.reshape(B, S, D)

def first_inputs(seed: int = 0) -> dict:
    key = jax.random.key(seed)
    ks = jax.random.split(key, 24)
    f32 = jnp.float32
    L = DEPTH

    def nrm(k, shape, scale):
        return jax.random.normal(k, shape, dtype=f32) * scale

    offsets = jax.random.randint(ks[2], (BATCH, 1), 0, 1024, dtype=jnp.int32)
    positions = (jnp.arange(SEQ, dtype=jnp.int32)[None, :] + offsets).astype(jnp.int32)
    return {
        "x": nrm(ks[0], (BATCH, SEQ, D_MODEL), 1.0),
        "p": nrm(ks[1], (DEPTH, BATCH, SEQ, PLE_DIM), 1.0),
        "positions": positions,
        "w_in": nrm(ks[3], (L, D_MODEL, D_IN_PROJ), D_MODEL ** -0.5),
        "w_out": nrm(ks[4], (L, D_MIX, D_MODEL), D_MIX ** -0.5),
        "ret_gn_w": 1.0 + nrm(ks[5], (L, D_RET), 0.02),
        "pool_w": nrm(ks[6], (L, POOL_GROUPS, POOL_GROUP_DIM, POOL_GROUP_DIM), POOL_GROUP_DIM ** -0.5),
        "pool_scale": 1.0 + nrm(ks[7], (L, D_POOL), 0.02),
        "norm_mix_w": 1.0 + nrm(ks[8], (L, D_MODEL), 0.02),
        "norm_moe_w": 1.0 + nrm(ks[9], (L, D_MODEL), 0.02),
        "router_w": nrm(ks[10], (L, D_MODEL, N_EXPERTS), D_MODEL ** -0.5),
        "router_b": nrm(ks[11], (L, N_EXPERTS), 0.01),
        "expert_w_gate_up": nrm(ks[12], (L, N_EXPERTS, D_MODEL, 2 * D_EXPERT), D_MODEL ** -0.5),
        "expert_b_gate_up": nrm(ks[13], (L, N_EXPERTS, 2 * D_EXPERT), 0.02),
        "expert_w_down": nrm(ks[14], (L, N_EXPERTS, D_EXPERT, D_MODEL), D_EXPERT ** -0.5),
        "expert_b_down": nrm(ks[15], (L, N_EXPERTS, D_MODEL), 0.02),
        "norm_ple_w": 1.0 + nrm(ks[16], (L, D_MODEL), 0.02),
        "ple_gate_w": nrm(ks[17], (L, D_MODEL, D_MODEL), D_MODEL ** -0.5),
        "ple_proj_w": nrm(ks[18], (L, PLE_DIM, D_MODEL), PLE_DIM ** -0.5),
        "final_norm_w": 1.0 + nrm(ks[19], (D_MODEL,), 0.02),
    }

def first_block(x, p, positions, w_in, w_out, ret_gn_w, pool_w, pool_scale, norm_mix_w,
              norm_moe_w, router_w, router_b, expert_w_gate_up, expert_b_gate_up,
              expert_w_down, expert_b_down, norm_ple_w, ple_gate_w, ple_proj_w, final_norm_w):
    B, S, _ = x.shape
    h = x
    for l in range(DEPTH):
        hn = rms_norm(h, norm_mix_w[l])
        proj = hn @ w_in[l]
        q = proj[..., 0 * D_RET:1 * D_RET].reshape(B, S, RET_HEADS, RET_HEAD_DIM)
        k = proj[..., 1 * D_RET:2 * D_RET].reshape(B, S, RET_HEADS, RET_HEAD_DIM)
        v = proj[..., 2 * D_RET:3 * D_RET].reshape(B, S, RET_HEADS, RET_HEAD_DIM)
        g = proj[..., 3 * D_RET:4 * D_RET]
        u = proj[..., 4 * D_RET:]
        q = rope(q, positions)
        k = rope(k, positions)
        ret = jax.nn.silu(g) * retention(q, k, v, ret_gn_w[l])
        pool = pool_mixer(u, pool_w[l], pool_scale[l])
        h = h + jnp.concatenate([ret, pool], axis=-1) @ w_out[l]
        h = h + moe(rms_norm(h, norm_moe_w[l]), router_w[l], router_b[l],
                    expert_w_gate_up[l], expert_b_gate_up[l], expert_w_down[l], expert_b_down[l])
        gate = jax.nn.sigmoid(rms_norm(h, norm_ple_w[l]) @ ple_gate_w[l])
        h = h + gate * (p[l] @ ple_proj_w[l])
    return rms_norm(h, final_norm_w)


D_MIX_2 = D_MODEL
ATTN_WIDTH = D_MIX_2 // 2
SSM_WIDTH = D_MIX_2 - ATTN_WIDTH
QK_NOPE_DIM = 128
QK_ROPE_DIM = 64
V_HEAD_DIM = 128
N_ATTN_HEADS = ATTN_WIDTH // V_HEAD_DIM
Q_RANK = D_MODEL // 4
KV_RANK = D_MODEL // 8
ROPE_THETA = 10000.0
Q_BLOCK = 128
SSM_GROUP_CH = 16
SSM_GROUPS = SSM_WIDTH // SSM_GROUP_CH
SSM_STATE = 64
DT_MIN = 1e-3
DT_MAX = 1e-1
EPS = 1e-6
SPLITS = (Q_RANK, KV_RANK, QK_ROPE_DIM, ATTN_WIDTH, SSM_WIDTH, SSM_WIDTH)
D_IN = sum(SPLITS)


def _rms_norm(x, g):
    xf = x.astype(jnp.float32)
    y = xf * lax.rsqrt(jnp.mean(xf * xf, axis=-1, keepdims=True) + EPS)
    return (y * g.astype(jnp.float32)).astype(x.dtype)

def _rope_tables(positions, dim):
    inv_freq = ROPE_THETA ** (-jnp.arange(0, dim, 2, dtype=jnp.float32) / dim)
    ang = positions.astype(jnp.float32)[..., None] * inv_freq
    return jnp.cos(ang), jnp.sin(ang)

def _apply_rope(t, cos, sin):
    tf = t.astype(jnp.float32)
    t1, t2 = jnp.split(tf, 2, axis=-1)
    return jnp.concatenate([t1 * cos - t2 * sin, t1 * sin + t2 * cos], axis=-1).astype(t.dtype)

def _mla_attention(z_q, z_kv, z_kr, positions, q_norm_g, w_uq, kv_norm_g, w_ukv):
    bsz, seq, _ = z_q.shape
    q = (_rms_norm(z_q, q_norm_g) @ w_uq).reshape(bsz, seq, N_ATTN_HEADS, QK_NOPE_DIM + QK_ROPE_DIM)
    q_nope, q_rope = q[..., :QK_NOPE_DIM], q[..., QK_NOPE_DIM:]
    kv = (_rms_norm(z_kv, kv_norm_g) @ w_ukv).reshape(bsz, seq, N_ATTN_HEADS, QK_NOPE_DIM + V_HEAD_DIM)
    k_nope, v = kv[..., :QK_NOPE_DIM], kv[..., QK_NOPE_DIM:]
    cos, sin = _rope_tables(positions, QK_ROPE_DIM)
    q_rope = _apply_rope(q_rope, cos[:, :, None, :], sin[:, :, None, :])
    k_rope = _apply_rope(z_kr, cos, sin)
    n_blocks = seq // Q_BLOCK
    scale = (QK_NOPE_DIM + QK_ROPE_DIM) ** -0.5

    def to_blocks(t):
        return t.reshape(bsz, n_blocks, Q_BLOCK, *t.shape[2:]).swapaxes(0, 1)

    def attend_block(args):
        qn, qr = args
        s = (jnp.einsum('bqhd,bkhd->bhqk', qn, k_nope, preferred_element_type=jnp.float32)
             + jnp.einsum('bqhr,bkr->bhqk', qr, k_rope, preferred_element_type=jnp.float32))
        p = jax.nn.softmax(s * scale, axis=-1).astype(v.dtype)
        return jnp.einsum('bhqk,bkhd->bqhd', p, v)

    o = lax.map(attend_block, (to_blocks(q_nope), to_blocks(q_rope)))
    return o.swapaxes(0, 1).reshape(bsz, seq, N_ATTN_HEADS * V_HEAD_DIM)

def _diag_scan_op(e_i, e_j):
    a_i, b_i = e_i
    a_j, b_j = e_j
    return a_j * a_i, a_j * b_i + b_j

def _s5_bidirectional(u, lam_re, lam_im, log_dt, b_re, b_im, c_re, c_im, d_skip):
    bsz, seq, _ = u.shape
    u_t = u.astype(jnp.float32).reshape(bsz, seq, SSM_GROUPS, SSM_GROUP_CH).transpose(1, 0, 2, 3)
    u_c = u_t.astype(jnp.complex64)
    y = jnp.zeros_like(u_t)
    for direction, reverse in ((0, False), (1, True)):
        lam = lax.complex(jnp.minimum(lam_re[direction].astype(jnp.float32), -1e-4),
                          lam_im[direction].astype(jnp.float32))
        dt = jnp.exp(log_dt[direction].astype(jnp.float32))[:, None]
        lam_bar = jnp.exp(lam * dt)
        b = lax.complex(b_re[direction].astype(jnp.float32), b_im[direction].astype(jnp.float32))
        b_bar = ((lam_bar - 1.0) / lam)[..., None] * b
        c = lax.complex(c_re[direction].astype(jnp.float32), c_im[direction].astype(jnp.float32))
        bu = jnp.einsum('sbgh,gph->sbgp', u_c, b_bar)
        a = jnp.broadcast_to(lam_bar, (seq, 1, SSM_GROUPS, SSM_STATE))
        _, h = lax.associative_scan(_diag_scan_op, (a, bu), reverse=reverse, axis=0)
        y = y + jnp.real(jnp.einsum('sbgp,ghp->sbgh', h, c))
    y = y + d_skip.astype(jnp.float32).reshape(SSM_GROUPS, SSM_GROUP_CH) * u_t
    return y.transpose(1, 0, 2, 3).reshape(bsz, seq, SSM_WIDTH).astype(u.dtype)

def second_inputs(seed: int = 0) -> dict:
    key = jax.random.key(seed)
    ks = jax.random.split(key, 24)
    f32 = jnp.float32
    L, G, P, H = DEPTH, SSM_GROUPS, SSM_STATE, SSM_GROUP_CH

    def nrm(k, shape, std):
        return jax.random.normal(k, shape, f32) * std

    def gain(k, n):
        return 1.0 + 0.05 * jax.random.normal(k, (L, n), f32)

    x = jax.random.normal(ks[0], (BATCH, SEQ, D_MODEL), f32)
    inc = jax.random.randint(ks[1], (BATCH, SEQ), 1, 3, dtype=jnp.int32)
    positions = jnp.cumsum(inc, axis=1, dtype=jnp.int32) - 1
    n_idx = jnp.arange(P, dtype=f32)
    lam_re = -0.5 + 0.01 * jax.random.normal(ks[2], (L, 2, G, P), f32)
    lam_im = math.pi * n_idx + 0.01 * jax.random.normal(ks[3], (L, 2, G, P), f32)
    log_dt = jax.random.uniform(ks[4], (L, 2, G), f32, math.log(DT_MIN), math.log(DT_MAX))
    return {
        "x": x,
        "positions": positions,
        "pre_norm_g": gain(ks[5], D_MODEL),
        "w_in": nrm(ks[6], (L, D_MODEL, D_IN), D_MODEL ** -0.5),
        "q_norm_g": gain(ks[7], Q_RANK),
        "w_uq": nrm(ks[8], (L, Q_RANK, N_ATTN_HEADS * (QK_NOPE_DIM + QK_ROPE_DIM)), Q_RANK ** -0.5),
        "kv_norm_g": gain(ks[9], KV_RANK),
        "w_ukv": nrm(ks[10], (L, KV_RANK, N_ATTN_HEADS * (QK_NOPE_DIM + V_HEAD_DIM)), KV_RANK ** -0.5),
        "attn_out_g": gain(ks[11], ATTN_WIDTH),
        "s5_lam_re": lam_re,
        "s5_lam_im": lam_im,
        "s5_log_dt": log_dt,
        "s5_b_re": nrm(ks[12], (L, 2, G, P, H), (2.0 * H) ** -0.5),
        "s5_b_im": nrm(ks[13], (L, 2, G, P, H), (2.0 * H) ** -0.5),
        "s5_c_re": nrm(ks[14], (L, 2, G, H, P), (2.0 * P) ** -0.5),
        "s5_c_im": nrm(ks[15], (L, 2, G, H, P), (2.0 * P) ** -0.5),
        "s5_d": nrm(ks[16], (L, SSM_WIDTH), 1.0),
        "w_glu": nrm(ks[17], (L, SSM_WIDTH, SSM_WIDTH), SSM_WIDTH ** -0.5),
        "b_glu": nrm(ks[18], (L, SSM_WIDTH), 0.02),
        "ssm_out_g": gain(ks[19], SSM_WIDTH),
        "w_out": nrm(ks[20], (L, D_MIX_2, D_MODEL), D_MIX_2 ** -0.5),
        "post_norm_g": gain(ks[21], D_MODEL),
    }

def second_block(x, positions, pre_norm_g, w_in, q_norm_g, w_uq, kv_norm_g, w_ukv, attn_out_g,
              s5_lam_re, s5_lam_im, s5_log_dt, s5_b_re, s5_b_im, s5_c_re, s5_c_im, s5_d,
              w_glu, b_glu, ssm_out_g, w_out, post_norm_g):
    split_points = list(np.cumsum(SPLITS)[:-1])
    for l in range(DEPTH):
        h = _rms_norm(x, pre_norm_g[l])
        z = h @ w_in[l]
        z_q, z_kv, z_kr, g_attn, u_ssm, g_ssm = jnp.split(z, split_points, axis=-1)
        attn = _mla_attention(z_q, z_kv, z_kr, positions, q_norm_g[l], w_uq[l], kv_norm_g[l], w_ukv[l])
        attn = _rms_norm(attn, attn_out_g[l]) * jax.nn.silu(g_attn)
        ssm = _s5_bidirectional(u_ssm, s5_lam_re[l], s5_lam_im[l], s5_log_dt[l], s5_b_re[l], s5_b_im[l],
                                s5_c_re[l], s5_c_im[l], s5_d[l])
        ssm = jax.nn.gelu(ssm)
        ssm = ssm * jax.nn.sigmoid(ssm @ w_glu[l] + b_glu[l])
        ssm = _rms_norm(ssm, ssm_out_g[l]) * jax.nn.silu(g_ssm)
        mixed = jnp.concatenate([attn, ssm], axis=-1) @ w_out[l]
        x = x + _rms_norm(mixed, post_norm_g[l])
    return x


def setup_inputs(seed=0):
    out = dict(first_inputs(seed))
    for name, value in second_inputs(seed + 1).items():
        if name != "x":
            out[name + "_2"] = value
    return out


def reference(
    x, p, positions, w_in, w_out, ret_gn_w, pool_w, pool_scale, norm_mix_w, norm_moe_w,
    router_w, router_b, expert_w_gate_up, expert_b_gate_up, expert_w_down, expert_b_down,
    norm_ple_w, ple_gate_w, ple_proj_w, final_norm_w, positions_2, pre_norm_g_2, w_in_2,
    q_norm_g_2, w_uq_2, kv_norm_g_2, w_ukv_2, attn_out_g_2, s5_lam_re_2, s5_lam_im_2,
    s5_log_dt_2, s5_b_re_2, s5_b_im_2, s5_c_re_2, s5_c_im_2, s5_d_2, w_glu_2, b_glu_2,
    ssm_out_g_2, w_out_2, post_norm_g_2,
):
    x = first_block(
        x, p, positions, w_in, w_out, ret_gn_w, pool_w, pool_scale, norm_mix_w, norm_moe_w,
        router_w, router_b, expert_w_gate_up, expert_b_gate_up, expert_w_down, expert_b_down,
        norm_ple_w, ple_gate_w, ple_proj_w, final_norm_w,
    )
    return second_block(
        x, positions_2, pre_norm_g_2, w_in_2, q_norm_g_2, w_uq_2, kv_norm_g_2, w_ukv_2,
        attn_out_g_2, s5_lam_re_2, s5_lam_im_2, s5_log_dt_2, s5_b_re_2, s5_b_im_2, s5_c_re_2,
        s5_c_im_2, s5_d_2, w_glu_2, b_glu_2, ssm_out_g_2, w_out_2, post_norm_g_2,
    )


_drawn_inputs = setup_inputs


def setup_inputs(seed=0):
    import zlib

    import numpy as np

    out = dict(_drawn_inputs(seed))
    spreads = {}
    factors = {'expert_b_gate_up': 4.244,
     'expert_b_down': 3.424,
     'norm_ple_w': 37.163,
     's5_lam_re_2': 200.0,
     'b_glu_2': 8.0,
     's5_lam_im_2': 30.176,
     's5_log_dt_2': 31.552,
     's5_b_re_2': 41.736,
     's5_b_im_2': 42.016,
     's5_c_re_2': 41.368,
     's5_c_im_2': 41.968}
    for name, (base, spread) in spreads.items():
        noise = np.random.default_rng([zlib.crc32(name.encode()), seed]).standard_normal(out[name].shape)
        drawn = base * np.exp(spread * noise) if base else spread * noise
        out[name] = __import__('jax').numpy.asarray(drawn.astype(out[name].dtype))
    for name, factor in factors.items():
        out[name] = (out[name] * factor).astype(out[name].dtype)
    return out
```

```python
from contextlib import ExitStack
import math

import numpy as np
import concourse.bass as bass
from concourse import mybir

F32 = mybir.dt.float32
I32 = mybir.dt.int32
U32 = mybir.dt.uint32
ALU = mybir.AluOpType
ACT = mybir.ActivationFunctionType
AX = mybir.AxisListType.X

P = 128
SEQ, D = 2048, 1024
TILES = SEQ // P
KD = D // P
BANK = 512

D_RET, HEADS, HD = 512, 8, 64
PAIRS = HEADS // 2
WINDOWS = (2, 4, 8, 16)
GROUPS = len(WINDOWS)
PROJ = 4 * D_RET + 512
LOG_GAMMA = [math.log1p(-(2.0 ** (-5 - h))) for h in range(HEADS)]
NORM_EPS, GN_EPS = 1e-5, 1e-5
ROPE_HALF = 32
INV_FREQ = [float(np.float32(10000.0 ** (-j / ROPE_HALF))) for j in range(ROPE_HALF)]
TWO_PI_HI = 6.28125
TWO_PI_MID = float(np.float32(2 * math.pi - TWO_PI_HI))
TWO_PI_LO = 2 * math.pi - TWO_PI_HI - TWO_PI_MID
ROUND = 12582912.0
PI_IN = 3.1415925

E, TOPK, CAP = 32, 4, SEQ
FF = 1024
BODY_LINKS = 57


def place_of(h):
    return h % 2 * PAIRS + h // 2


class Chain:

    def __init__(self, eng, sem):
        self.eng, self.sem, self.base, self.n = eng, sem, 0, 0

    def start(self, base):
        self.base, self.n = base, 0

    def link(self, ins):
        self.n += 1
        ins.then_inc(self.sem, 1)
        self.eng.wait_ge(self.sem, self.base + self.n)


def clear_semaphores(nc, s):
    with nc.Block() as block:
        @block.sync
        def _(sp):
            for signal in s.values():
                sp.sem_clear(signal)


def rsqrt(dve, ch, y, x, t, done=None):
    ch.link(dve.tensor_scalar(t.bitcast(I32), x.bitcast(I32), 1, None, ALU.logical_shift_right))
    ch.link(dve.tensor_scalar(y.bitcast(I32), t.bitcast(I32), -1.0, 1597463007.0, ALU.mult, ALU.add))
    for step in range(3):
        ch.link(dve.tensor_tensor(t, y, y, ALU.mult))
        ch.link(dve.scalar_tensor_tensor(t, t, -0.5, x, ALU.mult, ALU.mult))
        last = dve.scalar_tensor_tensor(y, t, 1.5, y, ALU.add, ALU.mult)
        if step == 2 and done is not None:
            last.then_inc(done, 1)
        else:
            ch.link(last)


def reduce_angles(dve, ch, ang, turns):
    ch.link(dve.tensor_scalar(turns, ang, 1.0 / (2 * math.pi), ROUND, ALU.mult, ALU.add))
    ch.link(dve.tensor_scalar(turns, turns, ROUND, None, ALU.subtract))
    for part in (TWO_PI_HI, TWO_PI_MID, TWO_PI_LO):
        ch.link(dve.scalar_tensor_tensor(ang, turns, -part, ang, ALU.mult, ALU.add))
    ch.link(dve.tensor_scalar(ang, ang, PI_IN, -PI_IN, ALU.min, ALU.max))


def mixer_phase(nc, I, S):
    with ExitStack() as ctx:
        sb = lambda name, shape, dt=F32: ctx.enter_context(nc.sbuf_tensor(name, shape, dt))
        pb = lambda name, w: ctx.enter_context(nc.psum_tensor(name, [P, w], F32))
        sem = lambda name: ctx.enter_context(nc.semaphore(name))

        w_in = sb("w_in_sb", [P, KD, PROJ])
        w_out = sb("w_out_sb", [P, KD, D])
        w_pool = sb("w_pool_sb", [P, GROUPS, P])
        w_rt = sb("w_rt_sb", [P, KD, E])
        gain_mix = sb("gain_mix", [P, KD])
        gain_out = sb("gain_out", [P, KD])
        gain_moe = sb("gain_moe", [P, D])
        bias_rt = sb("bias_rt", [P, E])
        ident = sb("ident", [P, P])
        ones = sb("ones", [P, P])
        rel = sb("rel", [P, P])
        causal = sb("causal", [P, P])
        before = sb("before", [P, P])
        step1 = sb("step1", [P, P])
        back = sb("back", [P, 1])
        decay = sb("decay", [P, HEADS, P])
        xi = sb("xi", [P, PAIRS, P])
        zeta = sb("zeta", [P, HEADS])
        chunk_decay = sb("chunk_decay", [P, PAIRS])
        band = sb("band", [P, GROUPS, P])
        band0 = sb("band0", [P, GROUPS, P])
        band_prev = sb("band_prev", [P, GROUPS, P])
        pos_i = sb("pos_i", [P, TILES], I32)
        pos_f = sb("pos_f", [P, TILES])
        freq = sb("freq", [P, ROPE_HALF])
        sin = sb("sin", [P, TILES, ROPE_HALF])
        cos = sb("cos", [P, TILES, ROPE_HALF])
        iota_e = sb("iota_e", [P, E])
        first_slot = sb("first_slot", [P, E])
        tok_id = sb("tok_id", [P, TILES], I32)

        x_sb = sb("x_sb", [P, 2, D])
        xT = sb("xT", [P, KD, P])
        qk = sb("qk", [P, 2 * HEADS, 2, ROPE_HALF])
        vgu = sb("vgu", [P, 2, 3 * BANK])
        squares = sb("squares", [P, D], mybir.dt.bfloat16)
        ss1, ms1, rstd1, nt1 = (sb(n, [P, 1]) for n in ("ss1", "ms1", "rstd1", "nt1"))
        ss2, ms2, rstd2, nt2 = (sb(n, [P, 1]) for n in ("ss2", "ms2", "rstd2", "nt2"))
        rot = sb("rot", [P, 2 * HEADS, 2, ROPE_HALF])
        rope_a = sb("rope_a", [P, 2 * HEADS, ROPE_HALF])
        rope_b = sb("rope_b", [P, 2 * HEADS, ROPE_HALF])
        kz = rope_b[:, :, :].rearrange("p (h two) f -> p h (two f)", two=2)
        turns = rope_a
        qT = sb("qT", [P, PAIRS, P])
        kT = sb("kT", [P, PAIRS, P])
        qxT = sb("qxT", [P, PAIRS, P])
        sT = sb("sT", [P, HEADS, P])
        inside, recip0 = sT[:, 0, :], sT[:, 1, :]
        ang = sT[:, 4:8, :].rearrange("p a (t f) -> p (a t) f", f=ROPE_HALF)
        state = sb("state", [P, PAIRS, 2, HD])
        pooledT = sb("pooledT", [P, GROUPS, P])
        catT = sb("catT", [P, KD, P])
        mean, var, gstd, gnt = (sb(n, [P, HEADS]) for n in ("mean", "var", "gstd", "gnt"))
        yc = sb("yc", [P, HEADS, HD])
        ysq = rope_a[:, :, :].rearrange("p (h two) f -> p h (two f)", two=2)
        tanh_g = sb("tanh_g", [P, D_RET])
        ret = yc
        hn_sb = sb("hn_sb", [P, D])
        hnT = xT
        zero_i = xT[:, 0:4, :].rearrange("p k c -> p (k c)").bitcast(I32)
        lg = sb("lg", [P, E])
        top8 = sb("top8", [P, 8])
        top4 = sb("top4", [P, TOPK])
        idx8 = sb("idx8", [P, 8], U32)
        idxf = sb("idxf", [P, TOPK])
        ntop = sb("ntop", [P, 1])
        ex = sb("ex", [P, TOPK])
        exsum = sb("exsum", [P, 1])
        exrec = sb("exrec", [P, 1])
        onehot = sb("onehot", [P, TOPK, E])
        mask = sb("mask", [P, E])
        cum = sb("cum", [P, E])
        slot = sb("slot", [P, E])
        hit = sb("hit", [P, TOPK, E])
        posf = sb("posf", [P, TOPK])
        pos_cur = sb("pos_cur", [P, TOPK], I32)
        tok_cur = sb("tok_cur", [P, 1], I32)
        cnt = sb("cnt", [P, E])
        cnt_i = sb("cnt_i", [P, E], I32)
        cnt_e = sb("cnt_e", [P, E])
        zero_e = sb("zero_e", [P, E])
        ends = sb("ends", [P, E])
        which = w_in[:, 0, 0:TILES * TOPK * E].rearrange("p (n e) -> p n e", e=E)
        posf_all = [w_in[:, 1, n * TILES * TOPK:(n + 1) * TILES * TOPK] for n in range(2)]

        TR = pb("TR", 2 * BANK)
        PJ = [pb("PJ0", BANK), pb("PJ1", BANK)]
        SC = pb("SC", 2 * BANK)
        KV = pb("KV", BANK)
        Y = pb("Y", BANK)

        names = """loads weights pool_chain dve_setup act_setup pool_setup tables_in sines
            x_loaded xT_ps xT_sb sumsq1 rstd1_ready proj_ps proj_sb rope_done qk_ps qkT_sb qx_sb sc_ps kv_ps
            sT_sb state_new y_ps pl_ps pl_sb mx_ps mx_sb tanh_done ret_done ret_ps ret_sb o_ps h_done sumsq2
            hn_done hn_ps hn_sb_done lg_ps mask_done ex_done rank_ps pos_done h_stored hn_stored
            dve_chain list_zeroed slots_seen totals_ps ends_ready """.split()
        s = {n: sem(n) for n in names}
        ctx.enter_context(nc.allow_non_contiguous_dma(reason="small vectors, a word per partition"))
        ctx.callback(clear_semaphores, nc, dict(s))
        s.update({n: S["keep"].enter_context(nc.semaphore(n)) for n in ('scattered',)})
        block = ctx.enter_context(nc.Block())

        x_t = I["x"][0].rearrange("(t p) d -> t p d", p=P)
        h_t = S["h1"].rearrange("(t p) d -> t p d", p=P)
        hn_t = S["hn"].rearrange("(t p) d -> t p d", p=P)
        row = lambda ap: ap.partition_broadcast(P)

        @block.sync
        def _(sp):
            def load_x(t, par):
                sp.dma_start(x_sb[:, par, :], x_t[bass.ds(t, 1)].squeeze(0)).then_inc(s["x_loaded"], 16)

            sp.dma_start(gain_mix[:, :], I["norm_mix_w"][0].rearrange("(k p) -> p k", p=P)).then_inc(s["loads"], 16)
            sp.dma_start(gain_out[:, 0:4], I["ret_gn_w"][0].rearrange("(k p) -> p k", p=P)).then_inc(s["loads"], 16)
            sp.dma_start(gain_out[:, 4:8], I["pool_scale"][0].rearrange("(k p) -> p k", p=P)).then_inc(s["loads"], 16)
            sp.dma_start(gain_moe[:, :], row(I["norm_moe_w"][0])).then_inc(s["loads"], 16)
            sp.dma_start(bias_rt[:, :], row(I["router_b"][0])).then_inc(s["loads"], 16)
            sp.dma_start(pos_i[:, :], I["positions"][0].rearrange("(t p) -> p t", p=P)).then_inc(s["loads"], 16)
            load_x(0, 0)
            for k in range(KD):
                sp.dma_start(w_in[:, k, :], I["w_in"][0, k * P:(k + 1) * P, :]).then_inc(s["weights"], 16)
            sp.dma_start(w_rt[:, :, :], I["router_w"][0].rearrange("(k p) e -> p k e", p=P)).then_inc(s["weights"], 16)
            sp.dma_start(w_pool[:, :, :], I["pool_w"][0].rearrange("g c d -> c g d")).then_inc(s["weights"], 16)
            for k in range(KD):
                sp.dma_start(w_out[:, k, :], I["w_out"][0, k * P:(k + 1) * P, :]).then_inc(s["weights"], 16)
            sp.wait_ge(s["pool_setup"], 1)
            sp.dma_start(S["tok_list"].rearrange("(p n) o -> p (n o)", p=P), zero_i[:, :]).then_inc(s["list_zeroed"], 16)
            sp.wait_ge(s["x_loaded"], 16)
            load_x(1, 1)

            def body(t, par, has_x):
                sp.wait_ge(s["h_done"], t + 1)
                sp.dma_start(h_t[bass.ds(t, 1)].squeeze(0), x_sb[:, par, :]).then_inc(s["h_stored"], 16)
                sp.wait_ge(s["hn_done"], t + 1)
                sp.dma_start(hn_t[bass.ds(t, 1)].squeeze(0), hn_sb[:, :]).then_inc(s["hn_stored"], 16)
                if has_x:
                    sp.wait_ge(s["h_stored"], t * 16 + 16)
                    load_x(t + 2, par)

            body(0, 0, True)
            with sp.Fori(0, 6) as i:
                for u in range(2):
                    body(i * 2 + (1 + u), (1 + u) % 2, True)
            for t in (13, 14, 15):
                body(t, t % 2, t + 2 < TILES)
            sp.wait_ge(s["h_stored"], 16 * TILES)
            sp.wait_ge(s["hn_stored"], 16 * TILES)

        @block.gpsimd
        def _(pool):
            ch = Chain(pool, s["pool_chain"])
            ch.link(pool.memset(zero_i, 0))
            pool.sem_inc(s["pool_setup"], 1)
            ch.link(pool.memset(ones[:, :], 1.0))
            ch.link(pool.memset(ident[:, :], 0.0))
            ch.link(pool.affine_select(out=ident[:, :], in_=ident[:, :], compare_op=ALU.not_equal, fill=1.0, base=0,
                                       pattern=[[-1, P]], channel_multiplier=1))
            for j in range(ROPE_HALF):
                pool.memset(freq[:, j:j + 1], INV_FREQ[j])
            pool.memset(state[:, :, :, :], 0.0)
            pool.memset(cum[:, :], 0.0)
            pool.memset(zero_e[:, :], 0.0)
            ch.link(pool.memset(vgu[:, 1, 2 * BANK:], 0.0))
            for h in range(HEADS):
                half = slice(HD * (h % 2), HD * (h % 2) + HD)
                ch.link(pool.memset(chunk_decay[half, h // 2:h // 2 + 1], math.exp(P * LOG_GAMMA[h])))
            iota = lambda out, pattern, base, cm: pool.iota(
                out, pattern=pattern, base=base, channel_multiplier=cm, allow_small_or_imprecise_dtypes=True)
            iota(rel[:, :], [[1, P]], 0, -1)
            iota(step1[:, :], [[1, P]], 1, 0)
            iota(back[:, :], [[0, 1]], P - 1, -1)
            iota(iota_e[:, :], [[1, E]], 0, 0)
            iota(tok_id[:, :], [[P, TILES]], 0, 1).then_inc(s["pool_setup"], 1)

            def body(t):
                pool.wait_ge(s["pos_done"], t + 1)
                pool.sem_inc(s["slots_seen"], 1)
                for k in range(TOPK):
                    pool.indirect_dma_start(
                        S["tok_list"], bass.IndirectOffsetOnAxis(ap=pos_cur[:, k:k + 1], axis=0),
                        tok_cur[:, :], None).then_inc(s["scattered"], 16)

            pool.wait_ge(s["list_zeroed"], 16)
            with pool.Fori(0, TILES) as t:
                body(t)
            pool.wait_ge(s["scattered"], 16 * TOPK * TILES)

        @block.scalar
        def _(act):
            act.wait_ge(s["pool_setup"], 2)
            act.wait_ge(s["dve_setup"], 1)
            act.activation(sin[:, :, :], ang[:, :, :], ACT.Sin)
            act.activation(cos[:, :, :], ang[:, :, :], ACT.Sin, scale=0.5).then_inc(s["sines"], 1)
            for h in range(HEADS):
                half = slice(HD * (h % 2), HD * (h % 2) + HD)
                act.activation(decay[:, place_of(h), :], rel[:, :], ACT.Exp, scale=LOG_GAMMA[h])
                act.activation(zeta[:, h:h + 1], back[:, :], ACT.Exp, scale=LOG_GAMMA[h])
                last = act.activation(xi[half, h // 2, :], step1[half, :], ACT.Exp, scale=LOG_GAMMA[h])
            last.then_inc(s["act_setup"], 1)

            def norm_x(t, par):
                act.wait_ge(s["x_loaded"], t * 16 + 16)
                act.activation(squares[:, :], x_sb[:, par, :], ACT.Square, accum_out=ss1[:, :]).then_inc(s["sumsq1"], 1)

            def copy_xT(t):
                act.wait_ge(s["xT_ps"], t + 1)
                act.activation(xT[:, 0:4, :], TR[:, 0:BANK], ACT.Copy)
                act.activation(xT[:, 4:8, :], TR[:, BANK:], ACT.Copy).then_inc(s["xT_sb"], 1)

            def evacuate(t, par, n, has_prev):
                act.wait_ge(s["proj_ps"], t * 5 + (n + 1))
                if n == 0:
                    act.wait_ge(s["rstd1_ready"], t + 1)
                if n == 4 and has_prev:
                    act.wait_ge(s["pl_ps"], t)
                if n < 2:
                    dst = qk[:, n * HEADS:(n + 1) * HEADS, :, :].rearrange("p h two f -> p (h two f)")
                else:
                    dst = vgu[:, par, (n - 2) * BANK:(n - 1) * BANK]
                act.activation(dst, PJ[n % 2][:, :], ACT.Copy, scale=rstd1[:, :]).then_inc(s["proj_sb"], 1)

            def body(t, par, has_next):
                np_ = 1 - par
                if has_next:
                    norm_x(t + 1, np_)
                    copy_xT(t + 1)
                act.wait_ge(s["qk_ps"], t + 1)
                act.activation(qT[:, :, :], SC[:, 0:BANK], ACT.Copy)
                act.activation(kT[:, :, :], SC[:, BANK:], ACT.Copy).then_inc(s["qkT_sb"], 1)
                if has_next:
                    evacuate(t + 1, np_, 0, True)
                    evacuate(t + 1, np_, 1, True)
                act.activation(tanh_g[:, :], vgu[:, par, BANK:2 * BANK], ACT.Tanh,
                               scale=0.5).then_inc(s["tanh_done"], 1)
                if has_next:
                    evacuate(t + 1, np_, 2, True)
                act.wait_ge(s["pl_ps"], t + 1)
                act.activation(pooledT[:, :, :], SC[:, 0:BANK], ACT.Copy).then_inc(s["pl_sb"], 1)
                if has_next:
                    evacuate(t + 1, np_, 3, True)
                act.wait_ge(s["mx_ps"], t + 1)
                act.activation(catT[:, 4:8, :], SC[:, BANK:], ACT.Copy).then_inc(s["mx_sb"], 1)
                act.wait_ge(s["ret_ps"], t + 1)
                act.activation(catT[:, 0:4, :], KV[:, :], ACT.Copy).then_inc(s["ret_sb"], 1)
                act.wait_ge(s["h_done"], t + 1)
                act.activation(squares[:, :], x_sb[:, par, :], ACT.Square, accum_out=ss2[:, :]).then_inc(s["sumsq2"], 1)
                if has_next:
                    evacuate(t + 1, np_, 4, True)
                act.wait_ge(s["hn_ps"], t + 1)
                act.activation(hnT[:, 0:4, :], SC[:, 0:BANK], ACT.Copy)
                act.activation(hnT[:, 4:8, :], SC[:, BANK:], ACT.Copy).then_inc(s["hn_sb_done"], 1)
                act.wait_ge(s["mask_done"], t + 1)
                act.activation(ex[:, :], top4[:, :], ACT.Exp, bias=ntop[:, :],
                               accum_out=exsum[:, :]).then_inc(s["ex_done"], 1)

            norm_x(0, 0)
            act.wait_ge(s["list_zeroed"], 16)
            copy_xT(0)
            for n in range(5):
                evacuate(0, 0, n, False)
            body(0, 0, True)
            with act.Fori(0, 7) as i:
                for u in range(2):
                    body(i * 2 + (1 + u), (1 + u) % 2, True)
            body(15, 1, False)

        @block.vector
        def _(dve):
            ch = Chain(dve, s["dve_chain"])
            dve.wait_ge(s["pool_setup"], 2)
            dve.wait_ge(s["loads"], 16 * 6)
            ch.link(dve.tensor_copy(pos_f[:, :], pos_i[:, :]))
            ch.link(dve.tensor_tensor(ang[:, :, :], pos_f[:, :].unsqueeze(2).to_broadcast([P, TILES, ROPE_HALF]),
                                      freq[:, :].unsqueeze(1).to_broadcast([P, TILES, ROPE_HALF]), ALU.mult))
            reduce_angles(dve, ch, ang[:, :, :], turns[:, :, :])
            dve.tensor_scalar(causal[:, :], rel[:, :], 0.0, HD ** -0.5, ALU.is_ge, ALU.mult)
            dve.tensor_scalar(before[:, :], rel[:, :], 0.0, None, ALU.is_gt)
            dve.tensor_scalar(first_slot[:, :], iota_e[:, :], float(CAP), None, ALU.mult)
            for g, w in enumerate(WINDOWS):
                ch.link(dve.tensor_scalar(inside[:, :], rel[:, :], 0.0, None, ALU.is_ge))
                ch.link(dve.scalar_tensor_tensor(inside[:, :], rel[:, :], float(w - 1), inside[:, :],
                                                 ALU.is_le, ALU.mult))
                ch.link(dve.scalar_tensor_tensor(band[:, g, :], inside[:, :], 1.0 / w, ident[:, :],
                                                 ALU.mult, ALU.subtract))
                ch.link(dve.tensor_scalar(recip0[:, :], step1[:, :], float(w), None, ALU.min))
                ch.link(dve.reciprocal(recip0[:, :], recip0[:, :]))
                ch.link(dve.tensor_tensor(recip0[:, :], recip0[:, :], inside[:, :], ALU.mult))
                ch.link(dve.tensor_tensor(band0[:, g, :], recip0[:, :], ident[:, :], ALU.subtract))
                ch.link(dve.tensor_scalar(band_prev[:, g, :], rel[:, :], float(w - 1 - P), 1.0 / w,
                                          ALU.is_le, ALU.mult))
            dve.tensor_scalar(rel[:, :], rel[:, :], 0.0, None, ALU.max).then_inc(s["dve_setup"], 1)
            dve.wait_ge(s["sines"], 1)
            ch.link(dve.tensor_tensor(cos[:, :, :], cos[:, :, :], cos[:, :, :], ALU.mult))
            ch.link(dve.tensor_scalar(cos[:, :, :], cos[:, :, :], -2.0, 1.0, ALU.mult, ALU.add))
            dve.wait_ge(s["act_setup"], 1)
            ch.link(dve.tensor_tensor(decay[:, :, :], decay[:, :, :],
                                      causal[:, :].unsqueeze(1).to_broadcast([P, HEADS, P]), ALU.mult))
            ch.link(dve.tensor_scalar(zeta[:, :], zeta[:, :], HD ** -0.5, None, ALU.mult))
            dve.wait_ge(s["weights"], 16 * (2 * KD + 2))
            for k in range(KD):
                dve.tensor_scalar(w_in[:, k, :], w_in[:, k, :], gain_mix[:, k:k + 1], None, ALU.mult)
                last = dve.tensor_scalar(w_out[:, k, :], w_out[:, k, :], gain_out[:, k:k + 1], None, ALU.mult)
            last.then_inc(s["dve_setup"], 1)

            def inv_rms(src, ms, y, t_, eps, count):
                ch.link(dve.tensor_scalar(ms[:, :], src[:, :], 1.0 / count, eps, ALU.mult, ALU.add))
                rsqrt(dve, ch, y[:, :], ms[:, :], t_[:, :])

            def norm_x(t, has_prev):
                dve.wait_ge(s["sumsq1"], t + 1)
                if has_prev:
                    dve.wait_ge(s["proj_sb"], t * 5)
                ch.link(dve.tensor_scalar(ms1[:, :], ss1[:, :], 1.0 / D, NORM_EPS, ALU.mult, ALU.add))
                rsqrt(dve, ch, rstd1[:, :], ms1[:, :], nt1[:, :], s["rstd1_ready"])

            def place(t, has_prev=True):
                dve.wait_ge(s["rank_ps"], t + 1)
                dve.wait_ge(s["ex_done"], t + 1)
                ch.link(dve.tensor_tensor(slot[:, :], KV[:, E:2 * E], first_slot[:, :], ALU.add))
                dve.tensor_tensor(cum[:, :], cum[:, :], mask[:, :], ALU.add)
                ch.link(dve.tensor_tensor(hit[:, :, :], onehot[:, :, :],
                                          slot[:, :].unsqueeze(1).to_broadcast([P, TOPK, E]), ALU.mult))
                ch.link(dve.tensor_reduce(posf[:, :], hit[:, :, :], AX, ALU.add))
                dve.tensor_copy(S["pos"][:, bass.ds(t * TOPK, TOPK)], posf[:, :])
                if has_prev:
                    dve.wait_ge(s["scattered"], t * (16 * TOPK))
                dve.tensor_copy(pos_cur[:, :], posf[:, :])
                dve.tensor_copy(tok_cur[:, :], tok_id[:, bass.ds(t, 1)])
                ch.link(dve.reciprocal(exrec[:, :], exsum[:, :]))
                dve.tensor_scalar(S["gates"][:, bass.ds(t * TOPK, TOPK)], ex[:, :], exrec[:, :], None,
                                  ALU.mult).then_inc(s["pos_done"], 1)

            def body(t, par, has_prev, has_next):
                c_t = cos[:, bass.ds(t, 1), :].to_broadcast([P, 2 * HEADS, ROPE_HALF])
                s_t = sin[:, bass.ds(t, 1), :].to_broadcast([P, 2 * HEADS, ROPE_HALF])
                dve.wait_ge(s["proj_sb"], t * 5 + 5)
                if has_prev:
                    dve.wait_ge(s["kv_ps"], t)
                dve.tensor_tensor(rope_a[:, :, :], qk[:, :, 0, :], c_t, ALU.mult)
                ch.link(dve.tensor_tensor(rope_b[:, :, :], qk[:, :, 1, :], s_t, ALU.mult))
                ch.link(dve.tensor_tensor(rot[:, :, 0, :], rope_a[:, :, :], rope_b[:, :, :], ALU.subtract))
                dve.tensor_tensor(rope_a[:, :, :], qk[:, :, 1, :], c_t, ALU.mult)
                ch.link(dve.tensor_tensor(rope_b[:, :, :], qk[:, :, 0, :], s_t, ALU.mult))
                ch.link(dve.tensor_tensor(rot[:, :, 1, :], rope_a[:, :, :], rope_b[:, :, :], ALU.add))
                k_rot = rot[:, HEADS:2 * HEADS, :, :].rearrange("p h two f -> p h (two f)")
                dve.tensor_tensor(kz[:, :, :], k_rot, zeta[:, :].unsqueeze(2).to_broadcast([P, HEADS, HD]),
                                  ALU.mult).then_inc(s["rope_done"], 1)
                if has_next:
                    norm_x(t + 1, True)
                dve.wait_ge(s["qkT_sb"], t + 1)
                dve.tensor_tensor(qxT[:, :, :], qT[:, :, :], xi[:, :, :], ALU.mult).then_inc(s["qx_sb"], 1)
                if has_prev:
                    place(t - 1, not isinstance(t, int) or t > 1)
                dve.wait_ge(s["sc_ps"], t + 1)
                dve.tensor_tensor(sT[:, :, :], TR[:, :].rearrange("p (h c) -> p h c", h=HEADS), decay[:, :, :],
                                  ALU.mult).then_inc(s["sT_sb"], 1)
                dve.wait_ge(s["y_ps"], t + 1)
                y = Y[:, :].rearrange("p (h e) -> p h e", h=HEADS)
                wide = lambda ap: ap.unsqueeze(2).to_broadcast([P, HEADS, HD])
                ch.link(dve.tensor_reduce(mean[:, :], y, AX, ALU.add))
                ch.link(dve.tensor_scalar(mean[:, :], mean[:, :], 1.0 / HD, None, ALU.mult))
                ch.link(dve.tensor_tensor(yc[:, :, :], y, wide(mean[:, :]), ALU.subtract))
                kv = KV[:, :].rearrange("p (a h2 e) -> p a h2 e", a=PAIRS, h2=2)
                both = state[:, :, :, :].rearrange("p a h2 e -> p a (h2 e)")
                ch.link(dve.tensor_tensor(both, both, chunk_decay[:, :].unsqueeze(2).to_broadcast([P, PAIRS, P]),
                                          ALU.mult))
                dve.tensor_tensor(state[0:HD, :, 0, :], state[0:HD, :, 0, :], kv[0:HD, :, 0, :], ALU.add)
                dve.tensor_tensor(state[HD:P, :, 1, :], state[HD:P, :, 1, :], kv[HD:P, :, 1, :],
                                  ALU.add).then_inc(s["state_new"], 1)
                ch.link(dve.tensor_tensor(ysq[:, :, :], yc[:, :, :], yc[:, :, :], ALU.mult))
                ch.link(dve.tensor_reduce(var[:, :], ysq[:, :, :], AX, ALU.add))
                inv_rms(var, var, gstd, gnt, GN_EPS, HD)
                ch.link(dve.tensor_tensor(yc[:, :, :], yc[:, :, :], wide(gstd[:, :]), ALU.mult))
                dve.wait_ge(s["tanh_done"], t + 1)
                g = vgu[:, par, BANK:2 * BANK]
                ch.link(dve.scalar_tensor_tensor(tanh_g[:, :], tanh_g[:, :], 1.0, g, ALU.add, ALU.mult))
                yn = yc[:, :, :].rearrange("p h e -> p (h e)")
                dve.scalar_tensor_tensor(yn, tanh_g[:, :], 0.5, yn, ALU.mult, ALU.mult).then_inc(s["ret_done"], 1)
                dve.wait_ge(s["o_ps"], t + 1)
                if has_prev:
                    dve.wait_ge(s["hn_stored"], t * 16)
                dve.tensor_tensor(x_sb[:, par, :], TR[:, :], x_sb[:, par, :], ALU.add).then_inc(s["h_done"], 1)
                dve.wait_ge(s["sumsq2"], t + 1)
                inv_rms(ss2, ms2, rstd2, nt2, NORM_EPS, D)
                dve.scalar_tensor_tensor(hn_sb[:, :], x_sb[:, par, :], rstd2[:, :], gain_moe[:, :],
                                         ALU.mult, ALU.mult).then_inc(s["hn_done"], 1)
                dve.wait_ge(s["lg_ps"], t + 1)
                ch.link(dve.tensor_tensor(lg[:, :], KV[:, 0:E], bias_rt[:, :], ALU.add))
                ch.link(dve.tensor_reduce(ntop[:, :], lg[:, :], AX, ALU.max))
                dve.tensor_scalar(ntop[:, :], ntop[:, :], -1.0, None, ALU.mult)
                ch.link(dve.max(top8[:, :], lg[:, :]))
                dve.tensor_copy(top4[:, :], top8[:, 0:TOPK])
                ch.link(dve.max_index(idx8[:, :], top8[:, :], lg[:, :]))
                ch.link(dve.tensor_copy(idxf[:, :], idx8[:, 0:TOPK]))
                ch.link(dve.tensor_tensor(onehot[:, :, :], iota_e[:, :].unsqueeze(1).to_broadcast([P, TOPK, E]),
                                          idxf[:, :].unsqueeze(2).to_broadcast([P, TOPK, E]), ALU.is_equal))
                dve.tensor_reduce(mask[:, :], onehot[:, :, :].rearrange("p k e -> p e k"), AX,
                                  ALU.add).then_inc(s["mask_done"], 1)

            norm_x(0, False)
            body(0, 0, False, True)
            body(1, 1, True, True)
            base = ch.n
            with dve.Fori(0, 6) as i:
                ch.start(base + i * (2 * BODY_LINKS))
                body(i * 2 + 2, 0, True, True)
                body(i * 2 + 3, 1, True, True)
                assert ch.n == 2 * BODY_LINKS, ch.n
            ch.start(base + 6 * 2 * BODY_LINKS)
            body(14, 0, True, True)
            body(15, 1, True, False)
            place(15)
            dve.wait_ge(s["totals_ps"], 1)
            ch.link(dve.tensor_scalar(cnt_i[:, :], Y[:, 0:E], float(P - 1), None, ALU.add))
            ch.link(dve.tensor_scalar(cnt_i[:, :], cnt_i[:, :], 7, None, ALU.arith_shift_right))
            ch.link(dve.tensor_scalar(cnt[:, :], cnt_i[:, :], 1.0, None, ALU.max))
            ch.link(dve.tensor_tensor_scan(ends[:, :], cnt[:, :], zero_e[:, :], 0.0, ALU.add, ALU.add))
            dve.memset(S["starts"][:, 0:1], 0)
            dve.tensor_copy(S["starts"][:, 1:E + 1], ends[:, :])
            dve.tensor_copy(S["n_tiles"][:, :], cnt[:, :])
            to_row, e_of, row_f = cnt_e, posf_all[0], posf_all[1]
            ch.link(dve.tensor_tensor(to_row[:, :], ends[:, :], cnt[:, :], ALU.subtract))
            ch.link(dve.scalar_tensor_tensor(to_row[:, :], to_row[:, :], float(P), first_slot[:, :], ALU.mult, ALU.subtract))
            ch.link(dve.tensor_scalar(e_of.bitcast(I32), S["pos"][:, :], CAP.bit_length() - 1, None, ALU.arith_shift_right))
            dve.tensor_copy(row_f, S["pos"][:, :])
            ch.link(dve.tensor_copy(e_of, e_of.bitcast(I32)))
            shape = [P, TILES * TOPK, E]
            ch.link(dve.tensor_tensor(which, iota_e[:, :].unsqueeze(1).to_broadcast(shape),
                                      e_of.unsqueeze(2).to_broadcast(shape), ALU.is_equal))
            ch.link(dve.tensor_tensor(which, which, to_row[:, :].unsqueeze(1).to_broadcast(shape), ALU.mult))
            ch.link(dve.tensor_reduce(e_of, which, AX, ALU.add))
            dve.tensor_tensor(S["pos"][:, :], row_f, e_of, ALU.add)

        @block.tensor
        def _(pe):
            pe.wait_ge(s["pool_setup"], 2)

            def transpose_x(t, par, has_prev):
                pe.wait_ge(s["x_loaded"], t * 16 + 16)
                if has_prev:
                    pe.wait_ge(s["h_done"], t - 1)
                for k in range(KD):
                    mm = pe.transpose(TR[:, k * P:(k + 1) * P], x_sb[:, par, k * P:(k + 1) * P], ident[:, :])
                mm.then_inc(s["xT_ps"], 1)

            def project(t, n, has_prev=True):
                if n == 0:
                    pe.wait_ge(s["xT_sb"], t + 1)
                if has_prev or n > 1:
                    pe.wait_ge(s["proj_sb"], t * 5 + max(n - 1, 0))
                for k in range(KD):
                    mm = pe.matmul(PJ[n % 2][:, :], xT[:, k, :], w_in[:, k, n * BANK:(n + 1) * BANK],
                                   start=(k == 0), stop=(k == KD - 1))
                mm.then_inc(s["proj_ps"], 1)

            def rank(t):
                pe.wait_ge(s["mask_done"], t + 1)
                pe.matmul(KV[:, E:2 * E], before[:, :], mask[:, :], start=True, stop=False)
                pe.matmul(KV[:, E:2 * E], ones[:, :], cum[:, :], start=False, stop=True).then_inc(s["rank_ps"], 1)

            def body(t, par, has_prev, has_next):
                if has_next:
                    transpose_x(t + 1, 1 - par, has_prev)
                pe.wait_ge(s["rope_done"], t + 1)
                if has_prev:
                    pe.wait_ge(s["hn_sb_done"], t)
                    pe.wait_ge(s["h_done"], t)
                for j in range(2 * PAIRS):
                    src = rot[:, 2 * j:2 * j + 2, :, :].rearrange("p h two f -> p (h two f)")
                    mm = pe.transpose(SC[:, j * P:(j + 1) * P], src, ident[:, :])
                mm.then_inc(s["qk_ps"], 1)
                if has_prev:
                    rank(t - 1)
                if has_next:
                    project(t + 1, 0)
                    project(t + 1, 1)
                pe.wait_ge(s["qkT_sb"], t + 1)
                for h in range(HEADS):
                    half = slice(HD * (h % 2), HD * (h % 2) + HD)
                    mm = pe.matmul(TR[:, place_of(h) * P:(place_of(h) + 1) * P], kT[half, h // 2, :], qT[half, h // 2, :],
                                   start=True, stop=True)
                mm.then_inc(s["sc_ps"], 1)
                if has_prev:
                    pe.wait_ge(s["pos_done"], t)
                for a in range(PAIRS):
                    v_pair = vgu[:, par, a * P:(a + 1) * P]
                    mm = pe.matmul(KV[:, a * P:(a + 1) * P], kz[:, 2 * a:2 * a + 2, :].rearrange("p h d -> p (h d)"),
                                   v_pair, start=True, stop=True)
                mm.then_inc(s["kv_ps"], 1)
                if has_next:
                    project(t + 1, 2)
                pe.wait_ge(s["qx_sb"], t + 1)
                for g in range(GROUPS):
                    ug = slice(2 * BANK + g * P, 2 * BANK + (g + 1) * P)
                    pe.matmul(SC[:, g * P:(g + 1) * P], vgu[:, 1 - par, ug], band_prev[:, g, :],
                              start=True, stop=False)
                    mm = pe.matmul(SC[:, g * P:(g + 1) * P], vgu[:, par, ug],
                                   (band if has_prev else band0)[:, g, :], start=False, stop=True)
                mm.then_inc(s["pl_ps"], 1)
                pe.wait_ge(s["sT_sb"], t + 1)
                if has_prev:
                    pe.wait_ge(s["state_new"], t)
                for a in range(PAIRS):
                    pe.matmul(Y[:, a * P:(a + 1) * P], qxT[:, a, :],
                              state[:, a, :, :].rearrange("p h2 e -> p (h2 e)"), start=True, stop=False)
                    for h in (2 * a, 2 * a + 1):
                        mm = pe.matmul(Y[:, h * HD:(h + 1) * HD], sT[:, place_of(h), :],
                                       vgu[:, par, h * HD:(h + 1) * HD], start=False, stop=(h % 2 == 1))
                mm.then_inc(s["y_ps"], 1)
                pe.wait_ge(s["pl_sb"], t + 1)
                for g in range(GROUPS):
                    mm = pe.matmul(SC[:, BANK + g * P:BANK + (g + 1) * P], w_pool[:, g, :], pooledT[:, g, :],
                                   start=True, stop=True)
                mm.then_inc(s["mx_ps"], 1)
                if has_next:
                    project(t + 1, 3)
                pe.wait_ge(s["ret_done"], t + 1)
                for a in range(PAIRS):
                    mm = pe.transpose(KV[:, a * P:(a + 1) * P], ret[:, 2 * a:2 * a + 2, :].rearrange("p h e -> p (h e)"), ident[:, :])
                mm.then_inc(s["ret_ps"], 1)
                pe.wait_ge(s["mx_sb"], t + 1)
                pe.wait_ge(s["ret_sb"], t + 1)
                for n in range(2):
                    for k in range(KD):
                        mm = pe.matmul(TR[:, n * BANK:(n + 1) * BANK], catT[:, k, :],
                                       w_out[:, k, n * BANK:(n + 1) * BANK], start=(k == 0), stop=(k == KD - 1))
                mm.then_inc(s["o_ps"], 1)
                if has_next:
                    project(t + 1, 4)
                pe.wait_ge(s["hn_done"], t + 1)
                for k in range(KD):
                    mm = pe.transpose(SC[:, k * P:(k + 1) * P], hn_sb[:, k * P:(k + 1) * P], ident[:, :])
                mm.then_inc(s["hn_ps"], 1)
                pe.wait_ge(s["hn_sb_done"], t + 1)
                for k in range(KD):
                    mm = pe.matmul(KV[:, 0:E], hnT[:, k, :], w_rt[:, k, :], start=(k == 0), stop=(k == KD - 1))
                mm.then_inc(s["lg_ps"], 1)

            transpose_x(0, 0, False)
            pe.wait_ge(s["dve_setup"], 2)
            for n in range(5):
                project(0, n, False)
            body(0, 0, False, True)
            with pe.Fori(0, 7) as i:
                for u in range(2):
                    body(i * 2 + (1 + u), (1 + u) % 2, True, True)
            body(15, 1, True, False)
            rank(15)
            pe.wait_ge(s["pos_done"], TILES)
            pe.matmul(Y[:, 0:E], ones[:, :], cum[:, :], start=True, stop=True).then_inc(s["totals_ps"], 1)


MAX_TILES = SEQ * TOPK // P + E
LIMIT, ALPHA = 7.0, 1.702
GU_CHUNKS = 2 * FF // BANK


def expert_phase(nc, I, S):
    with ExitStack() as ctx:
        sb = lambda name, shape, dt=F32: ctx.enter_context(nc.sbuf_tensor(name, shape, dt))
        pb = lambda name, w: ctx.enter_context(nc.psum_tensor(name, [P, w], F32))
        sem = lambda name: ctx.enter_context(nc.semaphore(name))

        w_gu = sb("w_gu", [P, KD, 2 * FF])
        w_d = sb("w_d", [P, FF // P, D])
        b_gu = sb("b_gu", [P, 2 * FF])
        b_d = sb("b_d", [P, D])
        ident = sb("ident2", [P, P])
        ids = sb("ids", [P, 1], I32)
        rows = sb("rows", [P, D])
        xT = sb("moe_xT", [P, KD, P])
        pre = sb("pre", [P, 2, BANK])
        gate = sb("gate", [P, 2, BANK // 2])
        tanh = sb("tanh", [P, 2, BANK // 2])
        up = sb("up", [P, 2, BANK // 2])
        acted = sb("acted", [P, FF])
        actT = sb("actT", [P, FF // P, P])
        y_sb = sb("y_sb", [P, D])
        zero = sb("zero_rows", [P, D])

        GU = [pb("GU0", BANK), pb("GU1", BANK)]
        TX = pb("TX", 2 * BANK)
        TA = pb("TA", 2 * BANK)
        Y = pb("Y2", 2 * BANK)

        names = """ident_ready rows_free ids_free ids_seen xT_ps xT_sb gu_in0 gu_in1 gu_in2 gu_in3 wd_in
            gu_ps gu_taken gate_ready tanh_ready acted_ready aT_ps aT_sb y_ps y_taken y_stored y_seen zero_ready zeroed
            dve_chain pool_chain""".split()
        s = {n: sem(n) for n in names}
        gu_in = [s[f"gu_in{c}"] for c in range(GU_CHUNKS)]
        ctx.enter_context(nc.allow_non_contiguous_dma(reason="a tile's token numbers, a word per partition"))
        ctx.callback(clear_semaphores, nc, dict(s))
        s.update({n: S["keep"].enter_context(nc.semaphore(n)) for n in ('ids_in', 'rows_in')})
        block = ctx.enter_context(nc.Block())

        list_t = S["tok_list"].rearrange("(n p) o -> n p o", p=P)
        y_t = S["y"].rearrange("(n p) d -> n p d", p=P)
        CAP_T = CAP // P
        half = BANK // 2

        def experts(eng, body, after=None):
            with eng.Fori(0, E) as e:
                n = eng.value_load(S["n_tiles"][0:1, bass.ds(e, 1)], min_val=1, max_val=CAP_T)
                first = eng.value_load(S["starts"][0:1, bass.ds(e, 1)], min_val=0, max_val=MAX_TILES - 1)
                with eng.Fori(0, n) as t:
                    body(e, t, eng.snap(first + t, min_val=0, max_val=MAX_TILES - 1))

        @block.sync
        def _(sp):
            def load_gu(e, c):
                cols = slice(c * BANK, (c + 1) * BANK)
                w = I["expert_w_gate_up"][0, bass.ds(e, 1), :, cols].squeeze(0).rearrange("(k p) n -> p k n", p=P)
                sp.dma_start(w_gu[:, :, cols], w).then_inc(gu_in[c], 16)
                b = I["expert_b_gate_up"][0, bass.ds(e, 1), cols].squeeze(0)
                sp.dma_start(b_gu[:, cols], b.partition_broadcast(P)).then_inc(gu_in[c], 16)

            def load_down(e):
                w = I["expert_w_down"][0, bass.ds(e, 1)].squeeze(0).rearrange("(k p) n -> p k n", p=P)
                sp.dma_start(w_d[:, :, :], w).then_inc(s["wd_in"], 16)
                b = I["expert_b_down"][0, bass.ds(e, 1)].squeeze(0)
                sp.dma_start(b_d[:, :], b.partition_broadcast(P)).then_inc(s["wd_in"], 16)

            for c in range(GU_CHUNKS):
                load_gu(0, c)
            load_down(0)
            with sp.Fori(1, E) as e:
                done = sp.value_load(S["starts"][0:1, bass.ds(e, 1)], min_val=0, max_val=MAX_TILES - 1)
                for c in range(GU_CHUNKS):
                    sp.wait_ge(s["gu_taken"], done * GU_CHUNKS + c)
                    load_gu(e, c)
                sp.wait_ge(s["y_taken"], done + 1)
                load_down(e)
            total = sp.value_load(S["starts"][0:1, E:E + 1], min_val=E, max_val=MAX_TILES)
            sp.wait_ge(s["zero_ready"], 1)
            with sp.Fori(total, MAX_TILES) as g:
                sp.dma_start(y_t[bass.ds(g, 1)].squeeze(0), zero[:, :]).then_inc(s["zeroed"], 16)
            with sp.Fori(0, total) as g:
                sp.sem_inc(s["zeroed"], 16)
            sp.wait_ge(s["zeroed"], 16 * MAX_TILES)

        @block.gpsimd
        def _(pool):
            ch = Chain(pool, s["pool_chain"])
            ch.link(pool.memset(zero[:, :], 0.0))
            pool.sem_inc(s["zero_ready"], 1)
            ch.link(pool.memset(ident[:, :], 0.0))
            pool.affine_select(out=ident[:, :], in_=ident[:, :], compare_op=ALU.not_equal, fill=1.0, base=0,
                               pattern=[[-1, P]], channel_multiplier=1).then_inc(s["ident_ready"], 1)

            def gather(slot, g):
                pool.dma_start(ids[:, :], list_t[bass.ds(slot, 1)].squeeze(0)).then_inc(s["ids_in"], 16)
                pool.wait_ge(s["xT_ps"], g + 1)
                pool.sem_inc(s["rows_free"], 1)
                pool.wait_ge(s["ids_in"], g * 16 + 16)
                pool.sem_inc(s["ids_seen"], 1)
                pool.indirect_dma_start(rows[:, :], None, S["hn"],
                                        bass.IndirectOffsetOnAxis(ap=ids[:, :], axis=0)).then_inc(s["rows_in"], 16)
                pool.wait_ge(s["rows_in"], g * 16 + 16)
                pool.sem_inc(s["ids_free"], 1)

            experts(pool, lambda e, t, g: gather(e * CAP_T + t, g))
            total = pool.value_load(S["starts"][0:1, E:E + 1], min_val=0, max_val=MAX_TILES)
            gather(0, total)

        @block.scalar
        def _(act):
            def copy_xT(g):
                act.wait_ge(s["xT_ps"], g + 2)
                act.activation(xT[:, 0:4, :], TX[:, 0:BANK], ACT.Copy)
                act.activation(xT[:, 4:8, :], TX[:, BANK:], ACT.Copy).then_inc(s["xT_sb"], 1)

            def copy_actT(g, n):
                act.wait_ge(s["aT_ps"], g * 2 + (n + 1))
                act.activation(actT[:, 4 * n:4 * n + 4, :], TA[:, n * BANK:(n + 1) * BANK], ACT.Copy,
                               scale=0.5).then_inc(s["aT_sb"], 1)

            def body(e, t, g):
                for c in range(GU_CHUNKS):
                    act.wait_ge(s["gate_ready"], g * GU_CHUNKS + (c + 1))
                    act.activation(tanh[:, c % 2, :], gate[:, c % 2, :], ACT.Tanh,
                                   scale=ALPHA / 2).then_inc(s["tanh_ready"], 1)
                    if c == GU_CHUNKS - 2:
                        copy_actT(g, 0)
                copy_xT(g + 1)
                copy_actT(g, 1)
                act.wait_ge(s["y_taken"], g + 2)
                tile = nc.s_assert_within(g, 0, MAX_TILES - 1, skip_runtime_bounds_check_because="the counts sum to MAX_TILES at most")
                act.dma_start(y_t[bass.ds(tile, 1)].squeeze(0), y_sb[:, :]).then_inc(s["y_stored"], 16)

            act.sem_inc(s["y_stored"], 16)
            copy_xT(0)
            experts(act, body)
            total = act.value_load(S["starts"][0:1, E:E + 1], min_val=0, max_val=MAX_TILES)
            act.wait_ge(s["y_stored"], total * 16 + 16)
            act.sem_inc(s["y_seen"], 1)

        @block.vector
        def _(dve):
            ch = Chain(dve, s["dve_chain"])
            dve.sem_inc(s["gu_taken"], 3)
            dve.sem_inc(s["y_taken"], 1)

            def body(e, t, g):
                ch.start(g * EXPERT_LINKS)
                for c in range(GU_CHUNKS):
                    b = c % 2
                    dve.wait_ge(s["gu_ps"], g * GU_CHUNKS + (c + 1))
                    ch.link(dve.tensor_tensor(pre[:, b, :], GU[b][:, :], b_gu[:, c * BANK:(c + 1) * BANK], ALU.add))
                    pair = pre[:, b, :].rearrange("p (j two) -> p j two", two=2)
                    dve.tensor_scalar(gate[:, b, :], pair[:, :, 0], LIMIT, None, ALU.min).then_inc(s["gate_ready"], 1)
                    ch.link(dve.tensor_scalar(up[:, b, :], pair[:, :, 1], LIMIT, -LIMIT, ALU.min, ALU.max))
                    dve.sem_inc(s["gu_taken"], 1)
                    dve.wait_ge(s["tanh_ready"], g * GU_CHUNKS + (c + 1))
                    ch.link(dve.scalar_tensor_tensor(gate[:, b, :], tanh[:, b, :], 1.0, gate[:, b, :],
                                                     ALU.add, ALU.mult))
                    dve.scalar_tensor_tensor(acted[:, c * half:(c + 1) * half], up[:, b, :], 1.0, gate[:, b, :],
                                             ALU.add, ALU.mult).then_inc(s["acted_ready"], 1)
                dve.wait_ge(s["y_ps"], g + 1)
                dve.wait_ge(s["y_stored"], g * 16 + 16)
                dve.tensor_tensor(y_sb[:, :], Y[:, :], b_d[:, :], ALU.add).then_inc(s["y_taken"], 1)
                assert ch.n == EXPERT_LINKS, ch.n

            experts(dve, body)

        @block.tensor
        def _(pe):
            def transpose_rows(g):
                pe.wait_ge(s["rows_in"], g * 16 + 16)
                for k in range(KD):
                    mm = pe.transpose(TX[:, k * P:(k + 1) * P], rows[:, k * P:(k + 1) * P], ident[:, :])
                mm.then_inc(s["xT_ps"], 1)

            def transpose_act(g, n):
                pe.wait_ge(s["acted_ready"], g * GU_CHUNKS + 2 * (n + 1))
                for k in range(4 * n, 4 * n + 4):
                    mm = pe.transpose(TA[:, k * P:(k + 1) * P], acted[:, k * P:(k + 1) * P], ident[:, :])
                mm.then_inc(s["aT_ps"], 1)

            def body(e, t, g):
                def gate_up(c):
                    pe.wait_ge(gu_in[c], e * 32 + 32)
                    if c == 0:
                        pe.wait_ge(s["xT_sb"], g + 1)
                    pe.wait_ge(s["gu_taken"], g * GU_CHUNKS + (c + 2))
                    for k in range(KD):
                        mm = pe.matmul(GU[c % 2][:, :], xT[:, k, :], w_gu[:, k, c * BANK:(c + 1) * BANK],
                                       start=(k == 0), stop=(k == KD - 1))
                    mm.then_inc(s["gu_ps"], 1)

                def down(n, kh):
                    for k in range(4 * kh, 4 * kh + 4):
                        mm = pe.matmul(Y[:, n * BANK:(n + 1) * BANK], actT[:, k, :],
                                       w_d[:, k, n * BANK:(n + 1) * BANK], start=(k == 0), stop=(k == 7))
                    return mm

                for c in range(GU_CHUNKS - 1):
                    gate_up(c)
                transpose_act(g, 0)
                gate_up(GU_CHUNKS - 1)
                transpose_rows(g + 1)
                pe.wait_ge(s["wd_in"], e * 32 + 32)
                pe.wait_ge(s["y_taken"], g + 1)
                pe.wait_ge(s["aT_sb"], g * 2 + 1)
                down(0, 0)
                transpose_act(g, 1)
                down(1, 0)
                pe.wait_ge(s["aT_sb"], g * 2 + 2)
                down(0, 1)
                down(1, 1).then_inc(s["y_ps"], 1)

            pe.sem_inc(s["xT_ps"], 1)
            pe.wait_ge(s["ident_ready"], 1)
            transpose_rows(0)
            experts(pe, body)


EXPERT_LINKS = 3 * GU_CHUNKS


PLE = 256
Q_RANK, KV_RANK, ROPE_D, ATTN_W, SSM_W = 256, 128, 64, 512, 512
Z_COLS = Q_RANK + KV_RANK + ROPE_D + ATTN_W + 2 * SSM_W
Z_KV, Z_KR, Z_GA = Q_RANK, Q_RANK + KV_RANK, Q_RANK + KV_RANK + ROPE_D
Z_U, Z_GS = Z_GA + ATTN_W, Z_GA + ATTN_W + SSM_W
Z_CHUNKS = [(c, min(c + BANK, Z_COLS)) for c in range(0, Z_COLS, BANK)]
EPS = 1e-6


def is_step(t, n):
    return isinstance(t, int) and t == n


def make_identity(pool, ch, ident, done):
    ch.link(pool.memset(ident, 0.0))
    pool.affine_select(out=ident, in_=ident, compare_op=ALU.not_equal, fill=1.0, base=0,
                       pattern=[[-1, P]], channel_multiplier=1).then_inc(done, 1)


def inv_rms(dve, ch, y, total, t, count, eps, done=None):
    ch.link(dve.tensor_scalar(total, total, 1.0 / count, eps, ALU.mult, ALU.add))
    rsqrt(dve, ch, y, total, t, done)


INV_RMS_LINKS = 12


def combine_phase(nc, I, S):
    with ExitStack() as ctx:
        sb = lambda name, shape, dt=F32: ctx.enter_context(nc.sbuf_tensor(name, shape, dt))
        pb = lambda name, w: ctx.enter_context(nc.psum_tensor(name, [P, w], F32))
        sem = lambda name: ctx.enter_context(nc.semaphore(name))

        w_gate = sb("w_gate", [P, KD, D])
        w_ple = sb("w_ple", [P, PLE // P, D])
        w_in = sb("w_in2", [P, KD, Z_COLS])
        gain_ple = sb("gain_ple", [P, KD])
        gain_pre = sb("gain_pre", [P, KD])
        gain_final = sb("gain_final", [P, D])
        ident = sb("ident3", [P, P])
        slots = [sb(f"slots{u}", [P, TOPK], I32) for u in range(2)]
        y_rows = sb("y_rows", [P, 2, TOPK, D])
        h = sb("h", [P, 2, D])
        p_sb = sb("p_sb", [P, 2, PLE])
        hT = sb("hT", [P, KD, P])
        pT = sb("pT", [P, PLE // P, P])
        x2T = sb("x2T", [P, KD, P])
        tanh = sb("tanh3", [P, D])
        z_sb = sb("z_sb", [P, 2, Z_COLS])
        squares = sb("squares3", [P, D], mybir.dt.bfloat16)
        ss_h, ss_3, ss_2, rstd_h, rstd_3, nt = (sb(n, [P, 1]) for n in ("ss_h", "ss_3", "ss_2", "rstd_h", "rstd_3", "nt"))
        rstd_2 = sb("rstd_2", [P, 2])

        TR = pb("TR3", 2 * BANK)
        G = pb("G3", 2 * BANK)
        PP = pb("PP3", 2 * BANK)
        Z = [pb("Z0", BANK), pb("Z1", BANK)]

        names = """gains gate_in ple_in proj_in ident_ready gate_scaled proj_scaled y_seen y_used h_loaded h2_done hT_ps hT_sb pT_ps
            pT_sb sumsq_h rstd_h_ready g_ps tanh_done pp_ps h3_done sumsq_3 x2_done sumsq_2 rstd_2_ready x2T_ps x2T_sb
            z_ps z_sb x2_stored z_stored dve_chain pool_chain""".split()
        s = {n: sem("c_" + n) for n in names}
        ctx.enter_context(nc.allow_non_contiguous_dma(reason="gains, a word per partition"))
        ctx.callback(clear_semaphores, nc, dict(s))
        s.update({n: S["keep"].enter_context(nc.semaphore(n)) for n in ('y_in',)})
        block = ctx.enter_context(nc.Block())

        tiles = lambda ap: ap.rearrange("(t p) d -> t p d", p=P)
        h_t, x2_t, z_t, p_t = tiles(S["h1"]), tiles(S["x2"]), tiles(S["z"]), tiles(I["p"][0, 0])

        @block.sync
        def _(sp):
            def load(t, par):
                sp.dma_start(h[:, par, :], h_t[bass.ds(t, 1)].squeeze(0)).then_inc(s["h_loaded"], 16)
                sp.dma_start(p_sb[:, par, :], p_t[bass.ds(t, 1)].squeeze(0)).then_inc(s["h_loaded"], 16)

            def store(t, par, has_next):
                sp.wait_ge(s["x2_done"], t + 1)
                sp.dma_start(x2_t[bass.ds(t, 1)].squeeze(0), h[:, par, :]).then_inc(s["x2_stored"], 16)
                if has_next:
                    sp.wait_ge(s["sumsq_2"], t + 1)
                    sp.wait_ge(s["x2T_ps"], t + 1)
                    sp.wait_ge(s["x2_stored"], t * 16 + 16)
                    load(t + 2, par)
                sp.wait_ge(s["z_sb"], (t + 1) * len(Z_CHUNKS))
                if not is_step(t, 0):
                    sp.wait_ge(s["z_stored"], t * 16)
                sp.dma_start(z_t[bass.ds(t, 1)].squeeze(0), z_sb[:, par, :]).then_inc(s["z_stored"], 16)

            load(0, 0)
            sp.dma_start(gain_ple[:, :], I["norm_ple_w"][0].rearrange("(k p) -> p k", p=P)).then_inc(s["gains"], 16)
            sp.dma_start(gain_pre[:, :], I["pre_norm_g_2"][0].rearrange("(k p) -> p k", p=P)).then_inc(s["gains"], 16)
            sp.dma_start(gain_final[:, :], I["final_norm_w"].partition_broadcast(P)).then_inc(s["gains"], 16)
            for k in range(KD):
                sp.dma_start(w_gate[:, k, :], I["ple_gate_w"][0, k * P:(k + 1) * P, :]).then_inc(s["gate_in"], 16)
            for k in range(PLE // P):
                sp.dma_start(w_ple[:, k, :], I["ple_proj_w"][0, k * P:(k + 1) * P, :]).then_inc(s["ple_in"], 16)
            for k in range(KD):
                sp.dma_start(w_in[:, k, :], I["w_in_2"][0, k * P:(k + 1) * P, :]).then_inc(s["proj_in"], 16)
            sp.wait_ge(s["h_loaded"], 32)
            load(1, 1)
            for t in (0, 1):
                store(t, t, True)
            with sp.Fori(1, TILES // 2 - 1) as i:
                for u in range(2):
                    store(i * 2 + u, u, True)
            for t in (TILES - 2, TILES - 1):
                store(t, t % 2, False)
            sp.wait_ge(s["x2_stored"], 16 * TILES)
            sp.wait_ge(s["z_stored"], 16 * TILES)

        @block.gpsimd
        def _(pool):
            ch = Chain(pool, s["pool_chain"])
            make_identity(pool, ch, ident[:, :], s["ident_ready"])

            def gather(t, par, has_prev):
                if has_prev:
                    pool.wait_ge(s["y_used"], t - 1)
                    pool.sem_inc(s["y_seen"], 1)
                ch.link(pool.tensor_copy(slots[par][:, :], S["pos"][:, bass.ds(t * TOPK, TOPK)]))
                pool.sem_inc(s["y_seen"], 1)
                for k in range(TOPK):
                    pool.indirect_dma_start(y_rows[:, par, k, :], None, S["y"], bass.IndirectOffsetOnAxis(
                        ap=slots[par][:, k:k + 1], axis=0)).then_inc(s["y_in"], 16)
                pool.wait_ge(s["y_in"], t * (16 * TOPK) + 16 * TOPK)
                pool.sem_inc(s["y_seen"], 1)

            gather(0, 0, False)
            gather(1, 1, False)
            base = ch.n
            with pool.Fori(1, TILES // 2) as i:
                ch.start(i * 2 + (base - 2))
                for u in range(2):
                    gather(i * 2 + u, u, True)

        @block.scalar
        def _(act):
            def square_h(t, par):
                act.wait_ge(s["h2_done"], t + 1)
                act.activation(squares[:, :], h[:, par, :], ACT.Square, accum_out=ss_h[:, :]).then_inc(s["sumsq_h"], 1)

            def copy_hT(t):
                act.wait_ge(s["hT_ps"], t + 1)
                act.activation(hT[:, 0:4, :], TR[:, 0:BANK], ACT.Copy)
                act.activation(hT[:, 4:8, :], TR[:, BANK:], ACT.Copy).then_inc(s["hT_sb"], 1)
                act.wait_ge(s["pT_ps"], t + 1)
                act.activation(pT[:, :, :], PP[:, 0:PLE], ACT.Copy).then_inc(s["pT_sb"], 1)

            def copy_x2T(t):
                act.wait_ge(s["x2T_ps"], t + 1)
                act.activation(x2T[:, 0:4, :], TR[:, 0:BANK], ACT.Copy)
                act.activation(x2T[:, 4:8, :], TR[:, BANK:], ACT.Copy).then_inc(s["x2T_sb"], 1)

            def gate(t):
                act.wait_ge(s["g_ps"], t + 1)
                act.wait_ge(s["rstd_h_ready"], t + 1)
                act.activation(tanh[:, 0:BANK], G[:, 0:BANK], ACT.Tanh, scale=rstd_h[:, :])
                act.activation(tanh[:, BANK:], G[:, BANK:], ACT.Tanh, scale=rstd_h[:, :]).then_inc(s["tanh_done"], 1)

            def square_3(t, par):
                act.wait_ge(s["h3_done"], t + 1)
                act.activation(squares[:, :], h[:, par, :], ACT.Square, accum_out=ss_3[:, :]).then_inc(s["sumsq_3"], 1)

            def square_2(t, par):
                act.wait_ge(s["x2_done"], t + 1)
                act.activation(squares[:, :], h[:, par, :], ACT.Square, accum_out=ss_2[:, :]).then_inc(s["sumsq_2"], 1)

            def copy_z(t, par, n, has_prev):
                lo, hi = Z_CHUNKS[n]
                act.wait_ge(s["z_ps"], t * len(Z_CHUNKS) + (n + 1))
                if n == 0:
                    act.wait_ge(s["rstd_2_ready"], t + 1)
                    if has_prev:
                        act.wait_ge(s["z_stored"], t * 16 - 16)
                act.activation(z_sb[:, par, lo:hi], Z[n % 2][:, 0:hi - lo], ACT.Copy,
                               scale=rstd_2[:, par:par + 1]).then_inc(s["z_sb"], 1)

            def body(t, par, has_next, has_prev):
                if has_next:
                    square_h(t, par)
                    copy_hT(t)
                if not is_step(t, 0):
                    copy_x2T(t - 1)
                if has_next:
                    gate(t)
                    square_3(t, par)
                if not is_step(t, 0):
                    copy_z(t - 1, 1 - par, 0, has_prev)
                if has_next:
                    square_2(t, par)
                if not is_step(t, 0):
                    for n in range(1, len(Z_CHUNKS)):
                        copy_z(t - 1, 1 - par, n, has_prev)

            body(0, 0, True, False)
            act.wait_ge(s["gains"], 48)
            for k in range(KD):
                act.wait_ge(s["proj_in"], 16 * KD)
                act.activation(w_in[:, k, :], w_in[:, k, :], ACT.Copy, scale=gain_pre[:, k:k + 1]).then_inc(s["proj_scaled"], 1)
            body(1, 1, True, False)
            body(2, 0, True, False)
            with act.Fori(1, TILES // 2 - 1) as i:
                body(i * 2 + 1, 1, True, True)
                body(i * 2 + 2, 0, True, True)
            body(TILES - 1, 1, True, True)
            body(TILES, 0, False, True)

        @block.vector
        def _(dve):
            ch = Chain(dve, s["dve_chain"])

            def combine(t, par):
                dve.wait_ge(s["y_in"], t * (16 * TOPK) + 16 * TOPK)
                dve.wait_ge(s["h_loaded"], t * 32 + 32)
                for k in range(TOPK):
                    last = dve.scalar_tensor_tensor(h[:, par, :], y_rows[:, par, k, :], S["gates"][:, bass.ds(t * TOPK + k, 1)],
                                                    h[:, par, :], ALU.mult, ALU.add)
                    if k < TOPK - 1:
                        ch.link(last)
                ch.link(last)
                dve.sem_inc(s["y_used"], 1)
                dve.sem_inc(s["h2_done"], 1)
                dve.wait_ge(s["sumsq_h"], t + 1)
                inv_rms(dve, ch, rstd_h[:, :], ss_h[:, :], nt[:, :], D, NORM_EPS)
                dve.tensor_scalar(rstd_h[:, :], rstd_h[:, :], 0.5, None, ALU.mult).then_inc(s["rstd_h_ready"], 1)

            def finish(t, par, has_prev):
                dve.wait_ge(s["tanh_done"], t + 1)
                dve.wait_ge(s["pp_ps"], t + 1)
                ch.link(dve.scalar_tensor_tensor(tanh[:, :], tanh[:, :], 1.0, PP[:, :], ALU.add, ALU.mult))
                dve.scalar_tensor_tensor(h[:, par, :], tanh[:, :], 0.5, h[:, par, :],
                                         ALU.mult, ALU.add).then_inc(s["h3_done"], 1)
                dve.wait_ge(s["sumsq_3"], t + 1)
                inv_rms(dve, ch, rstd_3[:, :], ss_3[:, :], nt[:, :], D, NORM_EPS)
                dve.scalar_tensor_tensor(h[:, par, :], h[:, par, :], rstd_3[:, :], gain_final[:, :],
                                         ALU.mult, ALU.mult).then_inc(s["x2_done"], 1)
                dve.wait_ge(s["sumsq_2"], t + 1)
                if has_prev:
                    dve.wait_ge(s["z_sb"], (t - 1) * len(Z_CHUNKS))
                inv_rms(dve, ch, rstd_2[:, par:par + 1], ss_2[:, :], nt[:, :], D, EPS, s["rstd_2_ready"])

            combine(0, 0)
            dve.wait_ge(s["gains"], 48)
            dve.wait_ge(s["gate_in"], 16 * KD)
            for k in range(KD):
                dve.tensor_scalar(w_gate[:, k, :], w_gate[:, k, :], gain_ple[:, k:k + 1], None, ALU.mult).then_inc(s["gate_scaled"], 1)
            base, first = ch.n, True
            for t in (0, 1):
                finish(t, t, False)
                combine(t + 1, 1 - t)
            with dve.Fori(1, TILES // 2 - 1) as i:
                per = (ch.n - base)
                ch.start(i * per + base)
                for u in range(2):
                    finish(i * 2 + u, u, True)
                    combine(i * 2 + (u + 1), 1 - u)
                assert ch.n == per, ch.n
            ch.start(base + per * (TILES // 2 - 1))
            finish(TILES - 2, 0, True)
            combine(TILES - 1, 1)
            finish(TILES - 1, 1, True)

        @block.tensor
        def _(pe):
            pe.wait_ge(s["ident_ready"], 1)

            def body(t, par, has_prev, has_next):
                if has_next:
                    pe.wait_ge(s["h2_done"], t + 1)
                    if has_prev:
                        pe.wait_ge(s["x2T_sb"], t - 1)
                    for k in range(KD):
                        mm = pe.transpose(TR[:, k * P:(k + 1) * P], h[:, par, k * P:(k + 1) * P], ident[:, :])
                    mm.then_inc(s["hT_ps"], 1)
                    if not is_step(t, 0):
                        pe.wait_ge(s["h3_done"], t)
                    for k in range(PLE // P):
                        mm = pe.transpose(PP[:, k * P:(k + 1) * P], p_sb[:, par, k * P:(k + 1) * P], ident[:, :])
                    mm.then_inc(s["pT_ps"], 1)
                    pe.wait_ge(s["hT_sb"], t + 1)
                    if is_step(t, 0):
                        pe.wait_ge(s["gate_scaled"], KD)
                    else:
                        pe.wait_ge(s["tanh_done"], t)
                    for n in range(2):
                        for k in range(KD):
                            mm = pe.matmul(G[:, n * BANK:(n + 1) * BANK], hT[:, k, :], w_gate[:, k, n * BANK:(n + 1) * BANK],
                                           start=(k == 0), stop=(k == KD - 1))
                    mm.then_inc(s["g_ps"], 1)
                if not is_step(t, 0):
                    pe.wait_ge(s["x2_done"], t)
                    for k in range(KD):
                        mm = pe.transpose(TR[:, k * P:(k + 1) * P], h[:, 1 - par, k * P:(k + 1) * P], ident[:, :])
                    mm.then_inc(s["x2T_ps"], 1)
                if has_next:
                    pe.wait_ge(s["pT_sb"], t + 1)
                    if is_step(t, 0):
                        pe.wait_ge(s["ple_in"], 16 * (PLE // P))
                    for n in range(2):
                        for k in range(PLE // P):
                            mm = pe.matmul(PP[:, n * BANK:(n + 1) * BANK], pT[:, k, :], w_ple[:, k, n * BANK:(n + 1) * BANK],
                                           start=(k == 0), stop=(k == PLE // P - 1))
                    mm.then_inc(s["pp_ps"], 1)
                if not is_step(t, 0):
                    pe.wait_ge(s["x2T_sb"], t)
                    if is_step(t, 1):
                        pe.wait_ge(s["proj_scaled"], KD)
                    for n, (lo, hi) in enumerate(Z_CHUNKS):
                        if has_prev or n > 1:
                            pe.wait_ge(s["z_sb"], (t - 1) * len(Z_CHUNKS) + (n - 1))
                        for k in range(KD):
                            mm = pe.matmul(Z[n % 2][:, 0:hi - lo], x2T[:, k, :], w_in[:, k, lo:hi],
                                           start=(k == 0), stop=(k == KD - 1))
                        mm.then_inc(s["z_ps"], 1)

            body(0, 0, False, True)
            body(1, 1, False, True)
            with pe.Fori(1, TILES // 2) as i:
                body(i * 2, 0, True, True)
                body(i * 2 + 1, 1, True, True)
            body(TILES, 0, True, False)


A_HEADS, NOPE, VD = 4, 128, 128
QH = NOPE + ROPE_D
A_SCALE = QH ** -0.5
Z_ATTN = Z_GA
QUADS = TILES // 4
ATTN_LINKS = A_HEADS + 2


def attention_phase(nc, I, S):
    with ExitStack() as ctx:
        sb = lambda name, shape, dt=F32: ctx.enter_context(nc.sbuf_tensor(name, shape, dt))
        pb = lambda name, w: ctx.enter_context(nc.psum_tensor(name, [P, w], F32))
        sem = lambda name: ctx.enter_context(nc.semaphore(name))

        w_uq = sb("w_uq", [P, 2, A_HEADS, QH])
        w_rope = sb("w_rope", [P, 2, 2, A_HEADS, ROPE_D])
        w_ukv = sb("w_ukv", [P, A_HEADS, NOPE + VD])
        gain_q = sb("gain_q", [P, 2])
        gain_kv = sb("gain_kv", [P, 1])
        ident = sb("ident4", [P, P])
        freq_row = sb("freq_row", [P, P])
        freq_col = sb("freq_col", [P, 1])
        cosT = sb("cosT", [P, SEQ])
        sinT = sb("sinT", [P, SEQ])
        kr4 = sb("kr4", [P, TILES, 2, 2, ROPE_D])
        ss = sb("ss4", [P, 2, TILES])
        rstd = sb("rstd4", [P, 2, TILES])
        nt = sb("nt4", [P, 2, TILES])
        zqT = sb("zqT", [P, 2, SEQ])
        squares = (zqT[:, :, :].rearrange("p k c -> p (k c)").bitcast(mybir.dt.bfloat16)[:, 0:TILES * Z_KR]
                   .rearrange("p (t c) -> p t c", t=TILES))
        zkvT = sb("zkvT", [P, SEQ])
        kT = sb("kT4", [P, A_HEADS, SEQ])
        krT = sb("krT", [P, SEQ])
        kr_sin = sb("kr_sin", [P, BANK])
        v = sb("v4", [P, TILES, A_HEADS * VD])
        z_in = v[:, :, 0:Z_ATTN]
        qn = sb("qn", [P, 2, A_HEADS, P])
        qr = sb("qr", [P, 2, A_HEADS // 2, P])
        qr_cos = sb("qr_cos", [P, 2, P])
        qr_sin = sb("qr_sin", [P, 2, P])
        probs = sb("probs", [P, 2, SEQ])
        turns, pos_i = probs[:, 0, :], probs[:, 1, :].bitcast(I32)
        probsT = sb("probsT", [P, 4, BANK])
        top = sb("top", [P, 1])
        ntop = sb("ntop4", [P, 2])
        sums = sb("sums", [P, 2, A_HEADS])
        recip = sb("recip", [P, A_HEADS])
        o_sb = sb("o_sb", [P, 2, A_HEADS * VD])

        SC = pb("SC4", 4 * BANK)
        PT = [pb("PT0", BANK), pb("PT1", BANK)]
        Q = pb("Q4", BANK)
        O = pb("O4", BANK)

        names = """weights positions z_in0 z_in1 z_in2 z_in3 ident_ready freq_ready w_ready angles_ready sines cos_ready
            sumsq scaled tq_ps t_sb kr_sb kT_ps kT_sb v_ps v_sb q_ps q_nope_sb q_rope_sb sc_ps max_done exp_done
            pt_ps pt_act pt_dve o_ps o_done o_seen o_stored dve_chain pool_chain""".split()
        s = {n: sem("a_" + n) for n in names}
        z_ins = [s[f"z_in{g}"] for g in range(QUADS)]
        ctx.enter_context(nc.allow_non_contiguous_dma(reason="gains, a word per partition"))
        ctx.callback(clear_semaphores, nc, s)
        block = ctx.enter_context(nc.Block())

        attn_t = S["attn"].rearrange("(t p) d -> t p d", p=P)

        def halves(ap):
            return ap.rearrange("p (two f) -> p two f", two=2)

        @block.sync
        def _(sp):
            sp.dma_start(pos_i, I["positions_2"][0].partition_broadcast(P)).then_inc(s["positions"], 16)
            for g in range(QUADS):
                src = S["z"][g * BANK:(g + 1) * BANK, 0:Z_ATTN].rearrange("(t p) d -> p t d", p=P)
                sp.dma_start(z_in[:, 4 * g:4 * g + 4, :], src).then_inc(z_ins[g], 16)
            sp.dma_start(gain_q[:, :], I["q_norm_g_2"][0].rearrange("(k p) -> p k", p=P)).then_inc(s["weights"], 16)
            sp.dma_start(gain_kv[:, :], I["kv_norm_g_2"][0].rearrange("(k p) -> p k", p=P)).then_inc(s["weights"], 16)
            sp.dma_start(w_uq[:, :, :, :], I["w_uq_2"][0].rearrange("(k p) (h n) -> p k h n", p=P, h=A_HEADS)).then_inc(s["weights"], 16)
            sp.dma_start(w_ukv[:, :, :], I["w_ukv_2"][0].rearrange("p (h n) -> p h n", h=A_HEADS)).then_inc(s["weights"], 16)

            def store(t, par):
                sp.wait_ge(s["o_done"], t + 1)
                sp.sem_inc(s["o_seen"], 1)
                if not is_step(t, 0):
                    sp.wait_ge(s["o_stored"], t * 16)
                sp.dma_start(attn_t[bass.ds(t, 1)].squeeze(0), o_sb[:, par, :]).then_inc(s["o_stored"], 16)

            store(0, 0)
            store(1, 1)
            with sp.Fori(1, TILES // 2) as i:
                for u in range(2):
                    store(i * 2 + u, u)
            sp.wait_ge(s["o_stored"], 16 * TILES)

        @block.gpsimd
        def _(pool):
            ch = Chain(pool, s["pool_chain"])
            make_identity(pool, ch, ident[:, :], s["ident_ready"])
            for j in range(ROPE_HALF):
                last = pool.memset(freq_row[:, :].rearrange("p (r f) -> p r f", f=ROPE_HALF)[:, :, j], INV_FREQ[j])
            last.then_inc(s["freq_ready"], 1)

        @block.scalar
        def _(act):
            act.wait_ge(s["angles_ready"], 1)
            act.activation(sinT[:, :], cosT[:, :], ACT.Sin)
            act.activation(cosT[:, :], cosT[:, :], ACT.Sin, scale=0.5).then_inc(s["sines"], 1)
            for t in range(TILES):
                act.wait_ge(z_ins[t // 4], 16)
                act.activation(squares[:, t, 0:Q_RANK], z_in[:, t, 0:Q_RANK], ACT.Square, accum_out=ss[:, 0, t:t + 1])
                act.activation(squares[:, t, Z_KV:Z_KR], z_in[:, t, Z_KV:Z_KR], ACT.Square,
                               accum_out=ss[:, 1, t:t + 1]).then_inc(s["sumsq"], 1)
            for g in range(QUADS):
                cols = slice(g * BANK, (g + 1) * BANK)
                for i, dst in enumerate((zqT[:, 0, cols], zqT[:, 1, cols], zkvT[:, cols])):
                    act.wait_ge(s["tq_ps"], 5 * g + i + 1)
                    act.activation(dst, SC[:, i * BANK:(i + 1) * BANK], ACT.Copy).then_inc(s["t_sb"], 1)
            for j in range(A_HEADS * QUADS):
                h, g = j % A_HEADS, j // A_HEADS
                act.wait_ge(s["kT_ps"], j + 1)
                act.activation(kT[:, h, g * BANK:(g + 1) * BANK], PT[j % 2][:, :], ACT.Copy).then_inc(s["kT_sb"], 1)

            def copy_q(t, par):
                act.wait_ge(s["q_ps"], t * 2 + 1)
                act.activation(qn[:, par, :, :], Q[:, :], ACT.Copy).then_inc(s["q_nope_sb"], 1)

            def exps(u, par, h):
                act.wait_ge(s["max_done"], u + 1)
                act.activation(probs[:, h % 2, :], SC[:, :], ACT.Exp, scale=A_SCALE, bias=ntop[:, h % 2:h % 2 + 1],
                               accum_out=sums[:, par, h:h + 1]).then_inc(s["exp_done"], 1)

            def body(t, par, has_next):
                for h in range(A_HEADS):
                    u = t * A_HEADS + h
                    for j in range(2):
                        act.wait_ge(s["pt_ps"], u * 4 + (j + 1))
                        act.activation(probsT[:, j, :], PT[j][:, :], ACT.Copy).then_inc(s["pt_act"], 1)
                    if h < A_HEADS - 1:
                        exps(u + 1, par, h + 1)
                    elif has_next:
                        exps(u + 1, 1 - par, 0)
                    if h == 0 and has_next:
                        copy_q(t + 1, 1 - par)

            copy_q(0, 0)
            exps(0, 0, 0)
            with act.Fori(0, TILES // 2 - 1) as i:
                for w in range(2):
                    body(i * 2 + w, w, True)
            body(TILES - 2, 0, True)
            body(TILES - 1, 1, False)

        @block.vector
        def _(dve):
            ch = Chain(dve, s["dve_chain"])
            dve.wait_ge(s["freq_ready"], 1)
            dve.wait_ge(s["ident_ready"], 1)
            ch.link(dve.tensor_tensor(freq_row[:, :], freq_row[:, :], ident[:, :], ALU.mult))
            ch.link(dve.tensor_reduce(freq_col[:, :], freq_row[:, :], AX, ALU.add))
            dve.wait_ge(s["positions"], 16)
            ch.link(dve.tensor_copy(cosT[:, :], pos_i))
            ch.link(dve.tensor_scalar(cosT[:, :], cosT[:, :], freq_col[:, :], None, ALU.mult))
            reduce_angles(dve, ch, cosT[:, :], turns)
            dve.sem_inc(s["angles_ready"], 1)
            dve.wait_ge(s["weights"], 64)
            for k in range(2):
                ch.link(dve.tensor_scalar(w_uq[:, k, :, :], w_uq[:, k, :, :], gain_q[:, k:k + 1], None, ALU.mult))
            dve.tensor_scalar(w_ukv[:, :, :], w_ukv[:, :, :], gain_kv[:, :], None, ALU.mult)
            half = ROPE_D // 2
            dve.tensor_copy(w_rope[:, 0, :, :, :], w_uq[:, :, :, NOPE:])
            dve.tensor_scalar(w_rope[:, 1, :, :, 0:half], w_uq[:, :, :, NOPE + half:QH], -1.0, None, ALU.mult)
            dve.tensor_copy(w_rope[:, 1, :, :, half:ROPE_D], w_uq[:, :, :, NOPE:NOPE + half]).then_inc(s["w_ready"], 1)
            dve.wait_ge(s["sines"], 1)
            ch.link(dve.tensor_tensor(cosT[:, :], cosT[:, :], cosT[:, :], ALU.mult))
            dve.tensor_scalar(cosT[:, :], cosT[:, :], -2.0, 1.0, ALU.mult, ALU.add).then_inc(s["cos_ready"], 1)
            for g in range(QUADS):
                dve.wait_ge(z_ins[g], 16)
                ts = slice(4 * g, 4 * g + 4)
                kr = z_in[:, ts, Z_KR:Z_ATTN].unsqueeze(2)
                dve.tensor_copy(kr4[:, ts, 0, :, :], kr.to_broadcast([P, 4, 2, ROPE_D]))
                dve.tensor_scalar(kr4[:, ts, 1, :, 0:half], kr[:, :, :, half:].to_broadcast([P, 4, 2, half]), -1.0, None, ALU.mult)
                dve.tensor_copy(kr4[:, ts, 1, :, half:], kr[:, :, :, 0:half].to_broadcast([P, 4, 2, half]))
            dve.wait_ge(s["sumsq"], TILES)
            dve.tensor_scalar(ss[:, 0, :], ss[:, 0, :], 1.0 / Q_RANK, EPS, ALU.mult, ALU.add)
            ch.link(dve.tensor_scalar(ss[:, 1, :], ss[:, 1, :], 1.0 / KV_RANK, EPS, ALU.mult, ALU.add))
            rsqrt(dve, ch, rstd[:, :, :], ss[:, :, :], nt[:, :, :])
            for t in range(TILES):
                dve.tensor_scalar(z_in[:, t, 0:Q_RANK], z_in[:, t, 0:Q_RANK], rstd[:, 0, t:t + 1], None, ALU.mult)
                dve.tensor_scalar(z_in[:, t, Z_KV:Z_KR], z_in[:, t, Z_KV:Z_KR], rstd[:, 1, t:t + 1], None,
                                  ALU.mult).then_inc(s["scaled"], 1)
            for g in range(QUADS):
                cols = slice(g * BANK, (g + 1) * BANK)
                dve.wait_ge(s["tq_ps"], 5 * g + 5)
                dve.tensor_tensor(krT[:, cols], SC[:, 3 * BANK:4 * BANK], cosT[:, cols], ALU.mult)
                ch.link(dve.tensor_tensor(kr_sin[:, :], Q[:, :], sinT[:, cols], ALU.mult))
                dve.tensor_tensor(krT[:, cols], krT[:, cols], kr_sin[:, :], ALU.add).then_inc(s["kr_sb"], 1)
            for t in range(TILES):
                dve.wait_ge(s["v_ps"], t + 1)
                dve.tensor_copy(v[:, t, :], (Q, O)[t % 2][:, :]).then_inc(s["v_sb"], 1)

            def rope_q(t, par):
                dve.wait_ge(s["q_ps"], t * 2 + 2)
                q = Q[:, :].rearrange("p (a r c) -> p a r c", a=2, r=2)
                tok = bass.ds(t * P, P)
                dve.tensor_tensor(qr_cos[:, :, :], q[:, :, 0, :], cosT[:, tok].unsqueeze(1).to_broadcast([P, 2, P]), ALU.mult)
                ch.link(dve.tensor_tensor(qr_sin[:, :, :], q[:, :, 1, :], sinT[:, tok].unsqueeze(1).to_broadcast([P, 2, P]), ALU.mult))
                dve.tensor_tensor(qr[:, par, :, :], qr_cos[:, :, :], qr_sin[:, :, :], ALU.add).then_inc(s["q_rope_sb"], 1)

            def maxima(u, h):
                dve.wait_ge(s["sc_ps"], u + 1)
                ch.link(dve.tensor_reduce(top[:, :], SC[:, :], AX, ALU.max))
                dve.tensor_scalar(ntop[:, h % 2:h % 2 + 1], top[:, :], -A_SCALE, None, ALU.mult).then_inc(s["max_done"], 1)

            def body(t, par, has_prev, has_next):
                for h in range(A_HEADS):
                    u = t * A_HEADS + h
                    if h < A_HEADS - 1 or has_next:
                        maxima(u + 1, (h + 1) % A_HEADS)
                    for j in (2, 3):
                        dve.wait_ge(s["pt_ps"], u * 4 + (j + 1))
                        dve.tensor_copy(probsT[:, j, :], PT[j % 2][:, :]).then_inc(s["pt_dve"], 1)
                    if h == 1 and has_next:
                        rope_q(t + 1, 1 - par)
                dve.wait_ge(s["o_ps"], t + 1)
                if has_prev:
                    dve.wait_ge(s["o_stored"], t * 16 - 16)
                ch.link(dve.reciprocal(recip[:, :], sums[:, par, :]))
                o = O[:, :].rearrange("p (h e) -> p h e", h=A_HEADS)
                dve.tensor_tensor(o_sb[:, par, :].rearrange("p (h e) -> p h e", h=A_HEADS), o,
                                  recip[:, :].unsqueeze(2).to_broadcast([P, A_HEADS, VD]), ALU.mult).then_inc(s["o_done"], 1)

            rope_q(0, 0)
            maxima(0, 0)
            for t in (0, 1):
                body(t, t, False, True)
            base = ch.n
            with dve.Fori(1, TILES // 2 - 1) as i:
                ch.start(i * (2 * ATTN_LINKS) + (base - 2 * ATTN_LINKS))
                for w in range(2):
                    body(i * 2 + w, w, True, True)
                assert ch.n == 2 * ATTN_LINKS, ch.n
            ch.start(base + (TILES // 2 - 2) * 2 * ATTN_LINKS)
            body(TILES - 2, 0, True, True)
            body(TILES - 1, 1, True, False)

        @block.tensor
        def _(pe):
            pe.wait_ge(s["ident_ready"], 1)
            for g in range(QUADS):
                pe.wait_ge(s["scaled"], 4 * g + 4)
                for i in range(5):
                    if g > 0 and i < 3:
                        pe.wait_ge(s["t_sb"], 3 * (g - 1) + i + 1)
                    if g > 0 and i == 3:
                        pe.wait_ge(s["kr_sb"], g)
                    dst = SC[:, i * BANK:(i + 1) * BANK] if i < 4 else Q[:, :]
                    for j in range(4):
                        t = 4 * g + j
                        src = (z_in[:, t, i * P:(i + 1) * P] if i < 3 else
                               kr4[:, t, i - 3, :, :].rearrange("p two d -> p (two d)"))
                        mm = pe.transpose(dst[:, j * P:(j + 1) * P], src, ident[:, :])
                    mm.then_inc(s["tq_ps"], 1)
            pe.wait_ge(s["w_ready"], 1)
            pe.wait_ge(s["t_sb"], 3 * QUADS)
            pe.wait_ge(s["kr_sb"], QUADS)
            for j in range(A_HEADS * QUADS):
                h, g = j % A_HEADS, j // A_HEADS
                if j > 1:
                    pe.wait_ge(s["kT_sb"], j - 1)
                pe.matmul(PT[j % 2][:, :], w_ukv[:, h, 0:NOPE], zkvT[:, g * BANK:(g + 1) * BANK],
                          start=True, stop=True).then_inc(s["kT_ps"], 1)
                if j > 1:
                    pe.wait_ge(s["v_sb"], j - 1)
                pe.matmul((Q, O)[j % 2][:, :], zkvT[:, j * P:(j + 1) * P], w_ukv[:, :, NOPE:],
                          start=True, stop=True).then_inc(s["v_ps"], 1)

            def q_nope(t):
                tok = bass.ds(t * P, P)
                for h in range(A_HEADS):
                    for k in range(2):
                        mm = pe.matmul(Q[:, h * P:(h + 1) * P], w_uq[:, k, h, 0:NOPE], zqT[:, k, tok],
                                       start=(k == 0), stop=(k == 1))
                mm.then_inc(s["q_ps"], 1)

            def q_rope(t):
                tok = bass.ds(t * P, P)
                pe.wait_ge(s["q_nope_sb"], t + 1)
                for a in range(A_HEADS // 2):
                    for r in range(2):
                        for k in range(2):
                            w = w_rope[:, r, k, 2 * a:2 * a + 2, :].rearrange("p h d -> p (h d)")
                            mm = pe.matmul(Q[:, (2 * a + r) * P:(2 * a + r + 1) * P], w, zqT[:, k, tok],
                                           start=(k == 0), stop=(k == 1))
                mm.then_inc(s["q_ps"], 1)

            def scores(t, par, h, first=False):
                if h == 0:
                    pe.wait_ge(s["q_nope_sb"], t + 1)
                    pe.wait_ge(s["q_rope_sb"], t + 1)
                if not first:
                    pe.wait_ge(s["exp_done"], t * A_HEADS + h)
                half = slice(ROPE_D * (h % 2), ROPE_D * (h % 2) + ROPE_D)
                for c in range(4):
                    cols = slice(c * BANK, (c + 1) * BANK)
                    pe.matmul(SC[:, cols], qn[:, par, h, :], kT[:, h, cols], start=True, stop=False)
                    mm = pe.matmul(SC[:, cols], qr[half, par, h // 2, :], krT[half, cols], start=False, stop=True)
                mm.then_inc(s["sc_ps"], 1)

            def body(t, par, has_prev, has_next):
                for h in range(A_HEADS):
                    u = t * A_HEADS + h
                    if h < A_HEADS - 1:
                        scores(t, par, h + 1)
                    elif has_next:
                        scores(t + 1, 1 - par, 0)
                    pe.wait_ge(s["exp_done"], u + 1)

                    def turn(j):
                        for kt in range(4 * j, 4 * j + 4):
                            mm = pe.transpose(PT[j % 2][:, kt % 4 * P:(kt % 4 + 1) * P],
                                              probs[:, h % 2, kt * P:(kt + 1) * P], ident[:, :])
                        mm.then_inc(s["pt_ps"], 1)

                    def apply(j):
                        if j < 2:
                            pe.wait_ge(s["pt_act"], u * 2 + (j + 1))
                        else:
                            pe.wait_ge(s["pt_dve"], u * 2 + (j - 1))
                        if j == 0 and h == 0 and has_prev:
                            pe.wait_ge(s["o_done"], t)
                        for kt in range(4 * j, 4 * j + 4):
                            mm = pe.matmul(O[:, h * VD:(h + 1) * VD], probsT[:, j, kt % 4 * P:(kt % 4 + 1) * P],
                                           v[:, kt, h * VD:(h + 1) * VD], start=(kt == 0), stop=(kt == TILES - 1))
                        return mm

                    turn(0)
                    turn(1)
                    apply(0)
                    turn(2)
                    apply(1)
                    turn(3)
                    apply(2)
                    mm = apply(3)
                    if h == A_HEADS - 1:
                        mm.then_inc(s["o_ps"], 1)
                    if h == 0 and has_next:
                        q_nope(t + 1)
                    if h == 1 and has_next:
                        q_rope(t + 1)

            pe.wait_ge(s["v_sb"], TILES)
            pe.wait_ge(s["kT_sb"], A_HEADS * QUADS)
            pe.wait_ge(s["cos_ready"], 1)
            q_nope(0)
            q_rope(0)
            scores(0, 0, 0, True)
            body(0, 0, False, True)
            body(1, 1, True, True)
            with pe.Fori(1, TILES // 2 - 1) as i:
                for w in range(2):
                    body(i * 2 + w, w, True, True)
            body(TILES - 2, 0, True, True)
            body(TILES - 1, 1, True, False)


GS, GC, NS = 32, 16, 64
QS = GS // 2
DQ = 2 * QS
T = 8
CHUNKS = SEQ // T
CT = CHUNKS // P
SLOTS = T + 1
SCAN_LINKS = 3
SCAN_UNROLL = 8


LN2_HI = 0.693145751953125
LN2_LO = math.log(2.0) - LN2_HI


def exact_exp(dve, ch, x, r, t, e):
    one = float(1 << 23)
    ch.link(dve.tensor_scalar(x, x, -110.0, 100.0, ALU.max, ALU.min))
    ch.link(dve.tensor_scalar(t, x, 1.0 / math.log(2.0), ROUND, ALU.mult, ALU.add))
    ch.link(dve.tensor_scalar(t, t, ROUND, None, ALU.subtract))
    ch.link(dve.scalar_tensor_tensor(r, t, -LN2_HI, x, ALU.mult, ALU.add))
    ch.link(dve.scalar_tensor_tensor(r, t, -LN2_LO, r, ALU.mult, ALU.add))
    ch.link(dve.tensor_scalar(x, r, 1.0 / math.factorial(7), None, ALU.mult))
    for k in range(6, 0, -1):
        ch.link(dve.scalar_tensor_tensor(x, x, 1.0 / math.factorial(k), r, ALU.add, ALU.mult))
    ch.link(dve.tensor_scalar(x, x, 1.0, None, ALU.add))
    ch.link(dve.tensor_scalar(e, t, -126.0, 127.0, ALU.max, ALU.min))
    ch.link(dve.tensor_tensor(t, t, e, ALU.subtract))
    for part in (e, t):
        ch.link(dve.tensor_scalar(part.bitcast(I32), part, one, 127.0 * one, ALU.mult, ALU.add))
        ch.link(dve.tensor_tensor(x, x, part, ALU.mult))


def s5_phase(nc, I, S):
    with ExitStack() as ctx:
        sb = lambda name, shape, dt=F32: ctx.enter_context(nc.sbuf_tensor(name, shape, dt))
        sem = lambda name: ctx.enter_context(nc.semaphore(name))

        region_a = sb("region_a", [P, DQ * 2 * P])
        region_b = sb("region_b", [P, DQ * 2 * P])
        X = sb("X", [P, CHUNKS + 1, 2, DQ])
        U = sb("U", [P, GS, CHUNKS])
        G = sb("G", [P, DQ, 2, SLOTS * GC])
        x_flat = X[:, :, :, :].rearrange("p c r q -> p (c r q)")
        u_rows = x_flat[:, 0:CT * T * SSM_W].rearrange("p (a s d) -> p a s d", a=CT, s=T)
        free = CT * T * SSM_W
        tmp_a = [x_flat[:, free + n * 2048:free + (n + 1) * 2048].rearrange("p (q s h) -> p q s h", q=QS, s=T) for n in range(2)]
        free += 2 * 2048
        part_g = QS // 4
        g_size = part_g * SLOTS * GC
        tmp_g = [x_flat[:, free + n * g_size:free + (n + 1) * g_size].rearrange("p (q s h) -> p q s h", q=part_g, s=SLOTS)
                 for n in range(2)]
        free += 2 * g_size
        b_raw, C = [x_flat[:, free + n * 2 * DQ * GC:free + (n + 1) * 2 * DQ * GC].rearrange("p (r q h) -> p r q h", r=2, q=DQ)
                    for n in range(2)]
        A1 = region_a[:, :].rearrange("p (q r m) -> p q r m", q=DQ, r=2)
        toep = region_a[:, :].rearrange("p (d g m) -> p d g m", d=2, g=GS)
        A1T = region_b[:, :].rearrange("p (q r m) -> p q r m", q=DQ, r=2)
        c_nat = region_b[:, 0:16 * P].rearrange("p (n two m) -> p n two m", n=16, two=2)
        W = region_b[0:GC, :].rearrange("p (d g m) -> p d g m", d=2, g=GS)
        y_rows = region_b[:, :].rearrange("p (a s d) -> p a s d", a=CT, s=T)
        u_perm = region_a[:, T * SSM_W:2 * T * SSM_W].rearrange("p (g s h) -> p g s h", g=GS, s=T)
        raw = region_b[0:DQ, 16 * P:19 * P].rearrange("p (n m) -> p n m", n=3)
        logdt = sb("logdt", [DQ, 2])
        par_ = sb("par", [P, 3, DQ])
        small = [sb(n, [P, DQ]) for n in ("lre", "dt", "mag", "ang5", "turns5", "sin5", "cos5", "den", "num", "t5")]
        lre, dt, mag, ang, turns, sin, cos, den, num, t5 = [x[:, :] for x in small]
        fac = sb("fac", [P, 2, DQ])
        pw = sb("pw", [P, SLOTS, 2, DQ])
        pw_t = [region_a[:, n * 8 * DQ:(n + 1) * 8 * DQ].rearrange("p (n r q) -> p n r q", n=4, r=2) for n in range(2)]
        b_bar = sb("b_bar", [P, 2, DQ, GC])
        b_t = [region_a[:, (1 + n) * DQ * GC:(2 + n) * DQ * GC].rearrange("p (q h) -> p q h", q=DQ) for n in range(2)]
        skip = sb("skip", [P, GS])
        ident = sb("ident5", [P, P])
        lr2 = sb("lr2", [P, 2, DQ])
        li2 = sb("li2", [P, 2, DQ])
        st = [sb(f"st{n}", [P, 2, DQ]) for n in range(2)]
        skip_m = toep[:, 1, 0:8, :]

        PS = [ctx.enter_context(nc.psum_tensor(f"PS{n}", [P, BANK], F32)) for n in range(8)]

        names = """params b_in c_in u_in skip_in ident_ready raw_ps raw_sb ang_ready sines c_ps C_ready u_ps
            u_sb u_by_group powers_ready b_ready G_ready A1_ready a_ps a_sb s_ps s_act s_dve scan_done w_ps w_sb toep_zero toep_in M_ready
            y_ps y_act y_dve y_stored dve_chain pool_chain raw_ready""".split()
        s = {n: sem("s_" + n) for n in names}
        ctx.enter_context(nc.allow_non_contiguous_dma(reason="small parameter tables"))
        ctx.callback(clear_semaphores, nc, s)
        block = ctx.enter_context(nc.Block())

        def states_in(eng, q):
            src = PS[q % 4][:, :].rearrange("p (r c) -> p r c", r=2)
            dst = X[:, 1:CHUNKS + 1, :, q] if q < QS else X[:, 0:CHUNKS, :, q]
            dst = dst.rearrange("p c r -> p r c")
            if q % 2 == 0:
                return eng.activation(dst, src, ACT.Copy)
            return eng.tensor_copy(dst, src)

        def outputs(eng, a, b, g2):
            bank = PS[2 * ((4 * a + b) % 2) + g2 + 2]
            src = bank[:, :].rearrange("c (j s h) -> c j s h", j=4, s=T)
            dst = y_rows[:, a, :, :].rearrange("c s (b j g h) -> c b g j s h", b=4, j=4, g=2)[:, b, g2]
            if g2 == 0:
                return eng.activation(dst, src, ACT.Copy)
            return eng.tensor_copy(dst, src)

        @block.sync
        def _(sp):
            for n, name in enumerate(("s5_lam_re_2", "s5_lam_im_2")):
                sp.dma_start(raw[:, n, :], I[name][0].rearrange("d (q g) p -> (d q) (g p)", g=2)).then_inc(s["params"], 16)
            sp.dma_start(logdt[:, :], I["s5_log_dt_2"][0].rearrange("d (q g) -> (d q) g", g=2)).then_inc(s["params"], 16)
            for r, name in enumerate(("s5_c_re_2", "s5_c_im_2")):
                for d in range(2):
                    src = I[name][0, d].rearrange("g h p -> (g h) p").rearrange("(b r) p -> r b p", r=P)
                    n = (r * 2 + d) * 4
                    for dup in range(2):
                        sp.dma_start(c_nat[:, n:n + 4, dup, :], src).then_inc(s["c_in"], 16)
            for r, name in enumerate(("s5_b_re_2", "s5_b_im_2")):
                for d in range(2):
                    src = I[name][0, d].rearrange("(q g) p h -> q (g p) h", g=2).rearrange("q r h -> r q h")
                    sp.dma_start(b_raw[:, r, d * QS:(d + 1) * QS, :], src).then_inc(s["b_in"], 16)
            u_t = S["z"].rearrange("(a c s) d -> a c s d", a=CT, s=T)
            for a in range(CT):
                sp.dma_start(u_rows[:, a, :, :], u_t[a, :, :, Z_U:Z_GS]).then_inc(s["u_in"], 16)
            for k in range(T):
                src = I["s5_d_2"][0].rearrange("(g h) -> h g", h=GC)
                sp.dma_start(skip[k * GC:(k + 1) * GC, :], src).then_inc(s["skip_in"], 16)
            sp.wait_ge(s["w_sb"], 16)
            sp.wait_ge(s["toep_zero"], 1)
            for k in range(T):
                rows = slice(k * GC, (k + 1) * GC)
                sp.dma_start(toep[rows, 0, :, k * GC:], W[:, 0, :, 0:(T - k) * GC]).then_inc(s["toep_in"], 16)
                sp.dma_start(toep[rows, 1, :, 0:(k + 1) * GC], W[:, 1, :, (T - 1 - k) * GC:]).then_inc(s["toep_in"], 16)
            y_t = S["ssm"].rearrange("(a c s) d -> a c s d", a=CT, s=T)
            for a in range(CT):
                sp.wait_ge(s["y_act"], 4 * (a + 1))
                sp.wait_ge(s["y_dve"], 4 * (a + 1))
                sp.dma_start(y_t[a], y_rows[:, a, :, :]).then_inc(s["y_stored"], 16)
            sp.wait_ge(s["y_stored"], 16 * CT)

        @block.gpsimd
        def _(pool):
            ch = Chain(pool, s["pool_chain"])
            make_identity(pool, ch, ident[:, :], s["ident_ready"])
            pool.wait_ge(s["powers_ready"], 1)
            pool.wait_ge(s["C_ready"], 1)
            for d in range(2):
                for part in range(4):
                    qs = slice(d * QS + part * part_g, d * QS + (part + 1) * part_g)
                    shape = [P, part_g, SLOTS, GC]
                    order = slice(None, None, -1 if d else 1)
                    p = [pw[:, order, r, qs].rearrange("p s q -> p q s").unsqueeze(3).to_broadcast(shape) for r in range(2)]
                    c = [C[:, r, qs, :].unsqueeze(2).to_broadcast(shape) for r in range(2)]
                    out = [G[:, qs, r, :].rearrange("p q (s h) -> p q s h", h=GC) for r in range(2)]
                    pool.tensor_tensor(tmp_g[0], c[0], p[0], ALU.mult)
                    ch.link(pool.tensor_tensor(tmp_g[1], c[1], p[1], ALU.mult))
                    ch.link(pool.tensor_tensor(out[0], tmp_g[0], tmp_g[1], ALU.subtract))
                    pool.tensor_tensor(tmp_g[0], c[0], p[1], ALU.mult)
                    ch.link(pool.tensor_tensor(tmp_g[1], c[1], p[0], ALU.mult))
                    ch.link(pool.tensor_tensor(tmp_g[0], tmp_g[0], tmp_g[1], ALU.add))
                    ch.link(pool.tensor_scalar(out[1], tmp_g[0], -1.0, None, ALU.mult))
            pool.sem_inc(s["G_ready"], 1)
            pool.wait_ge(s["a_ps"], 16)
            ch.link(pool.memset(region_a[:, :], 0.0))
            pool.sem_inc(s["toep_zero"], 1)
            pool.wait_ge(s["skip_in"], 16 * T)
            pool.wait_ge(s["toep_in"], 16 * 2 * T)
            ch.link(pool.tensor_tensor(toep[:, 0, :, :], toep[:, 0, :, :], toep[:, 1, :, :], ALU.add))
            for b in range(GS // 8):
                gs = slice(8 * b, 8 * b + 8)
                ch.link(pool.tensor_tensor(skip_m, ident[:, :].unsqueeze(1).to_broadcast([P, 8, P]),
                                           skip[:, gs].unsqueeze(2).to_broadcast([P, 8, P]), ALU.mult))
                ch.link(pool.tensor_tensor(toep[:, 0, gs, :], toep[:, 0, gs, :], skip_m, ALU.add))
            pool.sem_inc(s["M_ready"], 1)

        @block.scalar
        def _(act):
            act.wait_ge(s["raw_ps"], 1)
            act.activation(par_[:, :, :], PS[0][:, 0:3 * DQ], ACT.Copy).then_inc(s["raw_sb"], 1)
            act.wait_ge(s["ang_ready"], 1)
            act.activation(sin, ang, ACT.Sin)
            act.activation(cos, ang, ACT.Sin, scale=0.5).then_inc(s["sines"], 1)
            for n in range(4):
                act.wait_ge(s["c_ps"], n + 1)
                r, d = n // 2, n % 2
                src = PS[1 + n][:, :].rearrange("p (q g h) -> p q g h", g=2, h=GC)
                for g2 in range(2):
                    hp = slice(NS * g2, NS * g2 + NS)
                    last = act.activation(C[hp, r, d * QS:(d + 1) * QS, :], src[hp, :, g2, :], ACT.Copy)
            last.then_inc(s["C_ready"], 1)
            for n in range(16):
                a, b = n // 8, n % 8
                if b == 0:
                    act.wait_ge(s["u_in"], 16 * CT)
                    if a > 0:
                        act.wait_ge(s["u_ps"], n)
                    act.activation(u_perm, u_rows[:, a, :, :].rearrange("p s (g h) -> p g s h", h=GC),
                                   ACT.Copy).then_inc(s["u_by_group"], 1)
                act.wait_ge(s["u_ps"], n + 1)
                act.activation(U[:, 4 * b:4 * b + 4, a * P:(a + 1) * P],
                               PS[5 + n % 3][:, :].rearrange("p (g c) -> p g c", g=4), ACT.Copy).then_inc(s["u_sb"], 1)
            for n in range(16):
                act.wait_ge(s["a_ps"], n + 1)
                act.activation(A1T[:, 2 * n:2 * n + 2, :, :], PS[1 + n % 4][:, :], ACT.Copy).then_inc(s["a_sb"], 1)
            act.wait_ge(s["G_ready"], 1)
            for q in range(0, DQ, 2):
                act.wait_ge(s["s_ps"], q + 1)
                states_in(act, q).then_inc(s["s_act"], 1)
            for n in range(16):
                act.wait_ge(s["w_ps"], n + 1)
                d, first = n // 8, n % 8 // 2 * 8 + n % 2
                act.activation(W[:, d, first:first + 7:2, :], PS[n % 2][0:GC, :].rearrange("p (g m) -> p g m", g=4),
                               ACT.Copy).then_inc(s["w_sb"], 1)
            for a in range(CT):
                for b in range(4):
                    act.wait_ge(s["y_ps"], 2 * (4 * a + b) + 1)
                    outputs(act, a, b, 0).then_inc(s["y_act"], 1)

        @block.vector
        def _(dve):
            ch = Chain(dve, s["dve_chain"])
            tt = lambda out, a, b, op: dve.tensor_tensor(out, a, b, op)

            dve.wait_ge(s["params"], 48)
            dve.tensor_copy(raw[:, 2, :].rearrange("q (g p) -> q g p", g=2),
                            logdt[:, :].unsqueeze(2).to_broadcast([DQ, 2, NS])).then_inc(s["raw_ready"], 1)
            im = par_[:, 1, :]
            dve.wait_ge(s["raw_sb"], 1)
            dve.tensor_scalar(lre, par_[:, 0, :], -1e-4, None, ALU.min)
            ch.link(dve.tensor_copy(dt, par_[:, 2, :]))
            exact_exp(dve, ch, dt, num, t5, den)
            tt(mag, lre, dt, ALU.mult)
            ch.link(tt(ang, im, dt, ALU.mult))
            reduce_angles(dve, ch, ang, turns)
            dve.sem_inc(s["ang_ready"], 1)
            exact_exp(dve, ch, mag, num, t5, den)
            tt(den, lre, lre, ALU.mult)
            ch.link(tt(t5, im, im, ALU.mult))
            ch.link(tt(den, den, t5, ALU.add))
            ch.link(dve.reciprocal(den, den))
            dve.wait_ge(s["sines"], 1)
            ch.link(tt(cos, cos, cos, ALU.mult))
            ch.link(dve.tensor_scalar(cos, cos, -2.0, 1.0, ALU.mult, ALU.add))
            dve.memset(pw[:, 0, 0, :], 1.0)
            dve.memset(pw[:, 0, 1, :], 0.0)
            tt(pw[:, 1, 0, :], mag, cos, ALU.mult)
            ch.link(tt(pw[:, 1, 1, :], mag, sin, ALU.mult))
            ch.link(dve.tensor_scalar(num, pw[:, 1, 0, :], -1.0, None, ALU.add))
            tt(fac[:, 0, :], num, lre, ALU.mult)
            ch.link(tt(t5, pw[:, 1, 1, :], im, ALU.mult))
            ch.link(tt(fac[:, 0, :], fac[:, 0, :], t5, ALU.add))
            tt(fac[:, 1, :], pw[:, 1, 1, :], lre, ALU.mult)
            ch.link(tt(t5, num, im, ALU.mult))
            ch.link(tt(fac[:, 1, :], fac[:, 1, :], t5, ALU.subtract))
            ch.link(tt(fac[:, :, :], fac[:, :, :], den.unsqueeze(1).to_broadcast([P, 2, DQ]), ALU.mult))
            for n in (1, 2, 4):
                shape = [P, n, 2, DQ]
                a = pw[:, 1:1 + n, :, :]
                by = [pw[:, n, r, :].unsqueeze(1).unsqueeze(1).to_broadcast(shape) for r in range(2)]
                tt(pw_t[0][:, 0:n, :, :], a, by[0], ALU.mult)
                ch.link(tt(pw_t[1][:, 0:n, :, :], a[:, :, ::-1, :], by[1], ALU.mult))
                out = pw[:, 1 + n:1 + 2 * n, :, :]
                tt(out[:, :, 0, :], pw_t[0][:, 0:n, 0, :], pw_t[1][:, 0:n, 0, :], ALU.subtract)
                ch.link(tt(out[:, :, 1, :], pw_t[0][:, 0:n, 1, :], pw_t[1][:, 0:n, 1, :], ALU.add))
            dve.sem_inc(s["powers_ready"], 1)
            for r in range(2):
                dve.tensor_copy(lr2[:, r, :], pw[:, T, 0, :])
            dve.tensor_copy(li2[:, 0, :], pw[:, T, 1, :])
            dve.tensor_scalar(li2[:, 1, :], pw[:, T, 1, :], -1.0, None, ALU.mult)
            dve.wait_ge(s["b_in"], 64)
            f = [fac[:, r, :].unsqueeze(2).to_broadcast([P, DQ, GC]) for r in range(2)]
            for r, op in ((0, ALU.subtract), (1, ALU.add)):
                tt(b_t[0][:, :, :], f[0], b_raw[:, r, :, :], ALU.mult)
                ch.link(tt(b_t[1][:, :, :], f[1], b_raw[:, 1 - r, :, :], ALU.mult))
                ch.link(tt(b_bar[:, r, :, :], b_t[0][:, :, :], b_t[1][:, :, :], op))
            dve.sem_inc(s["b_ready"], 1)
            shape = [P, QS, T, GC]
            for d in range(2):
                if d == 1:
                    dve.wait_ge(s["u_ps"], 16)
                qs = slice(d * QS, (d + 1) * QS)
                powers = pw[:, 0:T, :, qs] if d else pw[:, T - 1::-1, :, qs]
                p = [powers[:, :, r, :].rearrange("p s q -> p q s").unsqueeze(3).to_broadcast(shape) for r in range(2)]
                b = [b_bar[:, r, qs, :].unsqueeze(2).to_broadcast(shape) for r in range(2)]
                for r, op in ((0, ALU.subtract), (1, ALU.add)):
                    tt(tmp_a[0], b[r], p[0], ALU.mult)
                    ch.link(tt(tmp_a[1], b[1 - r], p[1], ALU.mult))
                    ch.link(tt(A1[:, qs, r, :].rearrange("p q (s h) -> p q s h", h=GC), tmp_a[0], tmp_a[1], op))
                dve.sem_inc(s["A1_ready"], 1)
            dve.wait_ge(s["G_ready"], 1)
            dve.memset(X[:, 0, :, 0:QS], 0.0)
            dve.memset(X[:, CHUNKS, :, QS:], 0.0)
            for q in range(1, DQ, 2):
                dve.wait_ge(s["s_ps"], q + 1)
                states_in(dve, q).then_inc(s["s_dve"], 1)
            dve.wait_ge(s["s_dve"], DQ // 2)
            dve.wait_ge(s["s_act"], DQ // 2)

            def step(j, c):
                fwd, bwd = slice(0, QS), slice(QS, DQ)
                at = lambda n, qs: X[:, bass.ds(n, 1), :, qs].squeeze(1)
                sides = ((fwd, j, j + 1), (bwd, c + 1, c))
                for qs, old, _ in sides:
                    tt(st[0][:, :, qs], at(old, qs), lr2[:, :, qs], ALU.mult)
                for qs, old, _ in sides:
                    last = tt(st[1][:, :, qs], at(old, qs), li2[:, :, qs], ALU.mult)
                ch.link(last)
                for qs, _, new in sides:
                    last = tt(st[0][:, :, qs], st[0][:, :, qs], at(new, qs), ALU.add)
                ch.link(last)
                for qs, _, new in sides:
                    last = tt(at(new, qs), st[0][:, :, qs], st[1][:, ::-1, qs], ALU.add)
                ch.link(last)

            base = ch.n
            with dve.Fori(0, CHUNKS // SCAN_UNROLL) as i:
                ch.start(i * (SCAN_UNROLL * SCAN_LINKS) + base)
                for w in range(SCAN_UNROLL):
                    step(i * SCAN_UNROLL + w, i * -SCAN_UNROLL + (CHUNKS - 1 - w))
                assert ch.n == SCAN_UNROLL * SCAN_LINKS
            dve.sem_inc(s["scan_done"], 1)
            for a in range(CT):
                for b in range(4):
                    dve.wait_ge(s["y_ps"], 2 * (4 * a + b) + 2)
                    outputs(dve, a, b, 1).then_inc(s["y_dve"], 1)

        @block.tensor
        def _(pe):
            pe.wait_ge(s["ident_ready"], 1)
            pe.wait_ge(s["raw_ready"], 1)
            for n in range(3):
                mm = pe.transpose(PS[0][:, n * DQ:(n + 1) * DQ], raw[:, n, :], ident[0:DQ, 0:DQ])
            mm.then_inc(s["raw_ps"], 1)
            pe.wait_ge(s["c_in"], 16 * 8)
            for n in range(16):
                mm = pe.transpose(PS[1 + n // 4][:, n % 4 * P:(n % 4 + 1) * P],
                                  c_nat[:, n, :, :].rearrange("p two m -> p (two m)"), ident[:, :])
                if n % 4 == 3:
                    mm.then_inc(s["c_ps"], 1)
            for n in range(16):
                a, b = n // 8, n % 8
                if n > 2:
                    pe.wait_ge(s["u_sb"], n - 2)
                pe.wait_ge(s["u_by_group"], a + 1)
                for g in range(4):
                    src = u_perm[:, 4 * b + g, :, :].rearrange("p s h -> p (s h)")
                    mm = pe.transpose(PS[5 + n % 3][:, g * P:(g + 1) * P], src, ident[:, :])
                mm.then_inc(s["u_ps"], 1)
            pe.wait_ge(s["C_ready"], 1)
            for n in range(16):
                pe.wait_ge(s["A1_ready"], n // 8 + 1)
                if n > 3:
                    pe.wait_ge(s["a_sb"], n - 3)
                for m in range(4):
                    mm = pe.transpose(PS[1 + n % 4][:, m * P:(m + 1) * P], A1[:, 2 * n + m // 2, m % 2, :], ident[:, :])
                mm.then_inc(s["a_ps"], 1)
            pe.wait_ge(s["a_sb"], 16)
            pe.wait_ge(s["u_sb"], 16)
            for q in range(DQ):
                if q > 3:
                    if q % 2 == 0:
                        pe.wait_ge(s["s_act"], q // 2 - 1)
                    else:
                        pe.wait_ge(s["s_dve"], q // 2 - 1)
                for g2 in range(2):
                    for r in range(2):
                        mm = pe.matmul(PS[q % 4][NS * g2:NS * g2 + NS, r * CHUNKS:(r + 1) * CHUNKS],
                                       A1T[:, q, r, NS * g2:NS * g2 + NS], U[:, 2 * (q % QS) + g2, :], start=True, stop=True)
                mm.then_inc(s["s_ps"], 1)
            pe.wait_ge(s["s_act"], DQ // 2)
            pe.wait_ge(s["s_dve"], DQ // 2)
            for n in range(16):
                d, g2 = n // 8, n % 2
                hp = slice(NS * g2, NS * g2 + NS)
                if n > 1:
                    pe.wait_ge(s["w_sb"], n - 1)
                for g in range(4):
                    q = d * QS + n % 8 // 2 * 4 + g
                    for r in range(2):
                        mm = pe.matmul(PS[n % 2][0:GC, g * P:(g + 1) * P], b_bar[hp, r, q, :],
                                       G[hp, q, r, d * GC:(d + T) * GC], start=(r == 0), stop=(r == 1))
                mm.then_inc(s["w_ps"], 1)
            pe.wait_ge(s["M_ready"], 1)
            pe.wait_ge(s["scan_done"], 1)
            for a in range(CT):
                for b in range(4):
                    n = 4 * a + b
                    if n > 1:
                        pe.wait_ge(s["y_act"], n - 1)
                        pe.wait_ge(s["y_dve"], n - 1)
                    mms = [None, None]
                    for j in range(4):
                        for g2 in range(2):
                            g = 8 * b + 2 * j + g2
                            hp = slice(NS * g2, NS * g2 + NS)
                            out = PS[2 * (n % 2) + g2 + 2][:, j * P:(j + 1) * P]
                            pe.matmul(out, U[:, g, a * P:(a + 1) * P], toep[:, 0, g, :], start=True, stop=False)
                            for d in range(2):
                                q = d * QS + g // 2
                                steps = slice(a * P + d, a * P + d + P)
                                for r in range(2):
                                    mms[g2] = pe.matmul(out, X[hp, steps, r, q], G[hp, q, r, (1 - d) * GC:(1 - d + T) * GC],
                                                        start=False, stop=(d == 1 and r == 1))
                    mms[0].then_inc(s["y_ps"], 1)
                    mms[1].then_inc(s["y_ps"], 1)


GELU_A, GELU_S = 0.044715, math.sqrt(2.0 / math.pi)


def output_phase(nc, I, S):
    with ExitStack() as ctx:
        sb = lambda name, shape, dt=F32: ctx.enter_context(nc.sbuf_tensor(name, shape, dt))
        pb = lambda name, w: ctx.enter_context(nc.psum_tensor(name, [P, w], F32))
        sem = lambda name: ctx.enter_context(nc.semaphore(name))

        KS = SSM_W // P
        w_glu = sb("w_glu", [P, KS, SSM_W])
        w_out = sb("w_out6", [P, KD, D])
        gain_out = sb("gain_out6", [P, KD])
        gain_post = sb("gain_post", [P, D])
        b_glu = sb("b_glu", [P, SSM_W])
        ident = sb("ident6", [P, P])
        y_in = sb("y_in", [P, 2, SSM_W])
        g_in = sb("g_in", [P, 2, 2, SSM_W])
        a_in = sb("a_in", [P, 2, ATTN_W])
        x2 = sb("x2_6", [P, 2, D])
        poly = sb("poly", [P, SSM_W])
        tanh_y = sb("tanh_y", [P, SSM_W])
        gelu = sb("gelu", [P, SSM_W])
        geluT = sb("geluT", [P, KS, P])
        pre = sb("pre6", [P, SSM_W])
        tanh_p = sb("tanh_p", [P, SSM_W])
        ssm = sb("ssm6", [P, SSM_W])
        tanh_g = sb("tanh_g6", [P, 2, SSM_W])
        silu = sb("silu", [P, 2, 2, SSM_W])
        sq_a, sq_s, sq_o = (sb(n, [P, w], mybir.dt.bfloat16) for n, w in
                            (("sq_a", ATTN_W), ("sq_s", SSM_W), ("sq_o", D)))
        ss = sb("ss6", [P, 2, 2])
        rstd = sb("rstd6", [P, 2])
        nt = sb("nt6", [P, 2])
        ss_o, rstd_o, nt_o = (sb(n, [P, 1]) for n in ("ss_o", "rstd_o", "nt_o"))
        cat = sb("cat", [P, 2, SSM_W])
        catT = sb("catT6", [P, KD, P])
        o_n = sb("o_n", [P, D])
        out = sb("out_sb", [P, 2, D])

        TG = pb("TG", BANK)
        GL = pb("GL", BANK)
        TC = pb("TC", 2 * BANK)
        OUT = [pb("OUT0", 2 * BANK), pb("OUT1", 2 * BANK)]

        names = """gains weights ident_ready scaled in_loaded x_loaded poly_ready tanh_y_ready gelu_ready gT_ps gT_sb gl_ps
            pre_ready tanh_p_ready ssm_ready sumsq sumsq_a tanh_g_ready silu_ready cat_ready cT_ps cT_sb o_ps sumsq_o out_ready
            out_seen out_stored dve_chain pool_chain""".split()
        s = {n: sem("o_" + n) for n in names}
        ctx.enter_context(nc.allow_non_contiguous_dma(reason="gains, a word per partition"))
        block = ctx.enter_context(nc.Block())

        tiles = lambda ap: ap.rearrange("(t p) d -> t p d", p=P)
        z_t, a_t, y_t, x_t, out_t = tiles(S["z"]), tiles(S["attn"]), tiles(S["ssm"]), tiles(S["x2"]), tiles(S["out"])
        per_in = 64

        @block.sync
        def _(sp):
            def load(t, par):
                tile = bass.ds(t, 1)
                sp.dma_start(y_in[:, par, :], y_t[tile].squeeze(0)).then_inc(s["in_loaded"], 16)
                sp.dma_start(a_in[:, par, :], a_t[tile].squeeze(0)).then_inc(s["in_loaded"], 16)
                sp.dma_start(g_in[:, par, 0, :], z_t[tile, :, Z_GA:Z_U].squeeze(0)).then_inc(s["in_loaded"], 16)
                sp.dma_start(g_in[:, par, 1, :], z_t[tile, :, Z_GS:Z_COLS].squeeze(0)).then_inc(s["in_loaded"], 16)

            def load_x(t, par):
                sp.dma_start(x2[:, par, :], x_t[bass.ds(t, 1)].squeeze(0)).then_inc(s["x_loaded"], 16)

            def store(t, par):
                sp.wait_ge(s["out_ready"], t + 1)
                sp.sem_inc(s["out_seen"], 1)
                if not is_step(t, 0):
                    sp.wait_ge(s["out_stored"], t * 16)
                sp.dma_start(out_t[bass.ds(t, 1)].squeeze(0), out[:, par, :]).then_inc(s["out_stored"], 16)

            def body(t, par):
                sp.wait_ge(s["in_loaded"], t * per_in + 2 * per_in)
                sp.sem_inc(s["out_seen"], 1)
                sp.wait_ge(s["cat_ready"], t + 1)
                load(t + 2, par)
                if not is_step(t, 0):
                    store(t - 1, 1 - par)
                    sp.wait_ge(s["x_loaded"], t * 16 + 16)
                    load_x(t + 1, 1 - par)

            load(0, 0)
            load_x(0, 0)
            sp.dma_start(b_glu[:, :], I["b_glu_2"][0].partition_broadcast(P)).then_inc(s["gains"], 16)
            sp.dma_start(gain_post[:, :], I["post_norm_g_2"][0].partition_broadcast(P)).then_inc(s["gains"], 16)
            sp.dma_start(gain_out[:, 0:4], I["attn_out_g_2"][0].rearrange("(k p) -> p k", p=P)).then_inc(s["gains"], 16)
            sp.dma_start(gain_out[:, 4:8], I["ssm_out_g_2"][0].rearrange("(k p) -> p k", p=P)).then_inc(s["gains"], 16)
            for k in range(KS):
                sp.dma_start(w_glu[:, k, :], I["w_glu_2"][0, k * P:(k + 1) * P, :]).then_inc(s["weights"], 16)
            for k in range(KD):
                sp.dma_start(w_out[:, k, :], I["w_out_2"][0, k * P:(k + 1) * P, :]).then_inc(s["weights"], 16)
            sp.wait_ge(s["in_loaded"], per_in)
            load(1, 1)
            sp.wait_ge(s["x_loaded"], 16)
            load_x(1, 1)
            for t in (0, 1):
                body(t, t)
            with sp.Fori(1, TILES // 2 - 1) as i:
                for u in range(2):
                    body(i * 2 + u, u)
            store(TILES - 3, 1)
            sp.wait_ge(s["x_loaded"], 16 * (TILES - 1))
            load_x(TILES - 1, 1)
            store(TILES - 2, 0)
            store(TILES - 1, 1)
            sp.wait_ge(s["out_stored"], 16 * TILES)

        @block.gpsimd
        def _(pool):
            make_identity(pool, Chain(pool, s["pool_chain"]), ident[:, :], s["ident_ready"])

        @block.scalar
        def _(act):
            def ahead(t, par):
                act.wait_ge(s["poly_ready"], t + 1)
                act.activation(tanh_y[:, :], poly[:, :], ACT.Tanh, scale=GELU_S).then_inc(s["tanh_y_ready"], 1)
                act.wait_ge(s["in_loaded"], t * per_in + per_in)
                act.activation(sq_a[:, :], a_in[:, par, :], ACT.Square,
                               accum_out=ss[:, par, 0:1]).then_inc(s["sumsq_a"], 1)
                act.activation(tanh_g[:, :, :], g_in[:, par, :, :], ACT.Tanh, scale=0.5).then_inc(s["tanh_g_ready"], 1)

            def body(t, par, has_prev, has_this, has_next):
                if has_this:
                    act.wait_ge(s["gT_ps"], t + 1)
                    act.activation(geluT[:, :, :], TG[:, :], ACT.Copy, scale=0.5).then_inc(s["gT_sb"], 1)
                if has_prev:
                    act.wait_ge(s["cT_ps"], t)
                    act.activation(catT[:, 0:4, :], TC[:, 0:BANK], ACT.Copy, scale=0.5)
                    act.activation(catT[:, 4:8, :], TC[:, BANK:], ACT.Copy, scale=0.125).then_inc(s["cT_sb"], 1)
                if has_this:
                    act.wait_ge(s["pre_ready"], t + 1)
                    act.activation(tanh_p[:, :], pre[:, :], ACT.Tanh, scale=0.5).then_inc(s["tanh_p_ready"], 1)
                if has_next:
                    ahead(t + 1, 1 - par)
                if has_this:
                    act.wait_ge(s["ssm_ready"], t + 1)
                    act.wait_ge(s["sumsq_a"], t + 1)
                    act.activation(sq_s[:, :], ssm[:, :], ACT.Square,
                                   accum_out=ss[:, par, 1:2]).then_inc(s["sumsq"], 1)
                if has_prev:
                    act.wait_ge(s["o_ps"], t)
                    if is_step(t, TILES):
                        act.wait_ge(s["out_ready"], t - 1)
                    act.activation(sq_o[:, :], OUT[1 - par][:, :], ACT.Square, accum_out=ss_o[:, :]).then_inc(s["sumsq_o"], 1)

            ahead(0, 0)
            body(0, 0, False, True, True)
            with act.Fori(0, TILES // 2 - 1) as i:
                body(i * 2 + 1, 1, True, True, True)
                body(i * 2 + 2, 0, True, True, True)
            body(TILES - 1, 1, True, True, False)
            body(TILES, 0, True, False, False)

        @block.vector
        def _(dve):
            ch = Chain(dve, s["dve_chain"])

            def gelu_in(t, par):
                dve.wait_ge(s["in_loaded"], t * per_in + per_in)
                y = y_in[:, par, :]
                ch.link(dve.tensor_tensor(poly[:, :], y, y, ALU.mult))
                ch.link(dve.tensor_scalar(poly[:, :], poly[:, :], GELU_A, 1.0, ALU.mult, ALU.add))
                dve.tensor_tensor(poly[:, :], poly[:, :], y, ALU.mult).then_inc(s["poly_ready"], 1)

            def gelu_out(t, par):
                if not is_step(t, 0):
                    dve.wait_ge(s["ssm_ready"], t)
                dve.wait_ge(s["tanh_y_ready"], t + 1)
                dve.scalar_tensor_tensor(gelu[:, :], tanh_y[:, :], 1.0, y_in[:, par, :], ALU.add, ALU.mult).then_inc(s["gelu_ready"], 1)

            def gates(t, par):
                dve.wait_ge(s["tanh_g_ready"], t + 1)
                dve.scalar_tensor_tensor(silu[:, par, :, :], tanh_g[:, :, :], 1.0, g_in[:, par, :, :],
                                         ALU.add, ALU.mult).then_inc(s["silu_ready"], 1)

            def bias(t):
                dve.wait_ge(s["gl_ps"], t + 1)
                dve.tensor_tensor(pre[:, :], GL[:, :], b_glu[:, :], ALU.add).then_inc(s["pre_ready"], 1)

            def unit(t):
                dve.wait_ge(s["tanh_p_ready"], t + 1)
                dve.scalar_tensor_tensor(ssm[:, :], tanh_p[:, :], 1.0, gelu[:, :], ALU.add, ALU.mult).then_inc(s["ssm_ready"], 1)

            def join(t, par, has_prev):
                dve.wait_ge(s["sumsq"], t + 1)
                dve.tensor_scalar(ss[:, par, 0:1], ss[:, par, 0:1], 1.0 / ATTN_W, EPS, ALU.mult, ALU.add)
                ch.link(dve.tensor_scalar(ss[:, par, 1:2], ss[:, par, 1:2], 1.0 / (16 * SSM_W), EPS, ALU.mult, ALU.add))
                rsqrt(dve, ch, rstd[:, :], ss[:, par, :], nt[:, :])
                dve.wait_ge(s["silu_ready"], t + 1)
                if has_prev:
                    dve.wait_ge(s["cT_ps"], t)
                dve.scalar_tensor_tensor(cat[:, 0, :], a_in[:, par, :], rstd[:, 0:1], silu[:, par, 0, :], ALU.mult, ALU.mult)
                dve.scalar_tensor_tensor(cat[:, 1, :], ssm[:, :], rstd[:, 1:2], silu[:, par, 1, :],
                                         ALU.mult, ALU.mult).then_inc(s["cat_ready"], 1)

            def last_norm(t, par, reused):
                dve.wait_ge(s["sumsq_o"], t + 1)
                inv_rms(dve, ch, rstd_o[:, :], ss_o[:, :], nt_o[:, :], D, EPS)
                ch.link(dve.scalar_tensor_tensor(o_n[:, :], OUT[par][:, :], rstd_o[:, :], gain_post[:, :], ALU.mult, ALU.mult))
                dve.wait_ge(s["x_loaded"], t * 16 + 16)
                if reused:
                    dve.wait_ge(s["out_stored"], t * 16 - 16)
                dve.tensor_tensor(out[:, par, :], o_n[:, :], x2[:, par, :], ALU.add).then_inc(s["out_ready"], 1)

            def body(t, par, has_prev, has_next, reused):
                bias(t)
                if has_next:
                    gelu_in(t + 1, 1 - par)
                unit(t)
                if has_next:
                    gelu_out(t + 1, 1 - par)
                    gates(t + 1, 1 - par)
                join(t, par, has_prev)
                if has_prev:
                    last_norm(t - 1, 1 - par, reused)

            gelu_in(0, 0)
            gelu_out(0, 0)
            gates(0, 0)
            dve.wait_ge(s["gains"], 64)
            dve.wait_ge(s["weights"], 16 * (KS + KD))
            for k in range(KD):
                last = dve.tensor_scalar(w_out[:, k, :], w_out[:, k, :], gain_out[:, k:k + 1], None, ALU.mult)
            last.then_inc(s["scaled"], 1)
            body(0, 0, False, True, False)
            body(1, 1, True, True, False)
            body(2, 0, True, True, False)
            base = ch.n
            body(3, 1, True, True, True)
            per = ch.n - base
            body(4, 0, True, True, True)
            with dve.Fori(2, TILES // 2 - 1) as i:
                ch.start(i * (2 * per) + (base - 2 * per))
                body(i * 2 + 1, 1, True, True, True)
                body(i * 2 + 2, 0, True, True, True)
                assert ch.n == 2 * per, ch.n
            ch.start(base + (TILES - 4) * per)
            body(TILES - 1, 1, True, False, True)
            last_norm(TILES - 1, 1, True)

        @block.tensor
        def _(pe):
            pe.wait_ge(s["ident_ready"], 1)

            def body(t, par, has_prev, has_this, reused):
                if has_this:
                    pe.wait_ge(s["gelu_ready"], t + 1)
                    for k in range(KS):
                        mm = pe.transpose(TG[:, k * P:(k + 1) * P], gelu[:, k * P:(k + 1) * P], ident[:, :])
                    mm.then_inc(s["gT_ps"], 1)
                if has_prev:
                    pe.wait_ge(s["cat_ready"], t)
                    for k in range(KD):
                        mm = pe.transpose(TC[:, k * P:(k + 1) * P], cat[:, k // KS, k % KS * P:(k % KS + 1) * P], ident[:, :])
                    mm.then_inc(s["cT_ps"], 1)
                if has_this:
                    if is_step(t, 0):
                        pe.wait_ge(s["weights"], 16 * (KS + KD))
                    pe.wait_ge(s["gT_sb"], t + 1)
                    if has_prev:
                        pe.wait_ge(s["pre_ready"], t)
                    for k in range(KS):
                        mm = pe.matmul(GL[:, :], geluT[:, k, :], w_glu[:, k, :], start=(k == 0), stop=(k == KS - 1))
                    mm.then_inc(s["gl_ps"], 1)
                if has_prev:
                    if is_step(t, 1):
                        pe.wait_ge(s["scaled"], 1)
                    pe.wait_ge(s["cT_sb"], t)
                    if reused:
                        pe.wait_ge(s["out_ready"], t - 2)
                    for n in range(2):
                        for k in range(KD):
                            mm = pe.matmul(OUT[1 - par][:, n * BANK:(n + 1) * BANK], catT[:, k, :],
                                           w_out[:, k, n * BANK:(n + 1) * BANK], start=(k == 0), stop=(k == KD - 1))
                    mm.then_inc(s["o_ps"], 1)

            body(0, 0, False, True, False)
            body(1, 1, True, True, False)
            body(2, 0, True, True, False)
            with pe.Fori(1, TILES // 2 - 1) as i:
                body(i * 2 + 1, 1, True, True, True)
                body(i * 2 + 2, 0, True, True, True)
            body(TILES - 1, 1, True, True, True)
            body(TILES, 0, True, False, True)


def two_blocks(nc, I, out):
    with ExitStack() as ctx:
        sb = lambda name, shape, dt: ctx.enter_context(nc.sbuf_tensor(name, shape, dt))
        dram = lambda name, shape, dt=F32: nc.dram_tensor(name, shape, dt, kind="Internal").ap()
        S = {
            "keep": ctx,
            "pos": sb("pos", [P, TILES * TOPK], I32),
            "gates": sb("gates", [P, TILES * TOPK], F32),
            "starts": sb("starts", [P, E + 1], I32),
            "n_tiles": sb("n_tiles", [P, E], I32),
            "h1": dram("h1", [SEQ, D]),
            "hn": dram("hn", [SEQ, D]),
            "tok_list": dram("tok_list", [E * CAP, 1], I32),
            "y": dram("expert_rows", [MAX_TILES * P, D]),
            "x2": dram("x2", [SEQ, D]),
            "z": dram("z", [SEQ, Z_COLS]),
            "attn": dram("attn", [SEQ, ATTN_W]),
            "ssm": dram("ssm", [SEQ, SSM_W]),
            "out": out[0],
        }
        mixer_phase(nc, I, S)
        expert_phase(nc, I, S)
        combine_phase(nc, I, S)
        attention_phase(nc, I, S)
        s5_phase(nc, I, S)
        output_phase(nc, I, S)


def kernel(**inputs):
    import numpy as _np
    import concourse.bacc as _bacc
    from concourse import mybir as _mybir
    from concourse.bass_utils import run_bass_kernel_spmd as _run

    nc = _bacc.Bacc("TRN2", target_bir_lowering=False, num_devices=1)
    arrays, args = {}, {}
    for name, value in inputs.items():
        a = _np.ascontiguousarray(value)
        arrays[f"in_{name}_dram"] = a
        args[name] = nc.dram_tensor(f"in_{name}_dram", a.shape, _mybir.dt.from_np(a.dtype), kind="ExternalInput").ap()
    out = nc.dram_tensor("out_dram", (1, SEQ, D), _mybir.dt.float32, kind="ExternalOutput").ap()
    two_blocks(nc, args, out)
    r = _run(nc, [arrays], core_ids=[0])
    return r.results[0]["out_dram"]
```

```python
from contextlib import ExitStack
import math

import numpy as np
import concourse.bass as bass
from concourse import mybir

F32 = mybir.dt.float32
I32 = mybir.dt.int32
U32 = mybir.dt.uint32
ALU = mybir.AluOpType
ACT = mybir.ActivationFunctionType
AX = mybir.AxisListType.X

P = 128
SEQ, D = 2048, 1024
TILES = SEQ // P
KD = D // P
BANK = 512

D_RET, HEADS, HD = 512, 8, 64
PAIRS = HEADS // 2
WINDOWS = (2, 4, 8, 16)
GROUPS = len(WINDOWS)
PROJ = 4 * D_RET + 512
LOG_GAMMA = [math.log1p(-(2.0 ** (-5 - h))) for h in range(HEADS)]
NORM_EPS, GN_EPS = 1e-5, 1e-5
ROPE_HALF = 32
INV_FREQ = [float(np.float32(10000.0 ** (-j / ROPE_HALF))) for j in range(ROPE_HALF)]
TWO_PI_HI = 6.28125
TWO_PI_MID = float(np.float32(2 * math.pi - TWO_PI_HI))
TWO_PI_LO = 2 * math.pi - TWO_PI_HI - TWO_PI_MID
ROUND = 12582912.0
PI_IN = 3.1415925

E, TOPK, CAP = 32, 4, SEQ
FF = 1024
BODY_LINKS = 58


def place_of(h):
    return h % 2 * PAIRS + h // 2


class Chain:

    def __init__(self, eng, sem):
        self.eng, self.sem, self.base, self.n = eng, sem, 0, 0

    def start(self, base):
        self.base, self.n = base, 0

    def link(self, ins):
        self.n += 1
        ins.then_inc(self.sem, 1)
        self.eng.wait_ge(self.sem, self.base + self.n)


def clear_semaphores(nc, s):
    with nc.Block() as block:
        @block.sync
        def _(sp):
            for signal in s.values():
                sp.sem_clear(signal)


def rsqrt(dve, ch, y, x, t, done=None):
    ch.link(dve.tensor_scalar(t.bitcast(I32), x.bitcast(I32), 1, None, ALU.logical_shift_right))
    ch.link(dve.tensor_scalar(y.bitcast(I32), t.bitcast(I32), -1.0, 1597463007.0, ALU.mult, ALU.add))
    for step in range(3):
        ch.link(dve.tensor_tensor(t, y, y, ALU.mult))
        ch.link(dve.scalar_tensor_tensor(t, t, -0.5, x, ALU.mult, ALU.mult))
        last = dve.scalar_tensor_tensor(y, t, 1.5, y, ALU.add, ALU.mult)
        if step == 2 and done is not None:
            last.then_inc(done, 1)
        else:
            ch.link(last)


def reduce_angles(dve, ch, ang, turns):
    ch.link(dve.tensor_scalar(turns, ang, 1.0 / (2 * math.pi), ROUND, ALU.mult, ALU.add))
    ch.link(dve.tensor_scalar(turns, turns, ROUND, None, ALU.subtract))
    for part in (TWO_PI_HI, TWO_PI_MID, TWO_PI_LO):
        ch.link(dve.scalar_tensor_tensor(ang, turns, -part, ang, ALU.mult, ALU.add))
    ch.link(dve.tensor_scalar(ang, ang, PI_IN, -PI_IN, ALU.min, ALU.max))


def make_identity(pool, ch, ident, done):
    ch.link(pool.memset(ident, 0.0))
    pool.affine_select(out=ident, in_=ident, compare_op=ALU.not_equal, fill=1.0, base=0,
                       pattern=[[-1, P]], channel_multiplier=1).then_inc(done, 1)


def mixer_phase(nc, I, S):
    with ExitStack() as ctx:
        sb = lambda name, shape, dt=F32: ctx.enter_context(nc.sbuf_tensor(name, shape, dt))
        pb = lambda name, w: ctx.enter_context(nc.psum_tensor(name, [P, w], F32))
        sem = lambda name: ctx.enter_context(nc.semaphore(name))

        w_in = sb("w_in_sb", [P, KD, PROJ])
        w_out = sb("w_out_sb", [P, KD, D])
        w_pool = sb("w_pool_sb", [P, GROUPS, P])
        w_rt = sb("w_rt_sb", [P, KD, E])
        gain_mix = sb("gain_mix", [P, KD])
        gain_out = sb("gain_out", [P, KD])
        gain_moe = sb("gain_moe", [P, D])
        bias_rt = sb("bias_rt", [P, E])
        ident = sb("ident", [P, P])
        ones = sb("ones", [P, P])
        rel = sb("rel", [P, P])
        causal = sb("causal", [P, P])
        before = sb("before", [P, P])
        step1 = sb("step1", [P, P])
        back = sb("back", [P, 1])
        decay = sb("decay", [P, HEADS, P])
        xi = sb("xi", [P, PAIRS, P])
        zeta = sb("zeta", [P, HEADS])
        chunk_decay = sb("chunk_decay", [P, PAIRS])
        band = sb("band", [P, GROUPS, P])
        band0 = sb("band0", [P, GROUPS, P])
        band_prev = sb("band_prev", [P, GROUPS, P])
        pos_i = sb("pos_i", [P, TILES], I32)
        pos_f = sb("pos_f", [P, TILES])
        freq = sb("freq", [P, ROPE_HALF])
        sin = sb("sin", [P, TILES, ROPE_HALF])
        cos = sb("cos", [P, TILES, ROPE_HALF])
        iota_e = sb("iota_e", [P, E])
        first_slot = sb("first_slot", [P, E])
        tok_id = sb("tok_id", [P, TILES], I32)

        x_sb = sb("x_sb", [P, 2, D])
        xT = sb("xT", [P, KD, P])
        qk = sb("qk", [P, 2 * HEADS, 2, ROPE_HALF])
        vgu = sb("vgu", [P, 2, 3 * BANK])
        squares = sb("squares", [P, D], mybir.dt.bfloat16)
        ss1, ms1, rstd1, nt1 = (sb(n, [P, 1]) for n in ("ss1", "ms1", "rstd1", "nt1"))
        ss2 = sb("ss2", [P, 2])
        ms2, rstd2, nt2 = (sb(n, [P, 1]) for n in ("ms2", "rstd2", "nt2"))
        rot = sb("rot", [P, 2 * HEADS, 2, ROPE_HALF])
        rope_a = sb("rope_a", [P, 2 * HEADS, ROPE_HALF])
        rope_b = sb("rope_b", [P, 2 * HEADS, ROPE_HALF])
        kz = rope_b[:, :, :].rearrange("p (h two) f -> p h (two f)", two=2)
        turns = rope_a
        qT = sb("qT", [P, PAIRS, P])
        kT = sb("kT", [P, PAIRS, P])
        qxT = sb("qxT", [P, PAIRS, P])
        sT = sb("sT", [P, HEADS, P])
        inside, recip0 = sT[:, 0, :], sT[:, 1, :]
        ang = sT[:, 4:8, :].rearrange("p a (t f) -> p (a t) f", f=ROPE_HALF)
        state = sb("state", [P, PAIRS, 2, HD])
        pooledT = sb("pooledT", [P, GROUPS, P])
        catT = sb("catT", [P, KD, P])
        mean, var, gstd, gnt = (sb(n, [P, HEADS]) for n in ("mean", "var", "gstd", "gnt"))
        yc = sb("yc", [P, HEADS, HD])
        ysq = rope_a[:, :, :].rearrange("p (h two) f -> p h (two f)", two=2)
        tanh_g = sb("tanh_g", [P, D_RET])
        ret = yc
        hn_sb = sb("hn_sb", [P, D])
        hnT = xT
        zero_i = xT[:, 0:4, :].rearrange("p k c -> p (k c)").bitcast(I32)
        lg = sb("lg", [P, E])
        top8 = sb("top8", [P, 8])
        top4 = sb("top4", [P, TOPK])
        idx8 = sb("idx8", [P, 8], U32)
        idxf = sb("idxf", [P, TOPK])
        ntop = sb("ntop", [P, 1])
        ex = sb("ex", [P, TOPK])
        exsum = sb("exsum", [P, 1])
        exrec = sb("exrec", [P, 1])
        onehot = sb("onehot", [P, TOPK, E])
        mask = sb("mask", [P, E])
        cum = sb("cum", [P, E])
        slot = sb("slot", [P, E])
        hit = sb("hit", [P, TOPK, E])
        posf = sb("posf", [P, TOPK])
        pos_cur = sb("pos_cur", [P, TOPK], I32)
        tok_cur = sb("tok_cur", [P, 1], I32)
        cnt = sb("cnt", [P, E])
        cnt_i = sb("cnt_i", [P, E], I32)
        cnt_e = sb("cnt_e", [P, E])
        zero_e = sb("zero_e", [P, E])
        ends = sb("ends", [P, E])
        which = w_in[:, 0, 0:TILES * TOPK * E].rearrange("p (n e) -> p n e", e=E)
        posf_all = [w_in[:, 1, n * TILES * TOPK:(n + 1) * TILES * TOPK] for n in range(2)]

        TR = pb("TR", 2 * BANK)
        PJ = [pb("PJ0", BANK), pb("PJ1", BANK)]
        SC = pb("SC", 2 * BANK)
        KV = pb("KV", BANK)
        Y = pb("Y", BANK)

        names = [f"w_in_rows{k}" for k in range(KD)] + """loads weights w_in_scaled pool_chain dve_setup act_setup pool_setup tables_in sines
            x_loaded xT_ps xT_sb sumsq1 rstd1_ready proj_ps proj_sb rope_done qk_ps qkT_sb qx_sb sc_ps kv_ps
            sT_sb state_new y_ps pl_ps pl_sb mx_ps mx_sb tanh_done ret_done ret_ps ret_sb o_ps h_half h_done sumsq2
            hn_done hn_ps hn_sb_done lg_ps mask_done ex_done rank_ps pos_done h_stored hn_stored
            dve_chain list_zeroed slots_seen totals_ps ends_ready """.split()
        s = {n: sem(n) for n in names}
        ctx.enter_context(nc.allow_non_contiguous_dma(reason="small vectors, a word per partition"))
        ctx.callback(clear_semaphores, nc, dict(s))
        s.update({n: S["keep"].enter_context(nc.semaphore(n)) for n in ('scattered',)})
        block = ctx.enter_context(nc.Block())

        x_t = I["x"][0].rearrange("(t p) d -> t p d", p=P)
        h_t = S["h1"].rearrange("(t p) d -> t p d", p=P)
        hn_t = S["hn"].rearrange("(t p) d -> t p d", p=P)
        row = lambda ap: ap.partition_broadcast(P)

        @block.sync
        def _(sp):
            def load_x(t, par):
                sp.dma_start(x_sb[:, par, :], x_t[bass.ds(t, 1)].squeeze(0)).then_inc(s["x_loaded"], 16)

            sp.dma_start(gain_mix[:, :], I["norm_mix_w"][0].rearrange("(k p) -> p k", p=P)).then_inc(s["loads"], 16)
            sp.dma_start(gain_out[:, 0:4], I["ret_gn_w"][0].rearrange("(k p) -> p k", p=P)).then_inc(s["loads"], 16)
            sp.dma_start(gain_out[:, 4:8], I["pool_scale"][0].rearrange("(k p) -> p k", p=P)).then_inc(s["loads"], 16)
            sp.dma_start(gain_moe[:, :], row(I["norm_moe_w"][0])).then_inc(s["loads"], 16)
            sp.dma_start(bias_rt[:, :], row(I["router_b"][0])).then_inc(s["loads"], 16)
            sp.dma_start(pos_i[:, :], I["positions"][0].rearrange("(t p) -> p t", p=P)).then_inc(s["loads"], 16)
            load_x(0, 0)
            sp.wait_ge(s["pool_setup"], 1)
            sp.dma_start(S["tok_list"].rearrange("(p n) o -> p (n o)", p=P), zero_i[:, :]).then_inc(s["list_zeroed"], 16)
            for k in range(KD):
                sp.dma_start(w_in[:, k, :], I["w_in"][0, k * P:(k + 1) * P, :]).then_inc(s[f"w_in_rows{k}"], 16)
            sp.dma_start(w_rt[:, :, :], I["router_w"][0].rearrange("(k p) e -> p k e", p=P)).then_inc(s["weights"], 16)
            sp.dma_start(w_pool[:, :, :], I["pool_w"][0].rearrange("g c d -> c g d")).then_inc(s["weights"], 16)
            for k in range(KD):
                sp.dma_start(w_out[:, k, :], I["w_out"][0, k * P:(k + 1) * P, :]).then_inc(s["weights"], 16)
            sp.wait_ge(s["x_loaded"], 16)
            load_x(1, 1)

            def body(t, par, has_x):
                sp.wait_ge(s["h_done"], t + 1)
                sp.dma_start(h_t[bass.ds(t, 1)].squeeze(0), x_sb[:, par, :]).then_inc(s["h_stored"], 16)
                sp.wait_ge(s["hn_done"], t + 1)
                sp.dma_start(hn_t[bass.ds(t, 1)].squeeze(0), hn_sb[:, :]).then_inc(s["hn_stored"], 16)
                if has_x:
                    sp.wait_ge(s["h_stored"], t * 16 + 16)
                    load_x(t + 2, par)

            body(0, 0, True)
            with sp.Fori(0, 6) as i:
                for u in range(2):
                    body(i * 2 + (1 + u), (1 + u) % 2, True)
            for t in (13, 14, 15):
                body(t, t % 2, t + 2 < TILES)
            sp.wait_ge(s["h_stored"], 16 * TILES)
            sp.wait_ge(s["hn_stored"], 16 * TILES)

        @block.gpsimd
        def _(pool):
            ch = Chain(pool, s["pool_chain"])
            ch.link(pool.memset(zero_i, 0))
            pool.sem_inc(s["pool_setup"], 1)
            ch.link(pool.memset(ones[:, :], 1.0))
            ch.link(pool.memset(ident[:, :], 0.0))
            ch.link(pool.affine_select(out=ident[:, :], in_=ident[:, :], compare_op=ALU.not_equal, fill=1.0, base=0,
                                       pattern=[[-1, P]], channel_multiplier=1))
            for j in range(ROPE_HALF):
                pool.memset(freq[:, j:j + 1], INV_FREQ[j])
            pool.memset(state[:, :, :, :], 0.0)
            pool.memset(cum[:, :], 0.0)
            pool.memset(zero_e[:, :], 0.0)
            ch.link(pool.memset(vgu[:, 1, 2 * BANK:], 0.0))
            for h in range(HEADS):
                half = slice(HD * (h % 2), HD * (h % 2) + HD)
                ch.link(pool.memset(chunk_decay[half, h // 2:h // 2 + 1], math.exp(P * LOG_GAMMA[h])))
            iota = lambda out, pattern, base, cm: pool.iota(
                out, pattern=pattern, base=base, channel_multiplier=cm, allow_small_or_imprecise_dtypes=True)
            iota(rel[:, :], [[1, P]], 0, -1)
            iota(step1[:, :], [[1, P]], 1, 0)
            iota(back[:, :], [[0, 1]], P - 1, -1)
            iota(iota_e[:, :], [[1, E]], 0, 0)
            iota(tok_id[:, :], [[P, TILES]], 0, 1).then_inc(s["pool_setup"], 1)

            def body(t):
                pool.wait_ge(s["pos_done"], t + 1)
                pool.sem_inc(s["slots_seen"], 1)
                for k in range(TOPK):
                    pool.indirect_dma_start(
                        S["tok_list"], bass.IndirectOffsetOnAxis(ap=pos_cur[:, k:k + 1], axis=0),
                        tok_cur[:, :], None).then_inc(s["scattered"], 16)

            pool.wait_ge(s["list_zeroed"], 16)
            with pool.Fori(0, TILES) as t:
                body(t)
            pool.wait_ge(s["scattered"], 16 * TOPK * TILES)

        @block.scalar
        def _(act):
            def norm_x(t, par):
                act.wait_ge(s["x_loaded"], t * 16 + 16)
                act.activation(squares[:, :], x_sb[:, par, :], ACT.Square, accum_out=ss1[:, :]).then_inc(s["sumsq1"], 1)

            def copy_xT(t):
                act.wait_ge(s["xT_ps"], t + 1)
                act.activation(xT[:, 0:4, :], TR[:, 0:BANK], ACT.Copy).then_inc(s["xT_sb"], 1)
                act.activation(xT[:, 4:8, :], TR[:, BANK:], ACT.Copy).then_inc(s["xT_sb"], 1)

            def evacuate(t, par, n, has_prev):
                act.wait_ge(s["proj_ps"], t * 5 + (n + 1))
                if n == 0:
                    act.wait_ge(s["rstd1_ready"], t + 1)
                if n == 4 and has_prev:
                    act.wait_ge(s["pl_ps"], t)
                if n < 2:
                    dst = qk[:, n * HEADS:(n + 1) * HEADS, :, :].rearrange("p h two f -> p (h two f)")
                else:
                    dst = vgu[:, par, (n - 2) * BANK:(n - 1) * BANK]
                act.activation(dst, PJ[n % 2][:, :], ACT.Copy, scale=rstd1[:, :]).then_inc(s["proj_sb"], 1)

            def weigh(t):
                act.wait_ge(s["mask_done"], t + 1)
                act.activation(ex[:, :], top4[:, :], ACT.Exp, bias=ntop[:, :],
                               accum_out=exsum[:, :]).then_inc(s["ex_done"], 1)

            def body(t, par, has_prev, has_next):
                np_ = 1 - par
                if has_next:
                    if has_prev:
                        act.wait_ge(s["lg_ps"], t)
                    copy_xT(t + 1)
                    norm_x(t + 1, np_)
                if has_prev:
                    weigh(t - 1)
                act.wait_ge(s["qk_ps"], t + 1)
                act.activation(qT[:, :, :], SC[:, 0:BANK], ACT.Copy)
                act.activation(kT[:, :, :], SC[:, BANK:], ACT.Copy).then_inc(s["qkT_sb"], 1)
                if has_next:
                    evacuate(t + 1, np_, 0, True)
                    evacuate(t + 1, np_, 1, True)
                act.activation(tanh_g[:, :], vgu[:, par, BANK:2 * BANK], ACT.Tanh,
                               scale=0.5).then_inc(s["tanh_done"], 1)
                if has_next:
                    evacuate(t + 1, np_, 2, True)
                act.wait_ge(s["pl_ps"], t + 1)
                act.activation(pooledT[:, :, :], SC[:, 0:BANK], ACT.Copy).then_inc(s["pl_sb"], 1)
                act.wait_ge(s["mx_ps"], t + 1)
                act.activation(catT[:, 4:8, :], SC[:, BANK:], ACT.Copy).then_inc(s["mx_sb"], 1)
                if has_next:
                    evacuate(t + 1, np_, 3, True)
                act.wait_ge(s["ret_ps"], t + 1)
                act.activation(catT[:, 0:4, :], KV[:, :], ACT.Copy).then_inc(s["ret_sb"], 1)
                for n, done in enumerate(("h_half", "h_done")):
                    cols = slice(n * BANK, (n + 1) * BANK)
                    act.wait_ge(s[done], t + 1)
                    act.activation(squares[:, cols], x_sb[:, par, cols], ACT.Square,
                                   accum_out=ss2[:, n:n + 1]).then_inc(s["sumsq2"], 1)
                if has_next:
                    evacuate(t + 1, np_, 4, True)
                act.wait_ge(s["hn_ps"], t + 1)
                act.activation(hnT[:, 0:4, :], SC[:, 0:BANK], ACT.Copy).then_inc(s["hn_sb_done"], 1)
                act.activation(hnT[:, 4:8, :], SC[:, BANK:], ACT.Copy).then_inc(s["hn_sb_done"], 1)

            def scale_w_in(k):
                act.wait_ge(s[f"w_in_rows{k}"], 16)
                return act.activation(w_in[:, k, :], w_in[:, k, :], ACT.Copy, scale=gain_mix[:, k:k + 1])

            norm_x(0, 0)
            act.wait_ge(s["list_zeroed"], 16)
            copy_xT(0)
            act.wait_ge(s["loads"], 16 * 6)
            for k in range(4):
                scale_w_in(k)
            act.wait_ge(s["pool_setup"], 2)
            act.wait_ge(s["dve_setup"], 1)
            act.activation(sin[:, :, :], ang[:, :, :], ACT.Sin)
            act.activation(cos[:, :, :], ang[:, :, :], ACT.Sin, scale=0.5).then_inc(s["sines"], 1)
            for h in range(HEADS):
                half = slice(HD * (h % 2), HD * (h % 2) + HD)
                act.activation(decay[:, place_of(h), :], rel[:, :], ACT.Exp, scale=LOG_GAMMA[h])
                act.activation(zeta[:, h:h + 1], back[:, :], ACT.Exp, scale=LOG_GAMMA[h])
                last = act.activation(xi[half, h // 2, :], step1[half, :], ACT.Exp, scale=LOG_GAMMA[h])
            last.then_inc(s["act_setup"], 1)
            for k in range(4, KD):
                last = scale_w_in(k)
            last.then_inc(s["w_in_scaled"], 1)
            for n in range(5):
                evacuate(0, 0, n, False)
            body(0, 0, False, True)
            with act.Fori(0, 7) as i:
                for u in range(2):
                    body(i * 2 + (1 + u), (1 + u) % 2, True, True)
            body(15, 1, True, False)
            weigh(15)

        @block.vector
        def _(dve):
            ch = Chain(dve, s["dve_chain"])
            dve.wait_ge(s["pool_setup"], 2)
            dve.wait_ge(s["loads"], 16 * 6)
            ch.link(dve.tensor_copy(pos_f[:, :], pos_i[:, :]))
            ch.link(dve.tensor_tensor(ang[:, :, :], pos_f[:, :].unsqueeze(2).to_broadcast([P, TILES, ROPE_HALF]),
                                      freq[:, :].unsqueeze(1).to_broadcast([P, TILES, ROPE_HALF]), ALU.mult))
            reduce_angles(dve, ch, ang[:, :, :], turns[:, :, :])
            dve.tensor_scalar(causal[:, :], rel[:, :], 0.0, HD ** -0.5, ALU.is_ge, ALU.mult)
            dve.tensor_scalar(before[:, :], rel[:, :], 0.0, None, ALU.is_gt)
            dve.tensor_scalar(first_slot[:, :], iota_e[:, :], float(CAP), None, ALU.mult)
            for g, w in enumerate(WINDOWS):
                ch.link(dve.tensor_scalar(inside[:, :], rel[:, :], 0.0, None, ALU.is_ge))
                ch.link(dve.scalar_tensor_tensor(inside[:, :], rel[:, :], float(w - 1), inside[:, :],
                                                 ALU.is_le, ALU.mult))
                ch.link(dve.scalar_tensor_tensor(band[:, g, :], inside[:, :], 1.0 / w, ident[:, :],
                                                 ALU.mult, ALU.subtract))
                ch.link(dve.tensor_scalar(recip0[:, :], step1[:, :], float(w), None, ALU.min))
                ch.link(dve.reciprocal(recip0[:, :], recip0[:, :]))
                ch.link(dve.tensor_tensor(recip0[:, :], recip0[:, :], inside[:, :], ALU.mult))
                ch.link(dve.tensor_tensor(band0[:, g, :], recip0[:, :], ident[:, :], ALU.subtract))
                ch.link(dve.tensor_scalar(band_prev[:, g, :], rel[:, :], float(w - 1 - P), 1.0 / w,
                                          ALU.is_le, ALU.mult))
            dve.tensor_scalar(rel[:, :], rel[:, :], 0.0, None, ALU.max).then_inc(s["dve_setup"], 1)
            dve.wait_ge(s["sines"], 1)
            ch.link(dve.tensor_tensor(cos[:, :, :], cos[:, :, :], cos[:, :, :], ALU.mult))
            ch.link(dve.tensor_scalar(cos[:, :, :], cos[:, :, :], -2.0, 1.0, ALU.mult, ALU.add))
            dve.wait_ge(s["act_setup"], 1)
            ch.link(dve.tensor_tensor(decay[:, :, :], decay[:, :, :],
                                      causal[:, :].unsqueeze(1).to_broadcast([P, HEADS, P]), ALU.mult))
            ch.link(dve.tensor_scalar(zeta[:, :], zeta[:, :], HD ** -0.5, None, ALU.mult))
            def inv_rms(src, ms, y, t_, eps, count):
                ch.link(dve.tensor_scalar(ms[:, :], src[:, :], 1.0 / count, eps, ALU.mult, ALU.add))
                rsqrt(dve, ch, y[:, :], ms[:, :], t_[:, :])

            def norm_x(t, has_prev):
                dve.wait_ge(s["sumsq1"], t + 1)
                if has_prev:
                    dve.wait_ge(s["proj_sb"], t * 5)
                ch.link(dve.tensor_scalar(ms1[:, :], ss1[:, :], 1.0 / D, NORM_EPS, ALU.mult, ALU.add))
                rsqrt(dve, ch, rstd1[:, :], ms1[:, :], nt1[:, :], s["rstd1_ready"])

            def place(t, has_prev=True):
                dve.wait_ge(s["rank_ps"], t + 1)
                dve.wait_ge(s["ex_done"], t + 1)
                ch.link(dve.tensor_tensor(slot[:, :], KV[:, E:2 * E], first_slot[:, :], ALU.add))
                dve.tensor_tensor(cum[:, :], cum[:, :], mask[:, :], ALU.add)
                ch.link(dve.tensor_tensor(hit[:, :, :], onehot[:, :, :],
                                          slot[:, :].unsqueeze(1).to_broadcast([P, TOPK, E]), ALU.mult))
                ch.link(dve.tensor_reduce(posf[:, :], hit[:, :, :], AX, ALU.add))
                dve.tensor_copy(S["pos"][:, bass.ds(t * TOPK, TOPK)], posf[:, :])
                if has_prev:
                    dve.wait_ge(s["scattered"], t * (16 * TOPK))
                dve.tensor_copy(pos_cur[:, :], posf[:, :])
                dve.tensor_copy(tok_cur[:, :], tok_id[:, bass.ds(t, 1)])
                ch.link(dve.reciprocal(exrec[:, :], exsum[:, :]))
                dve.tensor_scalar(S["gates"][:, bass.ds(t * TOPK, TOPK)], ex[:, :], exrec[:, :], None,
                                  ALU.mult).then_inc(s["pos_done"], 1)

            def body(t, par, has_prev, has_next):
                c_t = cos[:, bass.ds(t, 1), :].to_broadcast([P, 2 * HEADS, ROPE_HALF])
                s_t = sin[:, bass.ds(t, 1), :].to_broadcast([P, 2 * HEADS, ROPE_HALF])
                dve.wait_ge(s["proj_sb"], t * 5 + 5)
                if has_prev:
                    dve.wait_ge(s["kv_ps"], t)
                dve.tensor_tensor(rope_a[:, :, :], qk[:, :, 0, :], c_t, ALU.mult)
                ch.link(dve.tensor_tensor(rope_b[:, :, :], qk[:, :, 1, :], s_t, ALU.mult))
                ch.link(dve.tensor_tensor(rot[:, :, 0, :], rope_a[:, :, :], rope_b[:, :, :], ALU.subtract))
                dve.tensor_tensor(rope_a[:, :, :], qk[:, :, 1, :], c_t, ALU.mult)
                ch.link(dve.tensor_tensor(rope_b[:, :, :], qk[:, :, 0, :], s_t, ALU.mult))
                ch.link(dve.tensor_tensor(rot[:, :, 1, :], rope_a[:, :, :], rope_b[:, :, :], ALU.add))
                k_rot = rot[:, HEADS:2 * HEADS, :, :].rearrange("p h two f -> p h (two f)")
                dve.tensor_tensor(kz[:, :, :], k_rot, zeta[:, :].unsqueeze(2).to_broadcast([P, HEADS, HD]),
                                  ALU.mult).then_inc(s["rope_done"], 1)
                if has_next:
                    norm_x(t + 1, True)
                dve.wait_ge(s["qkT_sb"], t + 1)
                dve.tensor_tensor(qxT[:, :, :], qT[:, :, :], xi[:, :, :], ALU.mult).then_inc(s["qx_sb"], 1)
                if has_prev:
                    place(t - 1, not isinstance(t, int) or t > 1)
                dve.wait_ge(s["sc_ps"], t + 1)
                dve.tensor_tensor(sT[:, :, :], TR[:, :].rearrange("p (h c) -> p h c", h=HEADS), decay[:, :, :],
                                  ALU.mult).then_inc(s["sT_sb"], 1)
                dve.wait_ge(s["y_ps"], t + 1)
                y = Y[:, :].rearrange("p (h e) -> p h e", h=HEADS)
                wide = lambda ap: ap.unsqueeze(2).to_broadcast([P, HEADS, HD])
                ch.link(dve.tensor_reduce(mean[:, :], y, AX, ALU.add))
                ch.link(dve.tensor_scalar(mean[:, :], mean[:, :], 1.0 / HD, None, ALU.mult))
                ch.link(dve.tensor_tensor(yc[:, :, :], y, wide(mean[:, :]), ALU.subtract))
                kv = KV[:, :].rearrange("p (a h2 e) -> p a h2 e", a=PAIRS, h2=2)
                both = state[:, :, :, :].rearrange("p a h2 e -> p a (h2 e)")
                ch.link(dve.tensor_tensor(both, both, chunk_decay[:, :].unsqueeze(2).to_broadcast([P, PAIRS, P]),
                                          ALU.mult))
                dve.tensor_tensor(state[0:HD, :, 0, :], state[0:HD, :, 0, :], kv[0:HD, :, 0, :], ALU.add)
                dve.tensor_tensor(state[HD:P, :, 1, :], state[HD:P, :, 1, :], kv[HD:P, :, 1, :],
                                  ALU.add).then_inc(s["state_new"], 1)
                ch.link(dve.tensor_tensor(ysq[:, :, :], yc[:, :, :], yc[:, :, :], ALU.mult))
                ch.link(dve.tensor_reduce(var[:, :], ysq[:, :, :], AX, ALU.add))
                inv_rms(var, var, gstd, gnt, GN_EPS, HD)
                ch.link(dve.tensor_tensor(yc[:, :, :], yc[:, :, :], wide(gstd[:, :]), ALU.mult))
                dve.wait_ge(s["tanh_done"], t + 1)
                g = vgu[:, par, BANK:2 * BANK]
                ch.link(dve.scalar_tensor_tensor(tanh_g[:, :], tanh_g[:, :], 1.0, g, ALU.add, ALU.mult))
                yn = yc[:, :, :].rearrange("p h e -> p (h e)")
                dve.scalar_tensor_tensor(yn, tanh_g[:, :], 0.5, yn, ALU.mult, ALU.mult).then_inc(s["ret_done"], 1)
                for n, done in enumerate(("h_half", "h_done")):
                    cols = slice(n * BANK, (n + 1) * BANK)
                    dve.wait_ge(s["o_ps"], t * 2 + (n + 1))
                    dve.tensor_tensor(x_sb[:, par, cols], TR[:, cols], x_sb[:, par, cols], ALU.add).then_inc(s[done], 1)
                dve.wait_ge(s["sumsq2"], t * 2 + 1)
                ch.link(dve.tensor_scalar(ms2[:, :], ss2[:, 0:1], 1.0 / D, NORM_EPS, ALU.mult, ALU.add))
                dve.wait_ge(s["sumsq2"], t * 2 + 2)
                ch.link(dve.scalar_tensor_tensor(ms2[:, :], ss2[:, 1:2], 1.0 / D, ms2[:, :], ALU.mult, ALU.add))
                rsqrt(dve, ch, rstd2[:, :], ms2[:, :], nt2[:, :])
                if has_prev:
                    dve.wait_ge(s["hn_stored"], t * 16)
                dve.scalar_tensor_tensor(hn_sb[:, :], x_sb[:, par, :], rstd2[:, :], gain_moe[:, :],
                                         ALU.mult, ALU.mult).then_inc(s["hn_done"], 1)
                dve.wait_ge(s["lg_ps"], t + 1)
                ch.link(dve.tensor_tensor(lg[:, :], KV[:, 0:E], bias_rt[:, :], ALU.add))
                ch.link(dve.tensor_reduce(ntop[:, :], lg[:, :], AX, ALU.max))
                dve.tensor_scalar(ntop[:, :], ntop[:, :], -1.0, None, ALU.mult)
                ch.link(dve.max(top8[:, :], lg[:, :]))
                dve.tensor_copy(top4[:, :], top8[:, 0:TOPK])
                ch.link(dve.max_index(idx8[:, :], top8[:, :], lg[:, :]))
                ch.link(dve.tensor_copy(idxf[:, :], idx8[:, 0:TOPK]))
                ch.link(dve.tensor_tensor(onehot[:, :, :], iota_e[:, :].unsqueeze(1).to_broadcast([P, TOPK, E]),
                                          idxf[:, :].unsqueeze(2).to_broadcast([P, TOPK, E]), ALU.is_equal))
                dve.tensor_reduce(mask[:, :], onehot[:, :, :].rearrange("p k e -> p e k"), AX,
                                  ALU.add).then_inc(s["mask_done"], 1)

            norm_x(0, False)
            dve.wait_ge(s["weights"], 16 * (KD + 2))
            for k in range(KD):
                last = dve.tensor_scalar(w_out[:, k, :], w_out[:, k, :], gain_out[:, k:k + 1], None, ALU.mult)
            last.then_inc(s["dve_setup"], 1)
            body(0, 0, False, True)
            body(1, 1, True, True)
            base = ch.n
            with dve.Fori(0, 6) as i:
                ch.start(base + i * (2 * BODY_LINKS))
                body(i * 2 + 2, 0, True, True)
                body(i * 2 + 3, 1, True, True)
                assert ch.n == 2 * BODY_LINKS, ch.n
            ch.start(base + 6 * 2 * BODY_LINKS)
            body(14, 0, True, True)
            body(15, 1, True, False)
            place(15)
            dve.wait_ge(s["totals_ps"], 1)
            ch.link(dve.tensor_scalar(cnt_i[:, :], Y[:, 0:E], float(P - 1), None, ALU.add))
            ch.link(dve.tensor_scalar(cnt_i[:, :], cnt_i[:, :], 7, None, ALU.arith_shift_right))
            ch.link(dve.tensor_scalar(cnt[:, :], cnt_i[:, :], 1.0, None, ALU.max))
            ch.link(dve.tensor_tensor_scan(ends[:, :], cnt[:, :], zero_e[:, :], 0.0, ALU.add, ALU.add))
            dve.memset(S["starts"][:, 0:1], 0)
            dve.tensor_copy(S["starts"][:, 1:E + 1], ends[:, :])
            dve.tensor_copy(S["n_tiles"][:, :], cnt[:, :])
            dve.tensor_scalar(S["n_more"][:, :], cnt[:, :], -1.0, None, ALU.add)
            dve.tensor_scalar(S["last"][:, :], ends[:, :], -1.0, None, ALU.add)
            to_row, e_of, row_f = cnt_e, posf_all[0], posf_all[1]
            ch.link(dve.tensor_tensor(to_row[:, :], ends[:, :], cnt[:, :], ALU.subtract))
            ch.link(dve.scalar_tensor_tensor(to_row[:, :], to_row[:, :], float(P), first_slot[:, :], ALU.mult, ALU.subtract))
            ch.link(dve.tensor_scalar(e_of.bitcast(I32), S["pos"][:, :], CAP.bit_length() - 1, None, ALU.arith_shift_right))
            dve.tensor_copy(row_f, S["pos"][:, :])
            ch.link(dve.tensor_copy(e_of, e_of.bitcast(I32)))
            shape = [P, TILES * TOPK, E]
            ch.link(dve.tensor_tensor(which, iota_e[:, :].unsqueeze(1).to_broadcast(shape),
                                      e_of.unsqueeze(2).to_broadcast(shape), ALU.is_equal))
            ch.link(dve.tensor_tensor(which, which, to_row[:, :].unsqueeze(1).to_broadcast(shape), ALU.mult))
            ch.link(dve.tensor_reduce(e_of, which, AX, ALU.add))
            dve.tensor_tensor(S["pos"][:, :], row_f, e_of, ALU.add)

        @block.tensor
        def _(pe):
            pe.wait_ge(s["pool_setup"], 2)

            def transpose_x(t, par, has_prev):
                pe.wait_ge(s["x_loaded"], t * 16 + 16)
                if has_prev:
                    pe.wait_ge(s["h_done"], t - 1)
                for k in range(KD):
                    mm = pe.transpose(TR[:, k * P:(k + 1) * P], x_sb[:, par, k * P:(k + 1) * P], ident[:, :])
                mm.then_inc(s["xT_ps"], 1)

            def project(t, n, has_prev=True):
                if has_prev or n > 1:
                    pe.wait_ge(s["proj_sb"], t * 5 + max(n - 1, 0))
                for k in range(KD):
                    if n == 0 and k % 4 == 0:
                        pe.wait_ge(s["xT_sb"], t * 2 + (k // 4 + 1))
                    mm = pe.matmul(PJ[n % 2][:, :], xT[:, k, :], w_in[:, k, n * BANK:(n + 1) * BANK],
                                   start=(k == 0), stop=(k == KD - 1))
                mm.then_inc(s["proj_ps"], 1)

            def project_out(n, steps):
                for k in steps:
                    mm = pe.matmul(TR[:, n * BANK:(n + 1) * BANK], catT[:, k, :], w_out[:, k, n * BANK:(n + 1) * BANK],
                                   start=(k == 4), stop=(k == 3))
                return mm

            def rank(t):
                pe.wait_ge(s["mask_done"], t + 1)
                pe.matmul(KV[:, E:2 * E], before[:, :], mask[:, :], start=True, stop=False)
                pe.matmul(KV[:, E:2 * E], ones[:, :], cum[:, :], start=False, stop=True).then_inc(s["rank_ps"], 1)

            def body(t, par, has_prev, has_next):
                if has_next:
                    transpose_x(t + 1, 1 - par, has_prev)
                    project(t + 1, 0)
                pe.wait_ge(s["rope_done"], t + 1)
                if has_prev:
                    pe.wait_ge(s["hn_sb_done"], t * 2)
                    pe.wait_ge(s["h_done"], t)
                for j in range(2 * PAIRS):
                    src = rot[:, 2 * j:2 * j + 2, :, :].rearrange("p h two f -> p (h two f)")
                    mm = pe.transpose(SC[:, j * P:(j + 1) * P], src, ident[:, :])
                mm.then_inc(s["qk_ps"], 1)
                if has_prev:
                    rank(t - 1)
                if has_next:
                    project(t + 1, 1)
                pe.wait_ge(s["qkT_sb"], t + 1)
                for h in range(HEADS):
                    half = slice(HD * (h % 2), HD * (h % 2) + HD)
                    mm = pe.matmul(TR[:, place_of(h) * P:(place_of(h) + 1) * P], kT[half, h // 2, :], qT[half, h // 2, :],
                                   start=True, stop=True)
                mm.then_inc(s["sc_ps"], 1)
                if has_prev:
                    pe.wait_ge(s["pos_done"], t)
                for a in range(PAIRS):
                    v_pair = vgu[:, par, a * P:(a + 1) * P]
                    mm = pe.matmul(KV[:, a * P:(a + 1) * P], kz[:, 2 * a:2 * a + 2, :].rearrange("p h d -> p (h d)"),
                                   v_pair, start=True, stop=True)
                mm.then_inc(s["kv_ps"], 1)
                if has_next:
                    project(t + 1, 2)
                pe.wait_ge(s["qx_sb"], t + 1)
                for g in range(GROUPS):
                    ug = slice(2 * BANK + g * P, 2 * BANK + (g + 1) * P)
                    pe.matmul(SC[:, g * P:(g + 1) * P], vgu[:, 1 - par, ug], band_prev[:, g, :],
                              start=True, stop=False)
                    mm = pe.matmul(SC[:, g * P:(g + 1) * P], vgu[:, par, ug],
                                   (band if has_prev else band0)[:, g, :], start=False, stop=True)
                mm.then_inc(s["pl_ps"], 1)
                pe.wait_ge(s["sT_sb"], t + 1)
                if has_prev:
                    pe.wait_ge(s["state_new"], t)
                for a in range(PAIRS):
                    pe.matmul(Y[:, a * P:(a + 1) * P], qxT[:, a, :],
                              state[:, a, :, :].rearrange("p h2 e -> p (h2 e)"), start=True, stop=False)
                    for h in (2 * a, 2 * a + 1):
                        mm = pe.matmul(Y[:, h * HD:(h + 1) * HD], sT[:, place_of(h), :],
                                       vgu[:, par, h * HD:(h + 1) * HD], start=False, stop=(h % 2 == 1))
                mm.then_inc(s["y_ps"], 1)
                pe.wait_ge(s["pl_sb"], t + 1)
                for g in range(GROUPS):
                    mm = pe.matmul(SC[:, BANK + g * P:BANK + (g + 1) * P], w_pool[:, g, :], pooledT[:, g, :],
                                   start=True, stop=True)
                mm.then_inc(s["mx_ps"], 1)
                if has_next:
                    project(t + 1, 3)
                pe.wait_ge(s["mx_sb"], t + 1)
                project_out(0, range(4, KD))
                project_out(1, range(4, 6))
                pe.wait_ge(s["ret_done"], t + 1)
                for a in range(PAIRS):
                    mm = pe.transpose(KV[:, a * P:(a + 1) * P], ret[:, 2 * a:2 * a + 2, :].rearrange("p h e -> p (h e)"), ident[:, :])
                mm.then_inc(s["ret_ps"], 1)
                project_out(1, range(6, KD))
                pe.wait_ge(s["ret_sb"], t + 1)
                project_out(0, range(4)).then_inc(s["o_ps"], 1)
                project_out(1, range(4)).then_inc(s["o_ps"], 1)
                if has_next:
                    project(t + 1, 4)
                pe.wait_ge(s["hn_done"], t + 1)
                for k in range(KD):
                    mm = pe.transpose(SC[:, k * P:(k + 1) * P], hn_sb[:, k * P:(k + 1) * P], ident[:, :])
                mm.then_inc(s["hn_ps"], 1)
                for k in range(KD):
                    if k % 4 == 0:
                        pe.wait_ge(s["hn_sb_done"], t * 2 + (k // 4 + 1))
                    mm = pe.matmul(KV[:, 0:E], hnT[:, k, :], w_rt[:, k, :], start=(k == 0), stop=(k == KD - 1))
                mm.then_inc(s["lg_ps"], 1)

            transpose_x(0, 0, False)
            pe.wait_ge(s["w_in_scaled"], 1)
            for n in range(5):
                project(0, n, False)
            pe.wait_ge(s["dve_setup"], 2)
            body(0, 0, False, True)
            with pe.Fori(0, 7) as i:
                for u in range(2):
                    body(i * 2 + (1 + u), (1 + u) % 2, True, True)
            body(15, 1, True, False)
            rank(15)
            pe.wait_ge(s["pos_done"], TILES)
            pe.matmul(Y[:, 0:E], ones[:, :], cum[:, :], start=True, stop=True).then_inc(s["totals_ps"], 1)


MAX_TILES = SEQ * TOPK // P + E
LIMIT, ALPHA = 7.0, 1.702
GU_CHUNKS = 2 * FF // BANK
CHUNKS_W = GU_CHUNKS + D // BANK
PARTS = 8
DVE_PARTS = 5
KP = KD // PARTS
ALL_PARTS = PARTS * CHUNKS_W
STAGES = PARTS
F32R = mybir.dt.float32r
BF16 = mybir.dt.bfloat16


def split_product(pe, out, high, low, short, w_high, w_low, ks, first, last):
    for k in ks:
        pe.matmul(out, high(k), w_high(k), start=(k == first), stop=False)
        pe.matmul(out, low(k), w_high(k), start=False, stop=False)
        mm = pe.matmul(out, short(k), w_low(k), start=False, stop=(k == last))
    return mm


def expert_phase(nc, I, S):
    with ExitStack() as ctx:
        sb = lambda name, shape, dt=F32: ctx.enter_context(nc.sbuf_tensor(name, shape, dt))
        pb = lambda name, w: ctx.enter_context(nc.psum_tensor(name, [P, w], F32))
        sem = lambda name: ctx.enter_context(nc.semaphore(name))

        w_hi = sb("w_hi", [P, CHUNKS_W, KD, BANK], F32R)
        w_lo = sb("w_lo", [P, CHUNKS_W, KD, BANK], BF16)
        stage = sb("stage", [P, STAGES, KP, BANK])
        b_gu = sb("b_gu", [P, 2 * FF])
        b_d = sb("b_d", [P, D])
        ident = sb("ident2", [P, P])
        ids = sb("ids", [P, 1], I32)
        rows = sb("rows", [P, D])
        x_hi = sb("x_hi", [P, KD, P], F32R)
        x_lo = sb("x_lo", [P, KD, P], F32R)
        x_bf = sb("x_bf", [P, KD, P], BF16)
        pre = sb("pre", [P, BANK])
        gate = sb("gate", [P, BANK // 2])
        tanh = sb("tanh", [P, BANK // 2])
        up = sb("up", [P, BANK // 2])
        acted = sb("acted", [P, FF])
        a_hi = sb("a_hi", [P, KD, P], F32R)
        a_lo = sb("a_lo", [P, KD, P], F32R)
        a_bf = sb("a_bf", [P, KD, P], BF16)
        y_sb = acted
        zero = sb("zero_rows", [P, P])

        GU = [pb(f"GU{n}", BANK) for n in range(3)]
        GU.append(GU[0])
        TX = pb("TX", 2 * BANK)
        TA = pb("TA", BANK)
        Y = pb("Y2", 2 * BANK)

        names = """ident_ready rows_free ids_free ids_seen xT_ps x_hi_ready x_ready bg_in0 bg_in1 bg_in2
            bg_in3 bd_in hi_done lo_dve lo_pool gu_ps gu_taken gate_ready tanh_ready acted_ready aT_ps a_hi_ready a_ready hi_seen y_half y_ps y_taken
            y_stored y_seen zero_ready zeroed dve_chain pool_chain""".split()
        s = {n: sem(n) for n in names}
        st_in = [sem(f"st_in{b}") for b in range(STAGES)]
        bg_in = [s[f"bg_in{c}"] for c in range(GU_CHUNKS)]
        ctx.enter_context(nc.allow_non_contiguous_dma(reason="a tile's token numbers, a word per partition"))
        s.update({f"st_in{b}": x for b, x in enumerate(st_in)})
        ctx.callback(clear_semaphores, nc, dict(s))
        s.update({n: S["keep"].enter_context(nc.semaphore(n)) for n in ("ids_in", "rows_in")})
        block = ctx.enter_context(nc.Block())

        list_t = S["tok_list"].rearrange("(n p) o -> n p o", p=P)
        y_t = S["y"].rearrange("(n p) d -> n p d", p=P)
        CAP_T = CAP // P
        half = BANK // 2

        def experts(eng, body, last_body):
            def read(table, e, most):
                return eng.value_load(S[table][0:1, bass.ds(e, 1)], min_val=0, max_val=most)

            with eng.Fori(0, E - 1) as e:
                first = read("starts", e, MAX_TILES - 1)
                with eng.Fori(0, read("n_more", e, CAP_T - 1)) as t:
                    body(e, eng.snap(first + t, min_val=0, max_val=MAX_TILES - 1))
                last_body(e, read("last", e, MAX_TILES - 1))
            first = read("starts", E - 1, MAX_TILES - 1)
            with eng.Fori(0, read("n_tiles", E - 1, CAP_T)) as t:
                body(E - 1, eng.snap(first + t, min_val=0, max_val=MAX_TILES - 1))

        def weights_of(m):
            c, part = m // PARTS, m % PARTS
            return c, slice(part * KP, (part + 1) * KP)

        def shared(c, engine):
            return range(PARTS * c + (DVE_PARTS if engine else 0), PARTS * c + (PARTS if engine else DVE_PARTS))

        def low_done(eng, e, m):
            c, part = divmod(m, PARTS)
            if part < DVE_PARTS:
                eng.wait_ge(s["lo_dve"], e * (CHUNKS_W * DVE_PARTS) + (c * DVE_PARTS + part + 1))
            else:
                rest = PARTS - DVE_PARTS
                eng.wait_ge(s["lo_pool"], e * (CHUNKS_W * rest) + (c * rest + part - DVE_PARTS + 1))

        @block.sync
        def _(sp):
            def load(e, m):
                c, ks = weights_of(m)
                name, col = ("expert_w_gate_up", c) if c < GU_CHUNKS else ("expert_w_down", c - GU_CHUNKS)
                w = I[name][0, bass.ds(e, 1), ks.start * P:ks.stop * P, col * BANK:(col + 1) * BANK].squeeze(0)
                sp.dma_start(stage[:, m % STAGES, :, :], w.rearrange("(k p) n -> p k n", p=P)).then_inc(st_in[m % STAGES], 16)

            for m in range(STAGES):
                load(0, m)
            for m in range(STAGES, ALL_PARTS):
                low_done(sp, 0, m - STAGES)
                load(0, m)
            with sp.Fori(1, E) as e:
                for m in range(ALL_PARTS):
                    if m < STAGES:
                        low_done(sp, e - 1, m + ALL_PARTS - STAGES)
                    else:
                        low_done(sp, e, m - STAGES)
                    load(e, m)
            total = sp.value_load(S["starts"][0:1, E:E + 1], min_val=E, max_val=MAX_TILES)
            sp.wait_ge(s["zero_ready"], 1)
            with sp.Fori(total, MAX_TILES) as g:
                sp.dma_start(y_t[bass.ds(g, 1)].squeeze(0).rearrange("p (r c) -> p r c", c=P),
                             zero[:, :].unsqueeze(1).to_broadcast([P, D // P, P])).then_inc(s["zeroed"], 16)
            with sp.Fori(0, total) as g:
                sp.sem_inc(s["zeroed"], 16)
            sp.wait_ge(s["zeroed"], 16 * MAX_TILES)

        @block.gpsimd
        def _(pool):
            ch = Chain(pool, s["pool_chain"])
            ch.link(pool.memset(zero[:, :], 0.0))
            pool.sem_inc(s["zero_ready"], 1)
            make_identity(pool, ch, ident[:, :], s["ident_ready"])

            def gather(slot, g):
                pool.dma_start(ids[:, :], list_t[bass.ds(slot, 1)].squeeze(0)).then_inc(s["ids_in"], 16)
                pool.wait_ge(s["xT_ps"], g + 1)
                pool.sem_inc(s["rows_free"], 1)
                pool.wait_ge(s["ids_in"], g * 16 + 16)
                pool.sem_inc(s["ids_seen"], 1)
                pool.indirect_dma_start(rows[:, :], None, S["hn"],
                                        bass.IndirectOffsetOnAxis(ap=ids[:, :], axis=0)).then_inc(s["rows_in"], 16)
                pool.wait_ge(s["rows_in"], g * 16 + 16)
                pool.sem_inc(s["ids_free"], 1)

            def split(e, c):
                for m in shared(c, 1):
                    ks = weights_of(m)[1]
                    pool.wait_ge(s["hi_done"], e * ALL_PARTS + (m + 1))
                    pool.sem_inc(s["hi_seen"], 1)
                    pool.tensor_tensor(w_lo[:, c, ks, :], stage[:, m % STAGES, :, :], w_hi[:, c, ks, :],
                                       ALU.subtract).then_inc(s["lo_pool"], 1)

            gather(0, 0)
            for c in range(CHUNKS_W):
                split(0, c)

            def read(table, e, most):
                return pool.value_load(S[table][0:1, bass.ds(e, 1)], min_val=0, max_val=most)

            def gathers(e):
                first = read("starts", e, MAX_TILES - 1)
                with pool.Fori(0, read("n_more", e, CAP_T - 1)) as t:
                    gather(e * CAP_T + t + 1, pool.snap(first + t + 1, min_val=0, max_val=MAX_TILES - 1))

            with pool.Fori(0, E - 1) as e:
                gathers(e)
                gather(e * CAP_T + CAP_T, read("last", e, MAX_TILES - 1) + 1)
                for c in range(CHUNKS_W):
                    split(e + 1, c)
            gathers(E - 1)
            total = pool.value_load(S["starts"][0:1, E:E + 1], min_val=0, max_val=MAX_TILES)
            gather(0, total)

        @block.scalar
        def _(act):
            def bias(e, c):
                cols = slice(c * BANK, (c + 1) * BANK)
                b = I["expert_b_gate_up"][0, bass.ds(e, 1), cols].squeeze(0)
                act.dma_start(b_gu[:, cols], b.partition_broadcast(P)).then_inc(bg_in[c], 16)

            def bias_down(e):
                b = I["expert_b_down"][0, bass.ds(e, 1)].squeeze(0)
                act.dma_start(b_d[:, :], b.partition_broadcast(P)).then_inc(s["bd_in"], 16)

            def split(e, c):
                for m in range(PARTS * c, PARTS * (c + 1)):
                    act.wait_ge(st_in[m % STAGES], (e * (ALL_PARTS // STAGES) + (m // STAGES + 1)) * 16)
                    act.activation(w_hi[:, c, weights_of(m)[1], :], stage[:, m % STAGES, :, :],
                                   ACT.Copy).then_inc(s["hi_done"], 1)

            def x_high(g):
                act.wait_ge(s["xT_ps"], g + 2)
                for n in range(2):
                    act.activation(x_hi[:, 4 * n:4 * n + 4, :], TX[:, n * BANK:(n + 1) * BANK],
                                   ACT.Copy).then_inc(s["x_hi_ready"], 1)
                act.wait_ge(s["x_hi_ready"], g * 2 + 2)
                act.activation(x_bf[:, :, :], x_hi[:, :, :], ACT.Copy).then_inc(s["x_ready"], 1)

            def a_high(g, n):
                ks = slice(4 * n, 4 * n + 4)
                act.wait_ge(s["aT_ps"], g * 2 + (n + 1))
                act.activation(a_hi[:, ks, :], TA[:, :], ACT.Copy,
                               scale=0.5).then_inc(s["a_hi_ready"], 1)
                act.wait_ge(s["a_hi_ready"], g * 2 + (n + 1))
                act.activation(a_bf[:, ks, :], a_hi[:, ks, :], ACT.Copy).then_inc(s["a_ready"], 1)

            def body(e, g, next_e=None):
                for c in range(GU_CHUNKS):
                    act.wait_ge(s["gate_ready"], g * GU_CHUNKS + (c + 1))
                    act.activation(tanh[:, :], gate[:, :], ACT.Tanh,
                                   scale=ALPHA / 2).then_inc(s["tanh_ready"], 1)
                    if c == GU_CHUNKS - 2:
                        a_high(g, 0)
                    if next_e is not None:
                        bias(next_e, c)
                        if c < GU_CHUNKS - 1:
                            split(next_e, c)
                a_high(g, 1)
                x_high(g + 1)
                if next_e is not None:
                    split(next_e, GU_CHUNKS - 1)
                    act.wait_ge(s["y_half"], g + 1)
                    split(next_e, GU_CHUNKS)
                act.wait_ge(s["y_taken"], g + 2)
                tile = nc.s_assert_within(g, 0, MAX_TILES - 1, skip_runtime_bounds_check_because="the counts sum to MAX_TILES at most")
                act.dma_start(y_t[bass.ds(tile, 1)].squeeze(0), y_sb[:, :]).then_inc(s["y_stored"], 16)
                if next_e is not None:
                    bias_down(next_e)
                    split(next_e, GU_CHUNKS + 1)

            act.sem_inc(s["y_stored"], 16)
            for c in range(GU_CHUNKS):
                bias(0, c)
            bias_down(0)
            split(0, 0)
            x_high(0)
            for c in range(1, CHUNKS_W):
                split(0, c)
            experts(act, body, lambda e, g: body(e, g, e + 1))
            total = act.value_load(S["starts"][0:1, E:E + 1], min_val=0, max_val=MAX_TILES)
            act.wait_ge(s["y_stored"], total * 16 + 16)
            act.sem_inc(s["y_seen"], 1)

        @block.vector
        def _(dve):
            ch = Chain(dve, s["dve_chain"])
            dve.sem_inc(s["gu_taken"], 1)
            dve.sem_inc(s["y_taken"], 1)

            def split(e, c, some=slice(None)):
                for m in shared(c, 0)[some]:
                    ks = weights_of(m)[1]
                    dve.wait_ge(s["hi_done"], e * ALL_PARTS + (m + 1))
                    dve.tensor_tensor(w_lo[:, c, ks, :], stage[:, m % STAGES, :, :], w_hi[:, c, ks, :],
                                      ALU.subtract).then_inc(s["lo_dve"], 1)

            def x_low(g):
                for n in range(2):
                    dve.wait_ge(s["x_hi_ready"], g * 2 + (n + 1))
                    dve.tensor_tensor(x_lo[:, 4 * n:4 * n + 4, :], TX[:, n * BANK:(n + 1) * BANK].rearrange("p (k c) -> p k c", k=4),
                                      x_hi[:, 4 * n:4 * n + 4, :], ALU.subtract).then_inc(s["x_ready"], 1)

            def a_low(g, n):
                dve.wait_ge(s["a_hi_ready"], g * 2 + (n + 1))
                dve.scalar_tensor_tensor(a_lo[:, 4 * n:4 * n + 4, :], TA[:, :].rearrange("p (k c) -> p k c", k=4),
                                         0.5, a_hi[:, 4 * n:4 * n + 4, :], ALU.mult, ALU.subtract).then_inc(s["a_ready"], 1)

            def body(e, g, next_e=None):
                ch.start(g * EXPERT_LINKS)
                for c in range(GU_CHUNKS):
                    dve.wait_ge(bg_in[c], e * 16 + 16)
                    dve.wait_ge(s["gu_ps"], g * GU_CHUNKS + (c + 1))
                    ch.link(dve.tensor_tensor(pre[:, :], GU[c][:, :], b_gu[:, c * BANK:(c + 1) * BANK], ALU.add))
                    pair = pre[:, :].rearrange("p (j two) -> p j two", two=2)
                    dve.tensor_scalar(gate[:, :], pair[:, :, 0], LIMIT, None, ALU.min).then_inc(s["gate_ready"], 1)
                    ch.link(dve.tensor_scalar(up[:, :], pair[:, :, 1], LIMIT, -LIMIT, ALU.min, ALU.max))
                    dve.sem_inc(s["gu_taken"], 1)
                    dve.wait_ge(s["tanh_ready"], g * GU_CHUNKS + (c + 1))
                    ch.link(dve.scalar_tensor_tensor(gate[:, :], tanh[:, :], 1.0, gate[:, :],
                                                     ALU.add, ALU.mult))
                    if c == 0:
                        dve.wait_ge(s["y_stored"], g * 16 + 16)
                    dve.scalar_tensor_tensor(acted[:, c * half:(c + 1) * half], up[:, :], 1.0, gate[:, :],
                                             ALU.add, ALU.mult).then_inc(s["acted_ready"], 1)
                    if c == GU_CHUNKS - 2:
                        a_low(g, 0)
                    if next_e is not None and c < GU_CHUNKS - 2:
                        split(next_e, c)
                    if next_e is not None and c >= GU_CHUNKS - 2:
                        split(next_e, GU_CHUNKS - 2, slice(0, 1) if c == GU_CHUNKS - 2 else slice(1, None))
                a_low(g, 1)
                x_low(g + 1)
                if next_e is not None:
                    split(next_e, GU_CHUNKS - 1)
                    split(next_e, GU_CHUNKS)
                dve.wait_ge(s["bd_in"], e * 16 + 16)
                dve.wait_ge(s["y_ps"], g + 1)
                dve.tensor_tensor(y_sb[:, :], Y[:, :], b_d[:, :], ALU.add).then_inc(s["y_taken"], 1)
                if next_e is not None:
                    split(next_e, GU_CHUNKS + 1)
                assert ch.n == EXPERT_LINKS, ch.n

            split(0, 0)
            x_low(0)
            for c in range(1, CHUNKS_W):
                split(0, c)
            experts(dve, body, lambda e, g: body(e, g, e + 1))

        @block.tensor
        def _(pe):
            def transpose_rows(g):
                pe.wait_ge(s["rows_in"], g * 16 + 16)
                for k in range(KD):
                    mm = pe.transpose(TX[:, k * P:(k + 1) * P], rows[:, k * P:(k + 1) * P], ident[:, :])
                mm.then_inc(s["xT_ps"], 1)

            def transpose_act(g, n):
                pe.wait_ge(s["acted_ready"], g * GU_CHUNKS + 2 * (n + 1))
                for k in range(4 * n, 4 * n + 4):
                    mm = pe.transpose(TA[:, k % 4 * P:(k % 4 + 1) * P], acted[:, k * P:(k + 1) * P], ident[:, :])
                mm.then_inc(s["aT_ps"], 1)

            def body(e, g):
                def product(out, parts, c, ks):
                    hi, lo, bf = parts
                    return split_product(pe, out, lambda k: hi[:, k, :], lambda k: lo[:, k, :], lambda k: bf[:, k, :],
                                         lambda k: w_hi[:, c, k, :], lambda k: w_lo[:, c, k, :], ks, 0, KD - 1)

                def gate_up(c):
                    for engine in range(2):
                        low_done(pe, e, shared(c, engine)[-1])
                    if c == 0:
                        pe.wait_ge(s["x_ready"], g * 3 + 3)
                    if c in (0, GU_CHUNKS - 1):
                        pe.wait_ge(s["gu_taken"], g * GU_CHUNKS + (1 if c == 0 else 2))
                    x_parts = (x_hi, x_lo, x_bf)
                    if c == GU_CHUNKS - 1:
                        product(GU[c][:, :], x_parts, c, range(KD // 2))
                        transpose_act(g, 0)
                        product(GU[c][:, :], x_parts, c, range(KD // 2, KD)).then_inc(s["gu_ps"], 1)
                    else:
                        product(GU[c][:, :], x_parts, c, range(KD)).then_inc(s["gu_ps"], 1)

                def down(n, kh):
                    return product(Y[:, n * BANK:(n + 1) * BANK], (a_hi, a_lo, a_bf), GU_CHUNKS + n,
                                   range(KD // 2 * kh, KD // 2 * (kh + 1)))

                for c in range(GU_CHUNKS):
                    gate_up(c)
                for engine in range(2):
                    low_done(pe, e, shared(CHUNKS_W - 1, engine)[-1])
                pe.wait_ge(s["y_taken"], g + 1)
                pe.wait_ge(s["a_ready"], g * 4 + 2)
                down(0, 0)
                transpose_rows(g + 1)
                transpose_act(g, 1)
                down(1, 0)
                pe.wait_ge(s["a_ready"], g * 4 + 4)
                down(0, 1).then_inc(s["y_half"], 1)
                down(1, 1).then_inc(s["y_ps"], 1)

            pe.sem_inc(s["xT_ps"], 1)
            pe.wait_ge(s["ident_ready"], 1)
            transpose_rows(0)
            experts(pe, body, body)


EXPERT_LINKS = 3 * GU_CHUNKS


PLE = 256
Q_RANK, KV_RANK, ROPE_D, ATTN_W, SSM_W = 256, 128, 64, 512, 512
Z_COLS = Q_RANK + KV_RANK + ROPE_D + ATTN_W + 2 * SSM_W
Z_KV, Z_KR, Z_GA = Q_RANK, Q_RANK + KV_RANK, Q_RANK + KV_RANK + ROPE_D
Z_U, Z_GS = Z_GA + ATTN_W, Z_GA + ATTN_W + SSM_W
Z_CHUNKS = [(c, min(c + BANK, Z_COLS)) for c in range(0, Z_COLS, BANK)]
EPS = 1e-6


def is_step(t, n):
    return isinstance(t, int) and t == n


def inv_rms(dve, ch, y, total, t, count, eps, done=None):
    ch.link(dve.tensor_scalar(total, total, 1.0 / count, eps, ALU.mult, ALU.add))
    rsqrt(dve, ch, y, total, t, done)


INV_RMS_LINKS = 12


def combine_phase(nc, I, S):
    with ExitStack() as ctx:
        sb = lambda name, shape, dt=F32: ctx.enter_context(nc.sbuf_tensor(name, shape, dt))
        pb = lambda name, w: ctx.enter_context(nc.psum_tensor(name, [P, w], F32))
        sem = lambda name: ctx.enter_context(nc.semaphore(name))

        w_gate = sb("w_gate", [P, KD, D])
        w_ple = sb("w_ple", [P, PLE // P, D])
        w_hi = sb("w_in2_hi", [P, KD, Z_COLS], F32R)
        w_lo = sb("w_in2_lo", [P, KD, Z_COLS], BF16)
        gain_ple = sb("gain_ple", [P, KD])
        gain_pre = sb("gain_pre", [P, KD])
        gain_final = sb("gain_final", [P, D])
        ident = sb("ident3", [P, P])
        slots = [sb(f"slots{u}", [P, TOPK], I32) for u in range(2)]
        y_rows = sb("y_rows", [P, TOPK, D])
        h = sb("h", [P, 2, D])
        p_sb = sb("p_sb", [P, 2, PLE])
        hT = sb("hT", [P, KD, P])
        pT = sb("pT", [P, PLE // P, P])
        x2_hi = sb("x2_hi", [P, KD, P], F32R)
        x2_lo = sb("x2_lo", [P, KD, P], F32R)
        x2_bf = sb("x2_bf", [P, KD, P], BF16)
        tanh = sb("tanh3", [P, D])
        z_sb = sb("z_sb", [P, 2, Z_COLS])
        squares = sb("squares3", [P, D], mybir.dt.bfloat16)
        ss_h, ss_3, ss_2, rstd_h, rstd_3, nt = (sb(n, [P, 1]) for n in ("ss_h", "ss_3", "ss_2", "rstd_h", "rstd_3", "nt"))
        rstd_2 = sb("rstd_2", [P, 2])

        TR = pb("TR3", 2 * BANK)
        G = pb("G3", 2 * BANK)
        PP = pb("PP3", 2 * BANK)
        Z = [pb("Z0", BANK), pb("Z1", BANK)]

        names = """gains gate_in ple_in proj_in0 proj_in1 ident_ready gate_scaled proj_hi proj_lo y_seen y_used h_loaded h2_done hT_ps hT_sb pT_ps
            pT_sb sumsq_h rstd_h_ready g_ps tanh_done pp_ps h3_done sumsq_3 x2_done sumsq_2 rstd_2_ready x2T_ps x2_hi_ready x2T_sb
            z_ps z_sb x2_stored z_stored dve_chain pool_chain""".split()
        s = {n: sem("c_" + n) for n in names}
        ctx.enter_context(nc.allow_non_contiguous_dma(reason="gains, a word per partition"))
        ctx.callback(clear_semaphores, nc, dict(s))
        s.update({n: S["keep"].enter_context(nc.semaphore(n)) for n in ('y_in',)})
        block = ctx.enter_context(nc.Block())

        tiles = lambda ap: ap.rearrange("(t p) d -> t p d", p=P)
        h_t, x2_t, z_t, p_t = tiles(S["h1"]), tiles(S["x2"]), tiles(S["z"]), tiles(I["p"][0, 0])

        @block.sync
        def _(sp):
            def load(t, par):
                sp.dma_start(h[:, par, :], h_t[bass.ds(t, 1)].squeeze(0)).then_inc(s["h_loaded"], 16)
                sp.dma_start(p_sb[:, par, :], p_t[bass.ds(t, 1)].squeeze(0)).then_inc(s["h_loaded"], 16)

            def store(t, par, has_next):
                sp.wait_ge(s["x2_done"], t + 1)
                sp.dma_start(x2_t[bass.ds(t, 1)].squeeze(0), h[:, par, :]).then_inc(s["x2_stored"], 16)
                if has_next:
                    sp.wait_ge(s["sumsq_2"], t + 1)
                    sp.wait_ge(s["x2T_ps"], t + 1)
                    sp.wait_ge(s["x2_stored"], t * 16 + 16)
                    load(t + 2, par)
                sp.wait_ge(s["z_sb"], (t + 1) * len(Z_CHUNKS))
                if not is_step(t, 0):
                    sp.wait_ge(s["z_stored"], t * 16)
                sp.dma_start(z_t[bass.ds(t, 1)].squeeze(0), z_sb[:, par, :]).then_inc(s["z_stored"], 16)

            load(0, 0)
            sp.dma_start(gain_ple[:, :], I["norm_ple_w"][0].rearrange("(k p) -> p k", p=P)).then_inc(s["gains"], 16)
            sp.dma_start(gain_pre[:, :], I["pre_norm_g_2"][0].rearrange("(k p) -> p k", p=P)).then_inc(s["gains"], 16)
            sp.dma_start(gain_final[:, :], I["final_norm_w"].partition_broadcast(P)).then_inc(s["gains"], 16)
            for k in range(KD):
                sp.dma_start(w_gate[:, k, :], I["ple_gate_w"][0, k * P:(k + 1) * P, :]).then_inc(s["gate_in"], 16)
            for k in range(PLE // P):
                sp.dma_start(w_ple[:, k, :], I["ple_proj_w"][0, k * P:(k + 1) * P, :]).then_inc(s["ple_in"], 16)
            sp.wait_ge(s["h_loaded"], 32)
            load(1, 1)
            for k in range(KD):
                if k > 1:
                    sp.wait_ge(s["proj_lo"], k - 1)
                sp.dma_start(z_sb[:, k % 2, :], I["w_in_2"][0, k * P:(k + 1) * P, :]).then_inc(s[f"proj_in{k % 2}"], 16)
            for t in (0, 1):
                store(t, t, True)
            with sp.Fori(1, TILES // 2 - 1) as i:
                for u in range(2):
                    store(i * 2 + u, u, True)
            for t in (TILES - 2, TILES - 1):
                store(t, t % 2, False)
            sp.wait_ge(s["x2_stored"], 16 * TILES)
            sp.wait_ge(s["z_stored"], 16 * TILES)

        @block.gpsimd
        def _(pool):
            ch = Chain(pool, s["pool_chain"])
            make_identity(pool, ch, ident[:, :], s["ident_ready"])

            def gather(t, par, has_prev):
                if has_prev:
                    pool.wait_ge(s["y_used"], t)
                    pool.sem_inc(s["y_seen"], 1)
                ch.link(pool.tensor_copy(slots[par][:, :], S["pos"][:, bass.ds(t * TOPK, TOPK)]))
                pool.sem_inc(s["y_seen"], 1)
                for k in range(TOPK):
                    pool.indirect_dma_start(y_rows[:, k, :], None, S["y"], bass.IndirectOffsetOnAxis(
                        ap=slots[par][:, k:k + 1], axis=0)).then_inc(s["y_in"], 16)
                pool.wait_ge(s["y_in"], t * (16 * TOPK) + 16 * TOPK)
                pool.sem_inc(s["y_seen"], 1)

            gather(0, 0, False)
            gather(1, 1, True)
            base = ch.n
            with pool.Fori(1, TILES // 2) as i:
                ch.start(i * 2 + (base - 2))
                for u in range(2):
                    gather(i * 2 + u, u, True)

        @block.scalar
        def _(act):
            def square_h(t, par):
                act.wait_ge(s["h2_done"], t + 1)
                act.activation(squares[:, :], h[:, par, :], ACT.Square, accum_out=ss_h[:, :]).then_inc(s["sumsq_h"], 1)

            def copy_hT(t):
                act.wait_ge(s["hT_ps"], t + 1)
                act.activation(hT[:, 0:4, :], TR[:, 0:BANK], ACT.Copy)
                act.activation(hT[:, 4:8, :], TR[:, BANK:], ACT.Copy).then_inc(s["hT_sb"], 1)
                act.wait_ge(s["pT_ps"], t + 1)
                act.activation(pT[:, :, :], PP[:, 0:PLE], ACT.Copy).then_inc(s["pT_sb"], 1)

            def copy_x2T(t):
                act.wait_ge(s["x2T_ps"], t + 1)
                for n in range(2):
                    act.activation(x2_hi[:, 4 * n:4 * n + 4, :], TR[:, n * BANK:(n + 1) * BANK],
                                   ACT.Copy).then_inc(s["x2_hi_ready"], 1)
                act.wait_ge(s["x2_hi_ready"], t * 2 + 2)
                act.activation(x2_bf[:, :, :], x2_hi[:, :, :], ACT.Copy).then_inc(s["x2T_sb"], 1)

            def gate(t):
                act.wait_ge(s["g_ps"], t + 1)
                act.wait_ge(s["rstd_h_ready"], t + 1)
                act.activation(tanh[:, 0:BANK], G[:, 0:BANK], ACT.Tanh, scale=rstd_h[:, :])
                act.activation(tanh[:, BANK:], G[:, BANK:], ACT.Tanh, scale=rstd_h[:, :]).then_inc(s["tanh_done"], 1)

            def square_3(t, par):
                act.wait_ge(s["h3_done"], t + 1)
                act.activation(squares[:, :], h[:, par, :], ACT.Square, accum_out=ss_3[:, :]).then_inc(s["sumsq_3"], 1)

            def square_2(t, par):
                act.wait_ge(s["x2_done"], t + 1)
                act.activation(squares[:, :], h[:, par, :], ACT.Square, accum_out=ss_2[:, :]).then_inc(s["sumsq_2"], 1)

            def copy_z(t, par, n, has_prev):
                lo, hi = Z_CHUNKS[n]
                act.wait_ge(s["z_ps"], t * len(Z_CHUNKS) + (n + 1))
                if n == 0:
                    act.wait_ge(s["rstd_2_ready"], t + 1)
                    if has_prev:
                        act.wait_ge(s["z_stored"], t * 16 - 16)
                act.activation(z_sb[:, par, lo:hi], Z[n % 2][:, 0:hi - lo], ACT.Copy,
                               scale=rstd_2[:, par:par + 1]).then_inc(s["z_sb"], 1)

            def high_weights():
                act.wait_ge(s["gains"], 48)
                for k in range(KD):
                    act.wait_ge(s[f"proj_in{k % 2}"], 16 * (k // 2 + 1))
                    act.activation(w_hi[:, k, :], z_sb[:, k % 2, :], ACT.Copy,
                                   scale=gain_pre[:, k:k + 1]).then_inc(s["proj_hi"], 1)

            def body(t, par, has_next, has_prev):
                if has_next:
                    square_h(t, par)
                    copy_hT(t)
                    if is_step(t, 0):
                        high_weights()
                if not is_step(t, 0):
                    copy_x2T(t - 1)
                if has_next:
                    gate(t)
                    square_3(t, par)
                if not is_step(t, 0):
                    copy_z(t - 1, 1 - par, 0, has_prev)
                if has_next:
                    square_2(t, par)
                if not is_step(t, 0):
                    for n in range(1, len(Z_CHUNKS)):
                        copy_z(t - 1, 1 - par, n, has_prev)

            body(0, 0, True, False)
            body(1, 1, True, False)
            body(2, 0, True, False)
            with act.Fori(1, TILES // 2 - 1) as i:
                body(i * 2 + 1, 1, True, True)
                body(i * 2 + 2, 0, True, True)
            body(TILES - 1, 1, True, True)
            body(TILES, 0, False, True)

        @block.vector
        def _(dve):
            ch = Chain(dve, s["dve_chain"])

            def low_x2(t):
                dve.wait_ge(s["x2T_ps"], t + 1)
                for n in range(2):
                    dve.wait_ge(s["x2_hi_ready"], t * 2 + (n + 1))
                    dve.tensor_tensor(x2_lo[:, 4 * n:4 * n + 4, :], TR[:, n * BANK:(n + 1) * BANK].rearrange("p (k c) -> p k c", k=4),
                                      x2_hi[:, 4 * n:4 * n + 4, :], ALU.subtract).then_inc(s["x2T_sb"], 1)

            def combine(t, par):
                dve.wait_ge(s["y_in"], t * (16 * TOPK) + 16 * TOPK)
                dve.wait_ge(s["h_loaded"], t * 32 + 32)
                for k in range(TOPK):
                    last = dve.scalar_tensor_tensor(h[:, par, :], y_rows[:, k, :], S["gates"][:, bass.ds(t * TOPK + k, 1)],
                                                    h[:, par, :], ALU.mult, ALU.add)
                    if k < TOPK - 1:
                        ch.link(last)
                ch.link(last)
                dve.sem_inc(s["y_used"], 1)
                dve.sem_inc(s["h2_done"], 1)
                dve.wait_ge(s["sumsq_h"], t + 1)
                inv_rms(dve, ch, rstd_h[:, :], ss_h[:, :], nt[:, :], D, NORM_EPS)
                dve.tensor_scalar(rstd_h[:, :], rstd_h[:, :], 0.5, None, ALU.mult).then_inc(s["rstd_h_ready"], 1)

            def finish(t, par, has_prev):
                dve.wait_ge(s["tanh_done"], t + 1)
                dve.wait_ge(s["pp_ps"], t + 1)
                ch.link(dve.scalar_tensor_tensor(tanh[:, :], tanh[:, :], 1.0, PP[:, :], ALU.add, ALU.mult))
                dve.scalar_tensor_tensor(h[:, par, :], tanh[:, :], 0.5, h[:, par, :],
                                         ALU.mult, ALU.add).then_inc(s["h3_done"], 1)
                dve.wait_ge(s["sumsq_3"], t + 1)
                inv_rms(dve, ch, rstd_3[:, :], ss_3[:, :], nt[:, :], D, NORM_EPS)
                dve.scalar_tensor_tensor(h[:, par, :], h[:, par, :], rstd_3[:, :], gain_final[:, :],
                                         ALU.mult, ALU.mult).then_inc(s["x2_done"], 1)
                dve.wait_ge(s["sumsq_2"], t + 1)
                if has_prev:
                    dve.wait_ge(s["z_sb"], (t - 1) * len(Z_CHUNKS))
                inv_rms(dve, ch, rstd_2[:, par:par + 1], ss_2[:, :], nt[:, :], D, EPS, s["rstd_2_ready"])

            combine(0, 0)
            dve.wait_ge(s["gains"], 48)
            dve.wait_ge(s["gate_in"], 16 * KD)
            for k in range(KD):
                dve.tensor_scalar(w_gate[:, k, :], w_gate[:, k, :], gain_ple[:, k:k + 1], None, ALU.mult).then_inc(s["gate_scaled"], 1)
            for k in range(KD):
                dve.wait_ge(s["proj_hi"], k + 1)
                dve.scalar_tensor_tensor(w_lo[:, k, :], z_sb[:, k % 2, :], gain_pre[:, k:k + 1], w_hi[:, k, :],
                                         ALU.mult, ALU.subtract).then_inc(s["proj_lo"], 1)
            base, first = ch.n, True
            for t in (0, 1):
                if t == 1:
                    low_x2(0)
                finish(t, t, False)
                combine(t + 1, 1 - t)
            with dve.Fori(1, TILES // 2 - 1) as i:
                per = (ch.n - base)
                ch.start(i * per + base)
                for u in range(2):
                    low_x2(i * 2 + (u - 1))
                    finish(i * 2 + u, u, True)
                    combine(i * 2 + (u + 1), 1 - u)
                assert ch.n == per, ch.n
            ch.start(base + per * (TILES // 2 - 1))
            low_x2(TILES - 3)
            finish(TILES - 2, 0, True)
            combine(TILES - 1, 1)
            low_x2(TILES - 2)
            finish(TILES - 1, 1, True)
            low_x2(TILES - 1)

        @block.tensor
        def _(pe):
            pe.wait_ge(s["ident_ready"], 1)

            def body(t, par, has_prev, has_next):
                if has_next:
                    pe.wait_ge(s["h2_done"], t + 1)
                    if has_prev:
                        pe.wait_ge(s["x2T_sb"], (t - 1) * 3)
                    for k in range(KD):
                        mm = pe.transpose(TR[:, k * P:(k + 1) * P], h[:, par, k * P:(k + 1) * P], ident[:, :])
                    mm.then_inc(s["hT_ps"], 1)
                    if not is_step(t, 0):
                        pe.wait_ge(s["h3_done"], t)
                    for k in range(PLE // P):
                        mm = pe.transpose(PP[:, k * P:(k + 1) * P], p_sb[:, par, k * P:(k + 1) * P], ident[:, :])
                    mm.then_inc(s["pT_ps"], 1)
                    pe.wait_ge(s["hT_sb"], t + 1)
                    if is_step(t, 0):
                        pe.wait_ge(s["gate_scaled"], KD)
                    else:
                        pe.wait_ge(s["tanh_done"], t)
                    for n in range(2):
                        for k in range(KD):
                            mm = pe.matmul(G[:, n * BANK:(n + 1) * BANK], hT[:, k, :], w_gate[:, k, n * BANK:(n + 1) * BANK],
                                           start=(k == 0), stop=(k == KD - 1))
                    mm.then_inc(s["g_ps"], 1)
                if not is_step(t, 0):
                    pe.wait_ge(s["x2_done"], t)
                    for k in range(KD):
                        mm = pe.transpose(TR[:, k * P:(k + 1) * P], h[:, 1 - par, k * P:(k + 1) * P], ident[:, :])
                    mm.then_inc(s["x2T_ps"], 1)
                if has_next:
                    pe.wait_ge(s["pT_sb"], t + 1)
                    if is_step(t, 0):
                        pe.wait_ge(s["ple_in"], 16 * (PLE // P))
                    for n in range(2):
                        for k in range(PLE // P):
                            mm = pe.matmul(PP[:, n * BANK:(n + 1) * BANK], pT[:, k, :], w_ple[:, k, n * BANK:(n + 1) * BANK],
                                           start=(k == 0), stop=(k == PLE // P - 1))
                    mm.then_inc(s["pp_ps"], 1)
                if not is_step(t, 0):
                    pe.wait_ge(s["x2T_sb"], t * 3)
                    if is_step(t, 1):
                        pe.wait_ge(s["proj_lo"], KD)
                    for n, (lo, hi) in enumerate(Z_CHUNKS):
                        if has_prev or n > 1:
                            pe.wait_ge(s["z_sb"], (t - 1) * len(Z_CHUNKS) + (n - 1))
                        split_product(pe, Z[n % 2][:, 0:hi - lo], lambda k: x2_hi[:, k, :], lambda k: x2_lo[:, k, :],
                                      lambda k: x2_bf[:, k, :], lambda k: w_hi[:, k, lo:hi], lambda k: w_lo[:, k, lo:hi],
                                      range(KD), 0, KD - 1).then_inc(s["z_ps"], 1)

            body(0, 0, False, True)
            body(1, 1, False, True)
            with pe.Fori(1, TILES // 2) as i:
                body(i * 2, 0, True, True)
                body(i * 2 + 1, 1, True, True)
            body(TILES, 0, True, False)


A_HEADS, NOPE, VD = 4, 128, 128
QH = NOPE + ROPE_D
A_SCALE = QH ** -0.5
Z_ATTN = Z_GA
QUADS = TILES // 4
ATTN_LINKS = A_HEADS + 4


def attention_phase(nc, I, S):
    with ExitStack() as ctx:
        sb = lambda name, shape, dt=F32: ctx.enter_context(nc.sbuf_tensor(name, shape, dt))
        pb = lambda name, w: ctx.enter_context(nc.psum_tensor(name, [P, w], F32))
        sem = lambda name: ctx.enter_context(nc.semaphore(name))

        w_uq = sb("w_uq", [P, 2, A_HEADS, QH])
        w_rope = sb("w_rope", [P, 2, 2, A_HEADS, ROPE_D])
        w_ukv = sb("w_ukv", [P, A_HEADS, NOPE + VD])
        gain_q = sb("gain_q", [P, 2])
        gain_kv = sb("gain_kv", [P, 1])
        ident = sb("ident4", [P, P])
        freq_row = sb("freq_row", [P, P])
        freq_col = sb("freq_col", [P, 1])
        cosT = sb("cosT", [P, SEQ])
        sinT = sb("sinT", [P, SEQ])
        k_lo = sb("k_lo", [P, A_HEADS, SEQ], BF16)
        kr4 = (k_lo[:, :, :].rearrange("p h c -> p (h c)").bitcast(F32)
               .rearrange("p (t a b d) -> p t a b d", t=TILES, a=2, b=2))
        ss = sb("ss4", [P, 2, TILES])
        rstd = sb("rstd4", [P, 2, TILES])
        nt = sb("nt4", [P, 2, TILES])
        zqT = sb("zqT", [P, 2, SEQ])
        squares = (zqT[:, :, :].rearrange("p k c -> p (k c)").bitcast(mybir.dt.bfloat16)[:, 0:TILES * Z_KR]
                   .rearrange("p (t c) -> p t c", t=TILES))
        k_hi = sb("k_hi", [P, A_HEADS, SEQ], F32R)
        kr_hi = sb("kr_hi", [P, SEQ], F32R)
        kr_lo = sb("kr_lo", [P, SEQ], BF16)
        v = sb("v4", [P, TILES, A_HEADS * VD])
        z_in = v[:, :, 0:Z_ATTN]
        parts = lambda name, shape: [sb(f"{name}_{n}", shape, t) for n, t in (("hi", F32R), ("lo", F32R), ("bf", BF16))]
        qn = parts("qn", [P, 2, A_HEADS, P])
        qr = parts("qr", [P, 2, A_HEADS // 2, P])
        qr_cos = sb("qr_cos", [P, 2, P])
        qr_sin = sb("qr_sin", [P, 2, P])
        probs = sb("probs", [P, 2, SEQ])
        turns, pos_i = probs[:, 0, :], probs[:, 1, :].bitcast(I32)
        probsT = sb("probsT", [P, 4, BANK])
        zkvT = probsT[:, :, :].rearrange("p j c -> p (j c)")
        top = sb("top", [P, 1])
        ntop = sb("ntop4", [P, 2])
        sums = sb("sums", [P, 2, A_HEADS])
        recip = sb("recip", [P, A_HEADS])
        o_sb = sb("o_sb", [P, 2, A_HEADS * VD])
        kr_cos, kr_sin = o_sb[:, 0, :], o_sb[:, 1, :]

        SC = pb("SC4", 4 * BANK)
        PT = [pb("PT0", BANK), pb("PT1", BANK)]
        Q = pb("Q4", BANK)
        O = pb("O4", BANK)

        names = """weights positions z_in0 z_in1 z_in2 z_in3 ident_ready freq_ready w_ready angles_ready sines cos_ready
            sumsq scaled tq_ps t_sb kr_sb kr_done kT_ps k_hi_ready k_lo_ready v_ps v_sb q_ps q_hi_ready q_nope_sb q_rope_sb sc_ps max_done exp_done
            pt_ps pt_act pt_dve o_ps o_done o_seen o_stored dve_chain pool_chain""".split()
        s = {n: sem("a_" + n) for n in names}
        z_ins = [s[f"z_in{g}"] for g in range(QUADS)]
        ctx.enter_context(nc.allow_non_contiguous_dma(reason="gains, a word per partition"))
        ctx.callback(clear_semaphores, nc, s)
        block = ctx.enter_context(nc.Block())

        attn_t = S["attn"].rearrange("(t p) d -> t p d", p=P)

        def halves(ap):
            return ap.rearrange("p (two f) -> p two f", two=2)

        @block.sync
        def _(sp):
            sp.dma_start(pos_i, I["positions_2"][0].partition_broadcast(P)).then_inc(s["positions"], 16)
            for g in range(QUADS):
                src = S["z"][g * BANK:(g + 1) * BANK, 0:Z_ATTN].rearrange("(t p) d -> p t d", p=P)
                sp.dma_start(z_in[:, 4 * g:4 * g + 4, :], src).then_inc(z_ins[g], 16)
            sp.dma_start(gain_q[:, :], I["q_norm_g_2"][0].rearrange("(k p) -> p k", p=P)).then_inc(s["weights"], 16)
            sp.dma_start(gain_kv[:, :], I["kv_norm_g_2"][0].rearrange("(k p) -> p k", p=P)).then_inc(s["weights"], 16)
            sp.dma_start(w_uq[:, :, :, :], I["w_uq_2"][0].rearrange("(k p) (h n) -> p k h n", p=P, h=A_HEADS)).then_inc(s["weights"], 16)
            sp.dma_start(w_ukv[:, :, :], I["w_ukv_2"][0].rearrange("p (h n) -> p h n", h=A_HEADS)).then_inc(s["weights"], 16)

            def store(t, par):
                sp.wait_ge(s["o_done"], t + 1)
                sp.sem_inc(s["o_seen"], 1)
                if not is_step(t, 0):
                    sp.wait_ge(s["o_stored"], t * 16)
                sp.dma_start(attn_t[bass.ds(t, 1)].squeeze(0), o_sb[:, par, :]).then_inc(s["o_stored"], 16)

            store(0, 0)
            store(1, 1)
            with sp.Fori(1, TILES // 2) as i:
                for u in range(2):
                    store(i * 2 + u, u)
            sp.wait_ge(s["o_stored"], 16 * TILES)

        @block.gpsimd
        def _(pool):
            ch = Chain(pool, s["pool_chain"])
            make_identity(pool, ch, ident[:, :], s["ident_ready"])
            for j in range(ROPE_HALF):
                last = pool.memset(freq_row[:, :].rearrange("p (r f) -> p r f", f=ROPE_HALF)[:, :, j], INV_FREQ[j])
            last.then_inc(s["freq_ready"], 1)

        @block.scalar
        def _(act):
            act.wait_ge(s["angles_ready"], 1)
            act.activation(sinT[:, :], cosT[:, :], ACT.Sin)
            act.activation(cosT[:, :], cosT[:, :], ACT.Sin, scale=0.5).then_inc(s["sines"], 1)
            for t in range(TILES):
                act.wait_ge(z_ins[t // 4], 16)
                act.activation(squares[:, t, 0:Q_RANK], z_in[:, t, 0:Q_RANK], ACT.Square, accum_out=ss[:, 0, t:t + 1])
                act.activation(squares[:, t, Z_KV:Z_KR], z_in[:, t, Z_KV:Z_KR], ACT.Square,
                               accum_out=ss[:, 1, t:t + 1]).then_inc(s["sumsq"], 1)
            for g in range(QUADS):
                cols = slice(g * BANK, (g + 1) * BANK)
                for i, dst in enumerate((zqT[:, 0, cols], zqT[:, 1, cols], zkvT[:, cols])):
                    act.wait_ge(s["tq_ps"], 5 * g + i + 1)
                    act.activation(dst, SC[:, i * BANK:(i + 1) * BANK], ACT.Copy).then_inc(s["t_sb"], 1)
            for j in range(A_HEADS * QUADS):
                h, g = j % A_HEADS, j // A_HEADS
                act.wait_ge(s["kT_ps"], j + 1)
                act.activation(k_hi[:, h, g * BANK:(g + 1) * BANK], PT[j % 2][:, :], ACT.Copy).then_inc(s["k_hi_ready"], 1)

            def copy_q(t, par):
                act.wait_ge(s["q_ps"], t * 2 + 1)
                act.activation(qn[0][:, par, :, :], Q[:, :], ACT.Copy).then_inc(s["q_hi_ready"], 1)
                act.wait_ge(s["q_hi_ready"], t + 1)
                act.activation(qn[2][:, par, :, :], qn[0][:, par, :, :], ACT.Copy).then_inc(s["q_nope_sb"], 1)

            def exps(u, par, h):
                act.wait_ge(s["max_done"], u + 1)
                act.activation(probs[:, h % 2, :], SC[:, :], ACT.Exp, scale=A_SCALE, bias=ntop[:, h % 2:h % 2 + 1],
                               accum_out=sums[:, par, h:h + 1]).then_inc(s["exp_done"], 1)

            def body(t, par, has_next):
                for h in range(A_HEADS):
                    u = t * A_HEADS + h
                    for j in range(2):
                        act.wait_ge(s["pt_ps"], u * 4 + (j + 1))
                        act.activation(probsT[:, j, :], PT[j][:, :], ACT.Copy).then_inc(s["pt_act"], 1)
                    if h < A_HEADS - 1:
                        exps(u + 1, par, h + 1)
                    elif has_next:
                        exps(u + 1, 1 - par, 0)
                    if h == 0 and has_next:
                        copy_q(t + 1, 1 - par)

            copy_q(0, 0)
            exps(0, 0, 0)
            with act.Fori(0, TILES // 2 - 1) as i:
                for w in range(2):
                    body(i * 2 + w, w, True)
            body(TILES - 2, 0, True)
            body(TILES - 1, 1, False)

        @block.vector
        def _(dve):
            ch = Chain(dve, s["dve_chain"])
            dve.wait_ge(s["freq_ready"], 1)
            dve.wait_ge(s["ident_ready"], 1)
            ch.link(dve.tensor_tensor(freq_row[:, :], freq_row[:, :], ident[:, :], ALU.mult))
            ch.link(dve.tensor_reduce(freq_col[:, :], freq_row[:, :], AX, ALU.add))
            dve.wait_ge(s["positions"], 16)
            ch.link(dve.tensor_copy(cosT[:, :], pos_i))
            ch.link(dve.tensor_scalar(cosT[:, :], cosT[:, :], freq_col[:, :], None, ALU.mult))
            reduce_angles(dve, ch, cosT[:, :], turns)
            dve.sem_inc(s["angles_ready"], 1)
            dve.wait_ge(s["weights"], 64)
            for k in range(2):
                ch.link(dve.tensor_scalar(w_uq[:, k, :, :], w_uq[:, k, :, :], gain_q[:, k:k + 1], None, ALU.mult))
            dve.tensor_scalar(w_ukv[:, :, :], w_ukv[:, :, :], gain_kv[:, :], None, ALU.mult)
            half = ROPE_D // 2
            dve.tensor_copy(w_rope[:, 0, :, :, :], w_uq[:, :, :, NOPE:])
            dve.tensor_scalar(w_rope[:, 1, :, :, 0:half], w_uq[:, :, :, NOPE + half:QH], -1.0, None, ALU.mult)
            dve.tensor_copy(w_rope[:, 1, :, :, half:ROPE_D], w_uq[:, :, :, NOPE:NOPE + half]).then_inc(s["w_ready"], 1)
            dve.wait_ge(s["sines"], 1)
            ch.link(dve.tensor_tensor(cosT[:, :], cosT[:, :], cosT[:, :], ALU.mult))
            dve.tensor_scalar(cosT[:, :], cosT[:, :], -2.0, 1.0, ALU.mult, ALU.add).then_inc(s["cos_ready"], 1)
            for g in range(QUADS):
                dve.wait_ge(z_ins[g], 16)
                ts = slice(4 * g, 4 * g + 4)
                kr = z_in[:, ts, Z_KR:Z_ATTN].unsqueeze(2)
                dve.tensor_copy(kr4[:, ts, 0, :, :], kr.to_broadcast([P, 4, 2, ROPE_D]))
                dve.tensor_scalar(kr4[:, ts, 1, :, 0:half], kr[:, :, :, half:].to_broadcast([P, 4, 2, half]), -1.0, None, ALU.mult)
                dve.tensor_copy(kr4[:, ts, 1, :, half:], kr[:, :, :, 0:half].to_broadcast([P, 4, 2, half]))
            dve.wait_ge(s["sumsq"], TILES)
            dve.tensor_scalar(ss[:, 0, :], ss[:, 0, :], 1.0 / Q_RANK, EPS, ALU.mult, ALU.add)
            ch.link(dve.tensor_scalar(ss[:, 1, :], ss[:, 1, :], 1.0 / KV_RANK, EPS, ALU.mult, ALU.add))
            rsqrt(dve, ch, rstd[:, :, :], ss[:, :, :], nt[:, :, :])
            for t in range(TILES):
                dve.tensor_scalar(z_in[:, t, 0:Q_RANK], z_in[:, t, 0:Q_RANK], rstd[:, 0, t:t + 1], None, ALU.mult)
                dve.tensor_scalar(z_in[:, t, Z_KV:Z_KR], z_in[:, t, Z_KV:Z_KR], rstd[:, 1, t:t + 1], None,
                                  ALU.mult).then_inc(s["scaled"], 1)
            for g in range(QUADS):
                cols = slice(g * BANK, (g + 1) * BANK)
                dve.wait_ge(s["tq_ps"], 5 * g + 5)
                dve.tensor_tensor(kr_cos, SC[:, 3 * BANK:4 * BANK], cosT[:, cols], ALU.mult)
                ch.link(dve.tensor_tensor(kr_sin, Q[:, :], sinT[:, cols], ALU.mult))
                dve.sem_inc(s["kr_sb"], 1)
                ch.link(dve.tensor_tensor(kr_cos, kr_cos, kr_sin, ALU.add))
                ch.link(dve.tensor_copy(kr_hi[:, cols], kr_cos))
                ch.link(dve.tensor_tensor(kr_lo[:, cols], kr_cos, kr_hi[:, cols], ALU.subtract))
            dve.sem_inc(s["kr_done"], 1)
            for j in range(TILES):
                h, g = j % A_HEADS, j // A_HEADS
                cols = slice(g * BANK, (g + 1) * BANK)
                dve.wait_ge(s["k_hi_ready"], j + 1)
                dve.tensor_tensor(k_lo[:, h, cols], PT[j % 2][:, :], k_hi[:, h, cols], ALU.subtract).then_inc(s["k_lo_ready"], 1)
                dve.wait_ge(s["v_ps"], j + 1)
                dve.tensor_copy(v[:, j, :], (Q, O)[j % 2][:, :]).then_inc(s["v_sb"], 1)

            def low_q(t, par):
                dve.wait_ge(s["q_hi_ready"], t + 1)
                dve.tensor_tensor(qn[1][:, par, :, :], Q[:, :].rearrange("p (h c) -> p h c", h=A_HEADS), qn[0][:, par, :, :],
                                  ALU.subtract).then_inc(s["q_nope_sb"], 1)

            def rope_q(t, par):
                dve.wait_ge(s["q_ps"], t * 2 + 2)
                q = Q[:, :].rearrange("p (a r c) -> p a r c", a=2, r=2)
                tok = bass.ds(t * P, P)
                dve.tensor_tensor(qr_cos[:, :, :], q[:, :, 0, :], cosT[:, tok].unsqueeze(1).to_broadcast([P, 2, P]), ALU.mult)
                ch.link(dve.tensor_tensor(qr_sin[:, :, :], q[:, :, 1, :], sinT[:, tok].unsqueeze(1).to_broadcast([P, 2, P]), ALU.mult))
                ch.link(dve.tensor_tensor(qr_cos[:, :, :], qr_cos[:, :, :], qr_sin[:, :, :], ALU.add))
                ch.link(dve.tensor_copy(qr[0][:, par, :, :], qr_cos[:, :, :]))
                dve.tensor_copy(qr[2][:, par, :, :], qr_cos[:, :, :])
                dve.tensor_tensor(qr[1][:, par, :, :], qr_cos[:, :, :], qr[0][:, par, :, :], ALU.subtract).then_inc(s["q_rope_sb"], 1)

            def maxima(u, h):
                dve.wait_ge(s["sc_ps"], u + 1)
                ch.link(dve.tensor_reduce(top[:, :], SC[:, :], AX, ALU.max))
                dve.tensor_scalar(ntop[:, h % 2:h % 2 + 1], top[:, :], -A_SCALE, None, ALU.mult).then_inc(s["max_done"], 1)

            def body(t, par, has_prev, has_next):
                for h in range(A_HEADS):
                    u = t * A_HEADS + h
                    if h < A_HEADS - 1 or has_next:
                        maxima(u + 1, (h + 1) % A_HEADS)
                    for j in (2, 3):
                        dve.wait_ge(s["pt_ps"], u * 4 + (j + 1))
                        dve.tensor_copy(probsT[:, j, :], PT[j % 2][:, :]).then_inc(s["pt_dve"], 1)
                    if h == 0 and has_next:
                        low_q(t + 1, 1 - par)
                    if h == 1 and has_next:
                        rope_q(t + 1, 1 - par)
                dve.wait_ge(s["o_ps"], t + 1)
                if has_prev:
                    dve.wait_ge(s["o_stored"], t * 16 - 16)
                ch.link(dve.reciprocal(recip[:, :], sums[:, par, :]))
                o = O[:, :].rearrange("p (h e) -> p h e", h=A_HEADS)
                dve.tensor_tensor(o_sb[:, par, :].rearrange("p (h e) -> p h e", h=A_HEADS), o,
                                  recip[:, :].unsqueeze(2).to_broadcast([P, A_HEADS, VD]), ALU.mult).then_inc(s["o_done"], 1)

            low_q(0, 0)
            rope_q(0, 0)
            maxima(0, 0)
            for t in (0, 1):
                body(t, t, False, True)
            base = ch.n
            with dve.Fori(1, TILES // 2 - 1) as i:
                ch.start(i * (2 * ATTN_LINKS) + (base - 2 * ATTN_LINKS))
                for w in range(2):
                    body(i * 2 + w, w, True, True)
                assert ch.n == 2 * ATTN_LINKS, ch.n
            ch.start(base + (TILES // 2 - 2) * 2 * ATTN_LINKS)
            body(TILES - 2, 0, True, True)
            body(TILES - 1, 1, True, False)

        @block.tensor
        def _(pe):
            pe.wait_ge(s["ident_ready"], 1)
            for g in range(QUADS):
                pe.wait_ge(s["scaled"], 4 * g + 4)
                for i in range(5):
                    if g > 0 and i < 3:
                        pe.wait_ge(s["t_sb"], 3 * (g - 1) + i + 1)
                    if g > 0 and i == 3:
                        pe.wait_ge(s["kr_sb"], g)
                    dst = SC[:, i * BANK:(i + 1) * BANK] if i < 4 else Q[:, :]
                    for j in range(4):
                        t = 4 * g + j
                        src = (z_in[:, t, i * P:(i + 1) * P] if i < 3 else
                               kr4[:, t, i - 3, :, :].rearrange("p two d -> p (two d)"))
                        mm = pe.transpose(dst[:, j * P:(j + 1) * P], src, ident[:, :])
                    mm.then_inc(s["tq_ps"], 1)
            pe.wait_ge(s["w_ready"], 1)
            pe.wait_ge(s["t_sb"], 3 * QUADS)
            pe.wait_ge(s["kr_sb"], QUADS)
            for j in range(A_HEADS * QUADS):
                h, g = j % A_HEADS, j // A_HEADS
                if j > 1:
                    pe.wait_ge(s["k_lo_ready"], j - 1)
                pe.matmul(PT[j % 2][:, :], w_ukv[:, h, 0:NOPE], zkvT[:, g * BANK:(g + 1) * BANK],
                          start=True, stop=True).then_inc(s["kT_ps"], 1)
                if j > 1:
                    pe.wait_ge(s["v_sb"], j - 1)
                pe.matmul((Q, O)[j % 2][:, :], zkvT[:, j * P:(j + 1) * P], w_ukv[:, :, NOPE:],
                          start=True, stop=True).then_inc(s["v_ps"], 1)

            def q_nope(t):
                tok = bass.ds(t * P, P)
                for h in range(A_HEADS):
                    for k in range(2):
                        mm = pe.matmul(Q[:, h * P:(h + 1) * P], w_uq[:, k, h, 0:NOPE], zqT[:, k, tok],
                                       start=(k == 0), stop=(k == 1))
                mm.then_inc(s["q_ps"], 1)

            def q_rope(t):
                tok = bass.ds(t * P, P)
                pe.wait_ge(s["q_nope_sb"], t * 2 + 2)
                for a in range(A_HEADS // 2):
                    for r in range(2):
                        for k in range(2):
                            w = w_rope[:, r, k, 2 * a:2 * a + 2, :].rearrange("p h d -> p (h d)")
                            mm = pe.matmul(Q[:, (2 * a + r) * P:(2 * a + r + 1) * P], w, zqT[:, k, tok],
                                           start=(k == 0), stop=(k == 1))
                mm.then_inc(s["q_ps"], 1)

            def scores(t, par, h, first=False):
                if h == 0:
                    pe.wait_ge(s["q_nope_sb"], t * 2 + 2)
                    pe.wait_ge(s["q_rope_sb"], t + 1)
                if not first:
                    pe.wait_ge(s["exp_done"], t * A_HEADS + h)
                half = slice(ROPE_D * (h % 2), ROPE_D * (h % 2) + ROPE_D)
                for c in range(4):
                    cols = slice(c * BANK, (c + 1) * BANK)
                    for n, keys in ((0, k_hi), (1, k_hi), (2, k_lo)):
                        pe.matmul(SC[:, cols], qn[n][:, par, h, :], keys[:, h, cols], start=(n == 0), stop=False)
                    for n, keys in ((0, kr_hi), (1, kr_hi), (2, kr_lo)):
                        mm = pe.matmul(SC[:, cols], qr[n][half, par, h // 2, :], keys[half, cols], start=False, stop=(n == 2))
                mm.then_inc(s["sc_ps"], 1)

            def body(t, par, has_prev, has_next):
                for h in range(A_HEADS):
                    u = t * A_HEADS + h
                    if h < A_HEADS - 1:
                        scores(t, par, h + 1)
                    elif has_next:
                        scores(t + 1, 1 - par, 0)
                    pe.wait_ge(s["exp_done"], u + 1)

                    def turn(j):
                        for kt in range(4 * j, 4 * j + 4):
                            mm = pe.transpose(PT[j % 2][:, kt % 4 * P:(kt % 4 + 1) * P],
                                              probs[:, h % 2, kt * P:(kt + 1) * P], ident[:, :])
                        mm.then_inc(s["pt_ps"], 1)

                    def apply(j):
                        if j < 2:
                            pe.wait_ge(s["pt_act"], u * 2 + (j + 1))
                        else:
                            pe.wait_ge(s["pt_dve"], u * 2 + (j - 1))
                        if j == 0 and h == 0 and has_prev:
                            pe.wait_ge(s["o_done"], t)
                        for kt in range(4 * j, 4 * j + 4):
                            mm = pe.matmul(O[:, h * VD:(h + 1) * VD], probsT[:, j, kt % 4 * P:(kt % 4 + 1) * P],
                                           v[:, kt, h * VD:(h + 1) * VD], start=(kt == 0), stop=(kt == TILES - 1))
                        return mm

                    turn(0)
                    turn(1)
                    apply(0)
                    turn(2)
                    apply(1)
                    turn(3)
                    apply(2)
                    mm = apply(3)
                    if h == A_HEADS - 1:
                        mm.then_inc(s["o_ps"], 1)
                    if h == 0 and has_next:
                        q_nope(t + 1)
                    if h == 1 and has_next:
                        q_rope(t + 1)

            pe.wait_ge(s["v_sb"], TILES)
            pe.wait_ge(s["k_lo_ready"], A_HEADS * QUADS)
            pe.wait_ge(s["kr_done"], 1)
            pe.wait_ge(s["cos_ready"], 1)
            q_nope(0)
            q_rope(0)
            scores(0, 0, 0, True)
            body(0, 0, False, True)
            body(1, 1, True, True)
            with pe.Fori(1, TILES // 2 - 1) as i:
                for w in range(2):
                    body(i * 2 + w, w, True, True)
            body(TILES - 2, 0, True, True)
            body(TILES - 1, 1, True, False)


GS, GC, NS = 32, 16, 64
QS = GS // 2
DQ = 2 * QS
T = 8
CHUNKS = SEQ // T
CT = CHUNKS // P
SLOTS = T + 1
RUN = 16
RUNS = CHUNKS // RUN


LN2_HI = 0.693145751953125
LN2_LO = math.log(2.0) - LN2_HI


def exact_exp(dve, ch, x, r, t, e):
    one = float(1 << 23)
    ch.link(dve.tensor_scalar(x, x, -110.0, 100.0, ALU.max, ALU.min))
    ch.link(dve.tensor_scalar(t, x, 1.0 / math.log(2.0), ROUND, ALU.mult, ALU.add))
    ch.link(dve.tensor_scalar(t, t, ROUND, None, ALU.subtract))
    ch.link(dve.scalar_tensor_tensor(r, t, -LN2_HI, x, ALU.mult, ALU.add))
    ch.link(dve.scalar_tensor_tensor(r, t, -LN2_LO, r, ALU.mult, ALU.add))
    ch.link(dve.tensor_scalar(x, r, 1.0 / math.factorial(7), None, ALU.mult))
    for k in range(6, 0, -1):
        ch.link(dve.scalar_tensor_tensor(x, x, 1.0 / math.factorial(k), r, ALU.add, ALU.mult))
    ch.link(dve.tensor_scalar(x, x, 1.0, None, ALU.add))
    ch.link(dve.tensor_scalar(e, t, -126.0, 127.0, ALU.max, ALU.min))
    ch.link(dve.tensor_tensor(t, t, e, ALU.subtract))
    for part in (e, t):
        ch.link(dve.tensor_scalar(part.bitcast(I32), part, one, 127.0 * one, ALU.mult, ALU.add))
        ch.link(dve.tensor_tensor(x, x, part, ALU.mult))


def s5_phase(nc, I, S):
    with ExitStack() as ctx:
        sb = lambda name, shape, dt=F32: ctx.enter_context(nc.sbuf_tensor(name, shape, dt))
        sem = lambda name: ctx.enter_context(nc.semaphore(name))

        region_a = sb("region_a", [P, DQ * 2 * P])
        region_b = sb("region_b", [P, DQ * 2 * P])
        X = sb("X", [P, CHUNKS + 1, 2, DQ])
        U = sb("U", [P, GS, CHUNKS])
        G = sb("G", [P, DQ, 2, SLOTS * GC])
        x_flat = X[:, :, :, :].rearrange("p c r q -> p (c r q)")
        u_rows = x_flat[:, 0:CT * T * SSM_W].rearrange("p (a s d) -> p a s d", a=CT, s=T)
        free = CT * T * SSM_W
        tmp_a = [x_flat[:, free + n * 2048:free + (n + 1) * 2048].rearrange("p (q s h) -> p q s h", q=QS, s=T) for n in range(2)]
        free += 2 * 2048
        part_g = QS // 4
        g_size = part_g * SLOTS * GC
        tmp_g = [x_flat[:, free + n * g_size:free + (n + 1) * g_size].rearrange("p (q s h) -> p q s h", q=part_g, s=SLOTS)
                 for n in range(2)]
        free += 2 * g_size
        b_raw, C = [x_flat[:, free + n * 2 * DQ * GC:free + (n + 1) * 2 * DQ * GC].rearrange("p (r q h) -> p r q h", r=2, q=DQ)
                    for n in range(2)]
        A1 = region_a[:, :].rearrange("p (q r m) -> p q r m", q=DQ, r=2)
        toep = region_a[:, :].rearrange("p (d g m) -> p d g m", d=2, g=GS)
        A1T = region_b[:, :].rearrange("p (q r m) -> p q r m", q=DQ, r=2)
        c_nat = region_b[:, 0:16 * P].rearrange("p (n two m) -> p n two m", n=16, two=2)
        W = region_b[0:GC, :].rearrange("p (d g m) -> p d g m", d=2, g=GS)
        y_rows = region_b[:, :].rearrange("p (a s d) -> p a s d", a=CT, s=T)
        u_perm = region_a[:, T * SSM_W:2 * T * SSM_W].rearrange("p (g s h) -> p g s h", g=GS, s=T)
        raw = region_b[0:DQ, 16 * P:19 * P].rearrange("p (n m) -> p n m", n=3)
        logdt = sb("logdt", [DQ, 2])
        per_state = sb("per_state", [P, 2 * QS * RUNS])
        cut = lambda at, n: per_state[:, at * DQ:(at + n) * DQ].rearrange("p (n q) -> p n q", n=n)
        par_, fac = cut(10, 3), cut(13, 2)
        lre, dt, mag, ang, turns, sin, cos, den, num, t5 = [cut(n, 1)[:, 0, :] for n in range(10)]
        pw = sb("pw", [P, SLOTS, 2, DQ])
        pw_t = [region_a[:, n * 8 * DQ:(n + 1) * 8 * DQ].rearrange("p (n r q) -> p n r q", n=4, r=2) for n in range(2)]
        b_bar = sb("b_bar", [P, 2, DQ, GC])
        b_t = [region_a[:, (1 + n) * DQ * GC:(2 + n) * DQ * GC].rearrange("p (q h) -> p q h", q=DQ) for n in range(2)]
        skip = sb("skip", [P, GS])
        ident = sb("ident5", [P, P])
        lr2 = sb("lr2", [P, 2, DQ])
        li2 = sb("li2", [P, 2, DQ])
        st = [sb(f"st{n}", [P, 2, DQ]) for n in range(2)]
        run_f = [sb(f"run_f{n}", [P, 2, DQ]) for n in range(2)]
        skip_m = toep[:, 1, 0:8, :]

        PS = [ctx.enter_context(nc.psum_tensor(f"PS{n}", [P, BANK], F32)) for n in range(8)]

        names = """params b_in c_in u_in skip_in ident_ready raw_ps raw_sb ang_ready sines c_ps C_ready u_ps
            u_sb u_by_group powers_ready b_ready G_ready A1_ready a_ps a_sb s_ps s_act s_dve scan_done w_ps w_sb toep_zero toep_in M_ready
            y_ps y_act y_dve y_stored dve_chain pool_chain raw_ready""".split()
        s = {n: sem("s_" + n) for n in names}
        ctx.enter_context(nc.allow_non_contiguous_dma(reason="small parameter tables"))
        ctx.callback(clear_semaphores, nc, s)
        block = ctx.enter_context(nc.Block())

        def states_in(eng, q):
            src = PS[q % 4][:, :].rearrange("p (r c) -> p r c", r=2)
            dst = X[:, 1:CHUNKS + 1, :, q] if q < QS else X[:, 0:CHUNKS, :, q]
            dst = dst.rearrange("p c r -> p r c")
            if q % 2 == 0:
                return eng.activation(dst, src, ACT.Copy)
            return eng.tensor_copy(dst, src)

        def outputs(eng, a, b, g2):
            bank = PS[2 * ((4 * a + b) % 2) + g2 + 2]
            src = bank[:, :].rearrange("c (j s h) -> c j s h", j=4, s=T)
            dst = y_rows[:, a, :, :].rearrange("c s (b j g h) -> c b g j s h", b=4, j=4, g=2)[:, b, g2]
            if g2 == 0:
                return eng.activation(dst, src, ACT.Copy)
            return eng.tensor_copy(dst, src)

        G_PARTS = [(d, part) for d in range(2) for part in range(4)]
        POOL_G = 5

        def out_tables(eng, ch, d, part, tmp):
            qs = slice(d * QS + part * part_g, d * QS + (part + 1) * part_g)
            shape = [P, part_g, SLOTS, GC]
            order = slice(None, None, -1 if d else 1)
            p = [pw[:, order, r, qs].rearrange("p s q -> p q s").unsqueeze(3).to_broadcast(shape) for r in range(2)]
            c = [C[:, r, qs, :].unsqueeze(2).to_broadcast(shape) for r in range(2)]
            out = [G[:, qs, r, :].rearrange("p q (s h) -> p q s h", h=GC) for r in range(2)]
            eng.tensor_tensor(tmp[0], c[0], p[0], ALU.mult)
            ch.link(eng.tensor_tensor(tmp[1], c[1], p[1], ALU.mult))
            ch.link(eng.tensor_tensor(out[0], tmp[0], tmp[1], ALU.subtract))
            eng.tensor_tensor(tmp[0], c[0], p[1], ALU.mult)
            ch.link(eng.tensor_tensor(tmp[1], c[1], p[0], ALU.mult))
            ch.link(eng.tensor_tensor(tmp[0], tmp[0], tmp[1], ALU.add))
            ch.link(eng.tensor_scalar(out[1], tmp[0], -1.0, None, ALU.mult))

        @block.sync
        def _(sp):
            for n, name in enumerate(("s5_lam_re_2", "s5_lam_im_2")):
                sp.dma_start(raw[:, n, :], I[name][0].rearrange("d (q g) p -> (d q) (g p)", g=2)).then_inc(s["params"], 16)
            sp.dma_start(logdt[:, :], I["s5_log_dt_2"][0].rearrange("d (q g) -> (d q) g", g=2)).then_inc(s["params"], 16)
            for r, name in enumerate(("s5_c_re_2", "s5_c_im_2")):
                for d in range(2):
                    src = I[name][0, d].rearrange("g h p -> (g h) p").rearrange("(b r) p -> r b p", r=P)
                    n = (r * 2 + d) * 4
                    for dup in range(2):
                        sp.dma_start(c_nat[:, n:n + 4, dup, :], src).then_inc(s["c_in"], 16)
            for r, name in enumerate(("s5_b_re_2", "s5_b_im_2")):
                for d in range(2):
                    src = I[name][0, d].rearrange("(q g) p h -> q (g p) h", g=2).rearrange("q r h -> r q h")
                    sp.dma_start(b_raw[:, r, d * QS:(d + 1) * QS, :], src).then_inc(s["b_in"], 16)
            u_t = S["z"].rearrange("(a c s) d -> a c s d", a=CT, s=T)
            for a in range(CT):
                sp.dma_start(u_rows[:, a, :, :], u_t[a, :, :, Z_U:Z_GS]).then_inc(s["u_in"], 16)
            for k in range(T):
                src = I["s5_d_2"][0].rearrange("(g h) -> h g", h=GC)
                sp.dma_start(skip[k * GC:(k + 1) * GC, :], src).then_inc(s["skip_in"], 16)
            sp.wait_ge(s["w_sb"], 16)
            sp.wait_ge(s["toep_zero"], 1)
            for k in range(T):
                rows = slice(k * GC, (k + 1) * GC)
                sp.dma_start(toep[rows, 0, :, k * GC:], W[:, 0, :, 0:(T - k) * GC]).then_inc(s["toep_in"], 16)
                sp.dma_start(toep[rows, 1, :, 0:(k + 1) * GC], W[:, 1, :, (T - 1 - k) * GC:]).then_inc(s["toep_in"], 16)
            y_t = S["ssm"].rearrange("(a c s) d -> a c s d", a=CT, s=T)
            for a in range(CT):
                sp.wait_ge(s["y_act"], 4 * (a + 1))
                sp.wait_ge(s["y_dve"], 4 * (a + 1))
                sp.dma_start(y_t[a], y_rows[:, a, :, :]).then_inc(s["y_stored"], 16)
            sp.wait_ge(s["y_stored"], 16 * CT)

        @block.gpsimd
        def _(pool):
            ch = Chain(pool, s["pool_chain"])
            make_identity(pool, ch, ident[:, :], s["ident_ready"])
            pool.wait_ge(s["powers_ready"], 1)
            pool.wait_ge(s["C_ready"], 1)
            for d, part in G_PARTS[0:POOL_G]:
                out_tables(pool, ch, d, part, tmp_g)
            pool.sem_inc(s["G_ready"], 1)
            pool.wait_ge(s["a_ps"], 16)
            ch.link(pool.memset(region_a[:, :], 0.0))
            pool.sem_inc(s["toep_zero"], 1)
            pool.wait_ge(s["skip_in"], 16 * T)
            pool.wait_ge(s["toep_in"], 16 * 2 * T)
            ch.link(pool.tensor_tensor(toep[:, 0, :, :], toep[:, 0, :, :], toep[:, 1, :, :], ALU.add))
            for b in range(GS // 8):
                gs = slice(8 * b, 8 * b + 8)
                ch.link(pool.tensor_tensor(skip_m, ident[:, :].unsqueeze(1).to_broadcast([P, 8, P]),
                                           skip[:, gs].unsqueeze(2).to_broadcast([P, 8, P]), ALU.mult))
                ch.link(pool.tensor_tensor(toep[:, 0, gs, :], toep[:, 0, gs, :], skip_m, ALU.add))
            pool.sem_inc(s["M_ready"], 1)

        @block.scalar
        def _(act):
            act.wait_ge(s["raw_ps"], 1)
            act.activation(par_[:, :, :], PS[0][:, 0:3 * DQ], ACT.Copy).then_inc(s["raw_sb"], 1)
            act.wait_ge(s["ang_ready"], 1)
            act.activation(sin, ang, ACT.Sin)
            act.activation(cos, ang, ACT.Sin, scale=0.5).then_inc(s["sines"], 1)
            for n in range(4):
                act.wait_ge(s["c_ps"], n + 1)
                r, d = n // 2, n % 2
                src = PS[1 + n][:, :].rearrange("p (q g h) -> p q g h", g=2, h=GC)
                for g2 in range(2):
                    hp = slice(NS * g2, NS * g2 + NS)
                    last = act.activation(C[hp, r, d * QS:(d + 1) * QS, :], src[hp, :, g2, :], ACT.Copy)
            last.then_inc(s["C_ready"], 1)
            for n in range(16):
                a, b = n // 8, n % 8
                if b == 0:
                    act.wait_ge(s["u_in"], 16 * CT)
                    if a > 0:
                        act.wait_ge(s["u_ps"], n)
                    act.activation(u_perm, u_rows[:, a, :, :].rearrange("p s (g h) -> p g s h", h=GC),
                                   ACT.Copy).then_inc(s["u_by_group"], 1)
                act.wait_ge(s["u_ps"], n + 1)
                act.activation(U[:, 4 * b:4 * b + 4, a * P:(a + 1) * P],
                               PS[5 + n % 3][:, :].rearrange("p (g c) -> p g c", g=4), ACT.Copy).then_inc(s["u_sb"], 1)
            for n in range(16):
                act.wait_ge(s["a_ps"], n + 1)
                act.activation(A1T[:, 2 * n:2 * n + 2, :, :], PS[1 + n % 4][:, :], ACT.Copy).then_inc(s["a_sb"], 1)
            act.wait_ge(s["G_ready"], 2)
            for q in range(0, DQ, 2):
                act.wait_ge(s["s_ps"], q + 1)
                states_in(act, q).then_inc(s["s_act"], 1)
            for n in range(16):
                act.wait_ge(s["w_ps"], n + 1)
                d, first = n // 8, n % 8 // 2 * 8 + n % 2
                act.activation(W[:, d, first:first + 7:2, :], PS[n % 2][0:GC, :].rearrange("p (g m) -> p g m", g=4),
                               ACT.Copy).then_inc(s["w_sb"], 1)
            for a in range(CT):
                for b in range(4):
                    act.wait_ge(s["y_ps"], 2 * (4 * a + b) + 1)
                    outputs(act, a, b, 0).then_inc(s["y_act"], 1)

        @block.vector
        def _(dve):
            ch = Chain(dve, s["dve_chain"])
            tt = lambda out, a, b, op: dve.tensor_tensor(out, a, b, op)

            dve.wait_ge(s["params"], 48)
            dve.tensor_copy(raw[:, 2, :].rearrange("q (g p) -> q g p", g=2),
                            logdt[:, :].unsqueeze(2).to_broadcast([DQ, 2, NS])).then_inc(s["raw_ready"], 1)
            im = par_[:, 1, :]
            dve.wait_ge(s["raw_sb"], 1)
            dve.tensor_scalar(lre, par_[:, 0, :], -1e-4, None, ALU.min)
            ch.link(dve.tensor_copy(dt, par_[:, 2, :]))
            exact_exp(dve, ch, dt, num, t5, den)
            tt(mag, lre, dt, ALU.mult)
            ch.link(tt(ang, im, dt, ALU.mult))
            reduce_angles(dve, ch, ang, turns)
            dve.sem_inc(s["ang_ready"], 1)
            exact_exp(dve, ch, mag, num, t5, den)
            tt(den, lre, lre, ALU.mult)
            ch.link(tt(t5, im, im, ALU.mult))
            ch.link(tt(den, den, t5, ALU.add))
            ch.link(dve.reciprocal(den, den))
            dve.wait_ge(s["sines"], 1)
            ch.link(tt(cos, cos, cos, ALU.mult))
            ch.link(dve.tensor_scalar(cos, cos, -2.0, 1.0, ALU.mult, ALU.add))
            dve.memset(pw[:, 0, 0, :], 1.0)
            dve.memset(pw[:, 0, 1, :], 0.0)
            tt(pw[:, 1, 0, :], mag, cos, ALU.mult)
            ch.link(tt(pw[:, 1, 1, :], mag, sin, ALU.mult))
            ch.link(dve.tensor_scalar(num, pw[:, 1, 0, :], -1.0, None, ALU.add))
            tt(fac[:, 0, :], num, lre, ALU.mult)
            ch.link(tt(t5, pw[:, 1, 1, :], im, ALU.mult))
            ch.link(tt(fac[:, 0, :], fac[:, 0, :], t5, ALU.add))
            tt(fac[:, 1, :], pw[:, 1, 1, :], lre, ALU.mult)
            ch.link(tt(t5, num, im, ALU.mult))
            ch.link(tt(fac[:, 1, :], fac[:, 1, :], t5, ALU.subtract))
            ch.link(tt(fac[:, :, :], fac[:, :, :], den.unsqueeze(1).to_broadcast([P, 2, DQ]), ALU.mult))
            for n in (1, 2, 4):
                shape = [P, n, 2, DQ]
                a = pw[:, 1:1 + n, :, :]
                by = [pw[:, n, r, :].unsqueeze(1).unsqueeze(1).to_broadcast(shape) for r in range(2)]
                tt(pw_t[0][:, 0:n, :, :], a, by[0], ALU.mult)
                ch.link(tt(pw_t[1][:, 0:n, :, :], a[:, :, ::-1, :], by[1], ALU.mult))
                out = pw[:, 1 + n:1 + 2 * n, :, :]
                tt(out[:, :, 0, :], pw_t[0][:, 0:n, 0, :], pw_t[1][:, 0:n, 0, :], ALU.subtract)
                ch.link(tt(out[:, :, 1, :], pw_t[0][:, 0:n, 1, :], pw_t[1][:, 0:n, 1, :], ALU.add))
            dve.sem_inc(s["powers_ready"], 1)
            for r in range(2):
                dve.tensor_copy(lr2[:, r, :], pw[:, T, 0, :])
            dve.tensor_copy(li2[:, 0, :], pw[:, T, 1, :])
            dve.tensor_scalar(li2[:, 1, :], pw[:, T, 1, :], -1.0, None, ALU.mult)
            dve.wait_ge(s["b_in"], 64)
            f = [fac[:, r, :].unsqueeze(2).to_broadcast([P, DQ, GC]) for r in range(2)]
            for r, op in ((0, ALU.subtract), (1, ALU.add)):
                tt(b_t[0][:, :, :], f[0], b_raw[:, r, :, :], ALU.mult)
                ch.link(tt(b_t[1][:, :, :], f[1], b_raw[:, 1 - r, :, :], ALU.mult))
                ch.link(tt(b_bar[:, r, :, :], b_t[0][:, :, :], b_t[1][:, :, :], op))
            dve.sem_inc(s["b_ready"], 1)
            shape = [P, QS, T, GC]
            for d in range(2):
                if d == 1:
                    dve.wait_ge(s["u_ps"], 16)
                qs = slice(d * QS, (d + 1) * QS)
                powers = pw[:, 0:T, :, qs] if d else pw[:, T - 1::-1, :, qs]
                p = [powers[:, :, r, :].rearrange("p s q -> p q s").unsqueeze(3).to_broadcast(shape) for r in range(2)]
                b = [b_bar[:, r, qs, :].unsqueeze(2).to_broadcast(shape) for r in range(2)]
                for r, op in ((0, ALU.subtract), (1, ALU.add)):
                    tt(tmp_a[0], b[r], p[0], ALU.mult)
                    ch.link(tt(tmp_a[1], b[1 - r], p[1], ALU.mult))
                    ch.link(tt(A1[:, qs, r, :].rearrange("p q (s h) -> p q s h", h=GC), tmp_a[0], tmp_a[1], op))
                dve.sem_inc(s["A1_ready"], 1)
            dve.wait_ge(s["C_ready"], 1)
            rest = [t[:, :, :, :].rearrange("p q s h -> p (q s h)")[:, 0:g_size].rearrange("p (q s h) -> p q s h", q=part_g, s=SLOTS)
                    for t in tmp_a]
            for d, part in G_PARTS[POOL_G:]:
                out_tables(dve, ch, d, part, rest)
            dve.sem_inc(s["G_ready"], 1)
            dve.wait_ge(s["G_ready"], 2)
            dve.memset(X[:, 0, :, 0:QS], 0.0)
            dve.memset(X[:, CHUNKS, :, QS:], 0.0)
            for q in range(1, DQ, 2):
                dve.wait_ge(s["s_ps"], q + 1)
                states_in(dve, q).then_inc(s["s_dve"], 1)
            dve.wait_ge(s["s_dve"], DQ // 2)
            dve.wait_ge(s["s_act"], DQ // 2)

            fwd, bwd = slice(0, QS), slice(QS, DQ)
            views = (X[:, 1:CHUNKS + 1, :, fwd].rearrange("p (n i) r q -> p n i r q", i=RUN),
                     X[:, 0:CHUNKS, :, bwd].rearrange("p (n i) r q -> p n i r q", i=RUN))
            by_run = lambda ap, runs: ap[:, 0:runs * 2 * QS].rearrange("p (n r q) -> p n r q", n=runs, r=2)
            bank = lambda n, runs: by_run(PS[n], runs)
            other = lambda d, runs: by_run((pw[:, :, :, :].rearrange("p s r q -> p (s r q)"), per_state)[d], runs)

            def at(side, i):
                return views[side][:, :, bass.ds(i if side == 0 else i * -1 + (RUN - 1), 1), :, :].squeeze(2)

            def times(factor, side, runs):
                return factor[:, :, (fwd, bwd)[side]].unsqueeze(1).to_broadcast([P, runs, 2, QS])

            def advance(old, new, runs, extra):
                for d in range(2):
                    tt(bank(2 + d, runs), old[d], times(lr2, d, runs), ALU.mult)
                for d in range(2):
                    last = tt(other(d, runs), old[d], times(li2, d, runs), ALU.mult)
                ch.link(last)
                if extra is not None:
                    for d in range(2):
                        last = tt(bank(2 + d, runs), bank(2 + d, runs), extra[d], ALU.add)
                    ch.link(last)
                for d in range(2):
                    last = tt(new[d], bank(2 + d, runs), other(d, runs)[:, :, ::-1, :], ALU.add)
                ch.link(last)

            base = ch.base + ch.n
            with dve.Fori(1, RUN) as i:
                ch.start(i * 3 + (base - 3))
                old, new = [[at(d, i + n) for d in range(2)] for n in (-1, 0)]
                advance(old, new, RUNS, new)
            ch.start(base + (RUN - 1) * 3)
            run_lr, run_li = [region_n[:, :, :] for region_n in run_f]
            dve.tensor_copy(run_lr, lr2[:, :, :])
            ch.link(dve.tensor_copy(run_li, li2[:, :, :]))
            for n in range(RUN.bit_length() - 1):
                ch.link(tt(st[0][:, :, :], run_lr, run_lr, ALU.mult))
                ch.link(tt(st[1][:, :, :], run_li, run_li, ALU.mult))
                ch.link(tt(run_li, run_li, run_lr, ALU.mult))
                ch.link(dve.tensor_scalar(run_li, run_li, 2.0, None, ALU.mult))
                ch.link(tt(run_lr, st[0][:, :, :], st[1][:, :, :], ALU.subtract))

            base = ch.base + ch.n
            with dve.Fori(1, RUNS) as n:
                ch.start(n * 3 + (base - 3))
                ends = [[views[0][:, bass.ds(n + m, 1), RUN - 1, :, :].squeeze(1) for m in (-1, 0)],
                        [views[1][:, bass.ds(n * -1 + (RUNS - 1 - m), 1), 0, :, :].squeeze(1) for m in (-1, 0)]]
                for d in range(2):
                    tt(st[0][:, :, (fwd, bwd)[d]], ends[d][0], run_lr[:, :, (fwd, bwd)[d]], ALU.mult)
                for d in range(2):
                    last = tt(st[1][:, :, (fwd, bwd)[d]], ends[d][0], run_li[:, :, (fwd, bwd)[d]], ALU.mult)
                ch.link(last)
                for d in range(2):
                    last = tt(st[0][:, :, (fwd, bwd)[d]], st[0][:, :, (fwd, bwd)[d]], ends[d][1], ALU.add)
                ch.link(last)
                for d in range(2):
                    last = tt(ends[d][1], st[0][:, :, (fwd, bwd)[d]], st[1][:, ::-1, (fwd, bwd)[d]], ALU.add)
                ch.link(last)
            ch.start(base + (RUNS - 1) * 3)
            carry = [bank(4 + d, RUNS - 1) for d in range(2)]
            tt_in = (views[0][:, 0:RUNS - 1, RUN - 1, :, :], views[1][:, 1:RUNS, 0, :, :])
            for d in range(2):
                last = dve.tensor_copy(carry[d], tt_in[d])
            ch.link(last)
            base = ch.base + ch.n
            with dve.Fori(0, RUN - 1) as i:
                ch.start(i * 3 + base)
                advance(carry, carry, RUNS - 1, None)
                for d in range(2):
                    runs = at(d, i)[:, 1:RUNS] if d == 0 else at(d, i)[:, 0:RUNS - 1]
                    last = tt(runs, runs, carry[d], ALU.add)
                ch.link(last)
            dve.sem_inc(s["scan_done"], 1)
            for a in range(CT):
                for b in range(4):
                    dve.wait_ge(s["y_ps"], 2 * (4 * a + b) + 2)
                    outputs(dve, a, b, 1).then_inc(s["y_dve"], 1)

        @block.tensor
        def _(pe):
            pe.wait_ge(s["ident_ready"], 1)
            pe.wait_ge(s["raw_ready"], 1)
            for n in range(3):
                mm = pe.transpose(PS[0][:, n * DQ:(n + 1) * DQ], raw[:, n, :], ident[0:DQ, 0:DQ])
            mm.then_inc(s["raw_ps"], 1)
            pe.wait_ge(s["c_in"], 16 * 8)
            for n in range(16):
                mm = pe.transpose(PS[1 + n // 4][:, n % 4 * P:(n % 4 + 1) * P],
                                  c_nat[:, n, :, :].rearrange("p two m -> p (two m)"), ident[:, :])
                if n % 4 == 3:
                    mm.then_inc(s["c_ps"], 1)
            for n in range(16):
                a, b = n // 8, n % 8
                if n > 2:
                    pe.wait_ge(s["u_sb"], n - 2)
                pe.wait_ge(s["u_by_group"], a + 1)
                for g in range(4):
                    src = u_perm[:, 4 * b + g, :, :].rearrange("p s h -> p (s h)")
                    mm = pe.transpose(PS[5 + n % 3][:, g * P:(g + 1) * P], src, ident[:, :])
                mm.then_inc(s["u_ps"], 1)
            pe.wait_ge(s["C_ready"], 1)
            for n in range(16):
                pe.wait_ge(s["A1_ready"], n // 8 + 1)
                if n > 3:
                    pe.wait_ge(s["a_sb"], n - 3)
                for m in range(4):
                    mm = pe.transpose(PS[1 + n % 4][:, m * P:(m + 1) * P], A1[:, 2 * n + m // 2, m % 2, :], ident[:, :])
                mm.then_inc(s["a_ps"], 1)
            pe.wait_ge(s["a_sb"], 16)
            pe.wait_ge(s["u_sb"], 16)
            for q in range(DQ):
                if q > 3:
                    if q % 2 == 0:
                        pe.wait_ge(s["s_act"], q // 2 - 1)
                    else:
                        pe.wait_ge(s["s_dve"], q // 2 - 1)
                for g2 in range(2):
                    for r in range(2):
                        mm = pe.matmul(PS[q % 4][NS * g2:NS * g2 + NS, r * CHUNKS:(r + 1) * CHUNKS],
                                       A1T[:, q, r, NS * g2:NS * g2 + NS], U[:, 2 * (q % QS) + g2, :], start=True, stop=True)
                mm.then_inc(s["s_ps"], 1)
            pe.wait_ge(s["s_act"], DQ // 2)
            pe.wait_ge(s["s_dve"], DQ // 2)
            for n in range(16):
                d, g2 = n // 8, n % 2
                hp = slice(NS * g2, NS * g2 + NS)
                if n > 1:
                    pe.wait_ge(s["w_sb"], n - 1)
                for g in range(4):
                    q = d * QS + n % 8 // 2 * 4 + g
                    for r in range(2):
                        mm = pe.matmul(PS[n % 2][0:GC, g * P:(g + 1) * P], b_bar[hp, r, q, :],
                                       G[hp, q, r, d * GC:(d + T) * GC], start=(r == 0), stop=(r == 1))
                mm.then_inc(s["w_ps"], 1)
            pe.wait_ge(s["M_ready"], 1)
            pe.wait_ge(s["scan_done"], 1)
            for a in range(CT):
                for b in range(4):
                    n = 4 * a + b
                    if n > 1:
                        pe.wait_ge(s["y_act"], n - 1)
                        pe.wait_ge(s["y_dve"], n - 1)
                    mms = [None, None]
                    for j in range(4):
                        for g2 in range(2):
                            g = 8 * b + 2 * j + g2
                            hp = slice(NS * g2, NS * g2 + NS)
                            out = PS[2 * (n % 2) + g2 + 2][:, j * P:(j + 1) * P]
                            pe.matmul(out, U[:, g, a * P:(a + 1) * P], toep[:, 0, g, :], start=True, stop=False)
                            for d in range(2):
                                q = d * QS + g // 2
                                steps = slice(a * P + d, a * P + d + P)
                                for r in range(2):
                                    mms[g2] = pe.matmul(out, X[hp, steps, r, q], G[hp, q, r, (1 - d) * GC:(1 - d + T) * GC],
                                                        start=False, stop=(d == 1 and r == 1))
                    mms[0].then_inc(s["y_ps"], 1)
                    mms[1].then_inc(s["y_ps"], 1)


HALVINGS = (0.5, 0.125)
GELU_A, GELU_S = 0.044715, math.sqrt(2.0 / math.pi)


def output_phase(nc, I, S):
    with ExitStack() as ctx:
        sb = lambda name, shape, dt=F32: ctx.enter_context(nc.sbuf_tensor(name, shape, dt))
        pb = lambda name, w: ctx.enter_context(nc.psum_tensor(name, [P, w], F32))
        sem = lambda name: ctx.enter_context(nc.semaphore(name))

        KS = SSM_W // P
        w_in = sb("w_6", [P, KS * SSM_W + KD * D])
        w_hi = sb("w_6_hi", [P, KS * SSM_W + KD * D], F32R)
        w_lo = sb("w_6_lo", [P, KS * SSM_W + KD * D], BF16)
        glu = lambda w: w[:, 0:KS * SSM_W].rearrange("p (k d) -> p k d", k=KS)
        outw = lambda w: w[:, KS * SSM_W:].rearrange("p (k d) -> p k d", k=KD)
        gain_out = sb("gain_out6", [P, KD])
        gain_post = sb("gain_post", [P, D])
        b_glu = sb("b_glu", [P, SSM_W])
        ident = sb("ident6", [P, P])
        y_in = sb("y_in", [P, 2, SSM_W])
        g_in = sb("g_in", [P, 2, 2, SSM_W])
        a_in = sb("a_in", [P, 2, ATTN_W])
        x2 = sb("x2_6", [P, 2, D])
        poly = sb("poly", [P, SSM_W])
        tanh_y = sb("tanh_y", [P, SSM_W])
        gelu = sb("gelu", [P, SSM_W])
        g_hi, g_lo, g_bf = (sb(n, [P, KS, P], t) for n, t in (("g_hi", F32R), ("g_lo", F32R), ("g_bf", BF16)))
        pre = sb("pre6", [P, SSM_W])
        tanh_p = sb("tanh_p", [P, SSM_W])
        ssm = sb("ssm6", [P, SSM_W])
        tanh_g = sb("tanh_g6", [P, 2, SSM_W])
        silu = sb("silu", [P, 2, 2, SSM_W])
        sq_a, sq_s, sq_o = (sb(n, [P, w], mybir.dt.bfloat16) for n, w in
                            (("sq_a", ATTN_W), ("sq_s", SSM_W), ("sq_o", D)))
        ss = sb("ss6", [P, 2, 2])
        rstd = sb("rstd6", [P, 2])
        nt = sb("nt6", [P, 2])
        ss_o, rstd_o, nt_o = (sb(n, [P, 1]) for n in ("ss_o", "rstd_o", "nt_o"))
        cat = sb("cat", [P, 2, SSM_W])
        c_hi, c_lo, c_bf = (sb(n, [P, KD, P], t) for n, t in (("c_hi", F32R), ("c_lo", F32R), ("c_bf", BF16)))
        o_n = sb("o_n", [P, D])
        out = sb("out_sb", [P, 2, D])

        TG = pb("TG", BANK)
        GL = pb("GL", BANK)
        TC = pb("TC", 2 * BANK)
        OUT = [pb("OUT0", 2 * BANK), pb("OUT1", 2 * BANK)]

        names = """gains glu_in out_in ident_ready w_high w_low in_loaded x_loaded poly_ready tanh_y_ready gelu_ready gT_ps g_hi_ready gT_sb gl_ps
            pre_ready tanh_p_ready ssm_ready sumsq sumsq_a tanh_g_ready silu_ready cat_ready cT_ps c_hi_ready cT_sb o_ps sumsq_o out_ready
            out_seen out_stored dve_chain pool_chain""".split()
        s = {n: sem("o_" + n) for n in names}
        ctx.enter_context(nc.allow_non_contiguous_dma(reason="gains, a word per partition"))
        block = ctx.enter_context(nc.Block())

        tiles = lambda ap: ap.rearrange("(t p) d -> t p d", p=P)
        z_t, a_t, y_t, x_t, out_t = tiles(S["z"]), tiles(S["attn"]), tiles(S["ssm"]), tiles(S["x2"]), tiles(S["out"])
        per_in = 64

        @block.sync
        def _(sp):
            def load(t, par):
                tile = bass.ds(t, 1)
                sp.dma_start(y_in[:, par, :], y_t[tile].squeeze(0)).then_inc(s["in_loaded"], 16)
                sp.dma_start(a_in[:, par, :], a_t[tile].squeeze(0)).then_inc(s["in_loaded"], 16)
                sp.dma_start(g_in[:, par, 0, :], z_t[tile, :, Z_GA:Z_U].squeeze(0)).then_inc(s["in_loaded"], 16)
                sp.dma_start(g_in[:, par, 1, :], z_t[tile, :, Z_GS:Z_COLS].squeeze(0)).then_inc(s["in_loaded"], 16)

            def load_x(t, par):
                sp.dma_start(x2[:, par, :], x_t[bass.ds(t, 1)].squeeze(0)).then_inc(s["x_loaded"], 16)

            def store(t, par):
                sp.wait_ge(s["out_ready"], t + 1)
                sp.sem_inc(s["out_seen"], 1)
                if not is_step(t, 0):
                    sp.wait_ge(s["out_stored"], t * 16)
                sp.dma_start(out_t[bass.ds(t, 1)].squeeze(0), out[:, par, :]).then_inc(s["out_stored"], 16)

            def body(t, par):
                sp.wait_ge(s["in_loaded"], t * per_in + 2 * per_in)
                sp.sem_inc(s["out_seen"], 1)
                sp.wait_ge(s["cat_ready"], t + 1)
                load(t + 2, par)
                if not is_step(t, 0):
                    store(t - 1, 1 - par)
                    sp.wait_ge(s["x_loaded"], t * 16 + 16)
                    load_x(t + 1, 1 - par)

            load(0, 0)
            load_x(0, 0)
            sp.dma_start(b_glu[:, :], I["b_glu_2"][0].partition_broadcast(P)).then_inc(s["gains"], 16)
            sp.dma_start(gain_post[:, :], I["post_norm_g_2"][0].partition_broadcast(P)).then_inc(s["gains"], 16)
            sp.dma_start(gain_out[:, 0:4], I["attn_out_g_2"][0].rearrange("(k p) -> p k", p=P)).then_inc(s["gains"], 16)
            sp.dma_start(gain_out[:, 4:8], I["ssm_out_g_2"][0].rearrange("(k p) -> p k", p=P)).then_inc(s["gains"], 16)
            for k in range(KS):
                sp.dma_start(glu(w_in)[:, k, :], I["w_glu_2"][0, k * P:(k + 1) * P, :]).then_inc(s["glu_in"], 16)
            for k in range(KD):
                sp.dma_start(outw(w_in)[:, k, :], I["w_out_2"][0, k * P:(k + 1) * P, :]).then_inc(s["out_in"], 16)
            sp.wait_ge(s["in_loaded"], per_in)
            load(1, 1)
            sp.wait_ge(s["x_loaded"], 16)
            load_x(1, 1)
            for t in (0, 1):
                body(t, t)
            with sp.Fori(1, TILES // 2 - 1) as i:
                for u in range(2):
                    body(i * 2 + u, u)
            store(TILES - 3, 1)
            sp.wait_ge(s["x_loaded"], 16 * (TILES - 1))
            load_x(TILES - 1, 1)
            store(TILES - 2, 0)
            store(TILES - 1, 1)
            sp.wait_ge(s["out_stored"], 16 * TILES)

        @block.gpsimd
        def _(pool):
            make_identity(pool, Chain(pool, s["pool_chain"]), ident[:, :], s["ident_ready"])

        @block.scalar
        def _(act):
            def ahead(t, par):
                act.wait_ge(s["poly_ready"], t + 1)
                act.activation(tanh_y[:, :], poly[:, :], ACT.Tanh, scale=GELU_S).then_inc(s["tanh_y_ready"], 1)
                act.wait_ge(s["in_loaded"], t * per_in + per_in)
                act.activation(sq_a[:, :], a_in[:, par, :], ACT.Square,
                               accum_out=ss[:, par, 0:1]).then_inc(s["sumsq_a"], 1)
                act.activation(tanh_g[:, :, :], g_in[:, par, :, :], ACT.Tanh, scale=0.5).then_inc(s["tanh_g_ready"], 1)

            def high_weights():
                act.wait_ge(s["out_in"], 16 * KD)
                act.wait_ge(s["gains"], 64)
                for k in range(KD):
                    act.activation(outw(w_hi)[:, k, :], outw(w_in)[:, k, :], ACT.Copy,
                                   scale=gain_out[:, k:k + 1]).then_inc(s["w_high"], 1)

            def body(t, par, has_prev, has_this, has_next):
                if has_this:
                    act.wait_ge(s["gT_ps"], t + 1)
                    act.activation(g_hi[:, :, :], TG[:, :], ACT.Copy, scale=0.5).then_inc(s["g_hi_ready"], 1)
                    act.wait_ge(s["g_hi_ready"], t + 1)
                    act.activation(g_bf[:, :, :], g_hi[:, :, :], ACT.Copy).then_inc(s["gT_sb"], 1)
                if is_step(t, 0):
                    high_weights()
                if has_prev:
                    act.wait_ge(s["cT_ps"], t)
                    for n, part in enumerate(HALVINGS):
                        act.activation(c_hi[:, 4 * n:4 * n + 4, :], TC[:, n * BANK:(n + 1) * BANK], ACT.Copy,
                                       scale=part).then_inc(s["c_hi_ready"], 1)
                    act.wait_ge(s["c_hi_ready"], t * 2)
                    act.activation(c_bf[:, :, :], c_hi[:, :, :], ACT.Copy).then_inc(s["cT_sb"], 1)
                if has_this:
                    act.wait_ge(s["pre_ready"], t + 1)
                    act.activation(tanh_p[:, :], pre[:, :], ACT.Tanh, scale=0.5).then_inc(s["tanh_p_ready"], 1)
                if has_next:
                    ahead(t + 1, 1 - par)
                if has_this:
                    act.wait_ge(s["ssm_ready"], t + 1)
                    act.wait_ge(s["sumsq_a"], t + 1)
                    act.activation(sq_s[:, :], ssm[:, :], ACT.Square,
                                   accum_out=ss[:, par, 1:2]).then_inc(s["sumsq"], 1)
                if has_prev:
                    act.wait_ge(s["o_ps"], t)
                    if is_step(t, TILES):
                        act.wait_ge(s["out_ready"], t - 1)
                    act.activation(sq_o[:, :], OUT[1 - par][:, :], ACT.Square, accum_out=ss_o[:, :]).then_inc(s["sumsq_o"], 1)

            ahead(0, 0)
            act.wait_ge(s["glu_in"], 16 * KS)
            act.activation(glu(w_hi), glu(w_in), ACT.Copy).then_inc(s["w_high"], 1)
            body(0, 0, False, True, True)
            with act.Fori(0, TILES // 2 - 1) as i:
                body(i * 2 + 1, 1, True, True, True)
                body(i * 2 + 2, 0, True, True, True)
            body(TILES - 1, 1, True, True, False)
            body(TILES, 0, True, False, False)

        @block.vector
        def _(dve):
            ch = Chain(dve, s["dve_chain"])

            def gelu_in(t, par):
                dve.wait_ge(s["in_loaded"], t * per_in + per_in)
                y = y_in[:, par, :]
                ch.link(dve.tensor_tensor(poly[:, :], y, y, ALU.mult))
                ch.link(dve.tensor_scalar(poly[:, :], poly[:, :], GELU_A, 1.0, ALU.mult, ALU.add))
                dve.tensor_tensor(poly[:, :], poly[:, :], y, ALU.mult).then_inc(s["poly_ready"], 1)

            def gelu_out(t, par):
                if not is_step(t, 0):
                    dve.wait_ge(s["ssm_ready"], t)
                dve.wait_ge(s["tanh_y_ready"], t + 1)
                dve.scalar_tensor_tensor(gelu[:, :], tanh_y[:, :], 1.0, y_in[:, par, :], ALU.add, ALU.mult).then_inc(s["gelu_ready"], 1)

            def gates(t, par):
                dve.wait_ge(s["tanh_g_ready"], t + 1)
                dve.scalar_tensor_tensor(silu[:, par, :, :], tanh_g[:, :, :], 1.0, g_in[:, par, :, :],
                                         ALU.add, ALU.mult).then_inc(s["silu_ready"], 1)

            def low_gelu(t):
                dve.wait_ge(s["g_hi_ready"], t + 1)
                dve.scalar_tensor_tensor(g_lo[:, :, :], TG[:, :].rearrange("p (k c) -> p k c", k=KS), 0.5, g_hi[:, :, :],
                                         ALU.mult, ALU.subtract).then_inc(s["gT_sb"], 1)

            def low_cat(t):
                for n, part in enumerate(HALVINGS):
                    dve.wait_ge(s["c_hi_ready"], t * 2 + (n + 1))
                    dve.scalar_tensor_tensor(c_lo[:, 4 * n:4 * n + 4, :], TC[:, n * BANK:(n + 1) * BANK].rearrange("p (k c) -> p k c", k=4),
                                             part, c_hi[:, 4 * n:4 * n + 4, :], ALU.mult, ALU.subtract).then_inc(s["cT_sb"], 1)

            def bias(t):
                dve.wait_ge(s["gl_ps"], t + 1)
                dve.tensor_tensor(pre[:, :], GL[:, :], b_glu[:, :], ALU.add).then_inc(s["pre_ready"], 1)

            def unit(t):
                dve.wait_ge(s["tanh_p_ready"], t + 1)
                dve.scalar_tensor_tensor(ssm[:, :], tanh_p[:, :], 1.0, gelu[:, :], ALU.add, ALU.mult).then_inc(s["ssm_ready"], 1)

            def join(t, par, has_prev):
                dve.wait_ge(s["sumsq"], t + 1)
                dve.tensor_scalar(ss[:, par, 0:1], ss[:, par, 0:1], 1.0 / ATTN_W, EPS, ALU.mult, ALU.add)
                ch.link(dve.tensor_scalar(ss[:, par, 1:2], ss[:, par, 1:2], 1.0 / (16 * SSM_W), EPS, ALU.mult, ALU.add))
                rsqrt(dve, ch, rstd[:, :], ss[:, par, :], nt[:, :])
                dve.wait_ge(s["silu_ready"], t + 1)
                if has_prev:
                    dve.wait_ge(s["cT_ps"], t)
                dve.scalar_tensor_tensor(cat[:, 0, :], a_in[:, par, :], rstd[:, 0:1], silu[:, par, 0, :], ALU.mult, ALU.mult)
                dve.scalar_tensor_tensor(cat[:, 1, :], ssm[:, :], rstd[:, 1:2], silu[:, par, 1, :],
                                         ALU.mult, ALU.mult).then_inc(s["cat_ready"], 1)

            def last_norm(t, par, reused):
                dve.wait_ge(s["sumsq_o"], t + 1)
                inv_rms(dve, ch, rstd_o[:, :], ss_o[:, :], nt_o[:, :], D, EPS)
                ch.link(dve.scalar_tensor_tensor(o_n[:, :], OUT[par][:, :], rstd_o[:, :], gain_post[:, :], ALU.mult, ALU.mult))
                dve.wait_ge(s["x_loaded"], t * 16 + 16)
                if reused:
                    dve.wait_ge(s["out_stored"], t * 16 - 16)
                dve.tensor_tensor(out[:, par, :], o_n[:, :], x2[:, par, :], ALU.add).then_inc(s["out_ready"], 1)

            def low_weights():
                for k in range(KD):
                    dve.wait_ge(s["w_high"], k + 2)
                    dve.scalar_tensor_tensor(outw(w_lo)[:, k, :], outw(w_in)[:, k, :], gain_out[:, k:k + 1], outw(w_hi)[:, k, :],
                                             ALU.mult, ALU.subtract).then_inc(s["w_low"], 1)

            def body(t, par, has_prev, has_next, has_two, reused):
                low_gelu(t)
                if has_prev:
                    low_cat(t - 1)
                if has_two:
                    last_norm(t - 2, par, reused)
                bias(t)
                if is_step(t, 0):
                    low_weights()
                if has_next:
                    gelu_in(t + 1, 1 - par)
                unit(t)
                if has_next:
                    gelu_out(t + 1, 1 - par)
                    gates(t + 1, 1 - par)
                join(t, par, has_prev)

            gelu_in(0, 0)
            gelu_out(0, 0)
            gates(0, 0)
            dve.wait_ge(s["gains"], 64)
            dve.wait_ge(s["w_high"], 1)
            dve.tensor_tensor(glu(w_lo), glu(w_in), glu(w_hi), ALU.subtract).then_inc(s["w_low"], 1)
            body(0, 0, False, True, False, False)
            body(1, 1, True, True, False, False)
            body(2, 0, True, True, True, False)
            base = ch.n
            body(3, 1, True, True, True, False)
            per = ch.n - base
            body(4, 0, True, True, True, True)
            with dve.Fori(2, TILES // 2 - 1) as i:
                ch.start(i * (2 * per) + (base - 2 * per))
                body(i * 2 + 1, 1, True, True, True, True)
                body(i * 2 + 2, 0, True, True, True, True)
                assert ch.n == 2 * per, ch.n
            ch.start(base + (TILES - 4) * per)
            body(TILES - 1, 1, True, False, True, True)
            low_cat(TILES - 1)
            last_norm(TILES - 2, 0, True)
            last_norm(TILES - 1, 1, True)

        @block.tensor
        def _(pe):
            pe.wait_ge(s["ident_ready"], 1)

            def body(t, par, has_prev, has_this, reused):
                if has_this:
                    pe.wait_ge(s["gelu_ready"], t + 1)
                    for k in range(KS):
                        mm = pe.transpose(TG[:, k * P:(k + 1) * P], gelu[:, k * P:(k + 1) * P], ident[:, :])
                    mm.then_inc(s["gT_ps"], 1)
                if has_prev:
                    pe.wait_ge(s["cat_ready"], t)
                    for k in range(KD):
                        mm = pe.transpose(TC[:, k * P:(k + 1) * P], cat[:, k // KS, k % KS * P:(k % KS + 1) * P], ident[:, :])
                    mm.then_inc(s["cT_ps"], 1)
                if has_this:
                    if is_step(t, 0):
                        pe.wait_ge(s["w_low"], 1)
                    pe.wait_ge(s["gT_sb"], t * 2 + 2)
                    if has_prev:
                        pe.wait_ge(s["pre_ready"], t)
                    split_product(pe, GL[:, :], lambda k: g_hi[:, k, :], lambda k: g_lo[:, k, :], lambda k: g_bf[:, k, :],
                                  lambda k: glu(w_hi)[:, k, :], lambda k: glu(w_lo)[:, k, :], range(KS), 0, KS - 1).then_inc(s["gl_ps"], 1)
                if has_prev:
                    if is_step(t, 1):
                        pe.wait_ge(s["w_low"], 1 + KD)
                    pe.wait_ge(s["cT_sb"], t * 3)
                    if reused:
                        pe.wait_ge(s["out_ready"], t - 2)
                    for n in range(2):
                        cols = slice(n * BANK, (n + 1) * BANK)
                        mm = split_product(pe, OUT[1 - par][:, cols], lambda k: c_hi[:, k, :], lambda k: c_lo[:, k, :],
                                           lambda k: c_bf[:, k, :], lambda k: outw(w_hi)[:, k, cols],
                                           lambda k: outw(w_lo)[:, k, cols], range(KD), 0, KD - 1)
                    mm.then_inc(s["o_ps"], 1)

            body(0, 0, False, True, False)
            body(1, 1, True, True, False)
            body(2, 0, True, True, False)
            with pe.Fori(1, TILES // 2 - 1) as i:
                body(i * 2 + 1, 1, True, True, True)
                body(i * 2 + 2, 0, True, True, True)
            body(TILES - 1, 1, True, True, True)
            body(TILES, 0, True, False, True)


def two_blocks(nc, I, out):
    with ExitStack() as ctx:
        sb = lambda name, shape, dt: ctx.enter_context(nc.sbuf_tensor(name, shape, dt))
        dram = lambda name, shape, dt=F32: nc.dram_tensor(name, shape, dt, kind="Internal").ap()
        S = {
            "keep": ctx,
            "pos": sb("pos", [P, TILES * TOPK], I32),
            "gates": sb("gates", [P, TILES * TOPK], F32),
            "starts": sb("starts", [P, E + 1], I32),
            "n_tiles": sb("n_tiles", [P, E], I32),
            "n_more": sb("n_more", [P, E], I32),
            "last": sb("last", [P, E], I32),
            "h1": dram("h1", [SEQ, D]),
            "hn": dram("hn", [SEQ, D]),
            "tok_list": dram("tok_list", [E * CAP, 1], I32),
            "y": dram("expert_rows", [MAX_TILES * P, D]),
            "x2": dram("x2", [SEQ, D]),
            "z": dram("z", [SEQ, Z_COLS]),
            "attn": dram("attn", [SEQ, ATTN_W]),
            "ssm": dram("ssm", [SEQ, SSM_W]),
            "out": out[0],
        }
        mixer_phase(nc, I, S)
        expert_phase(nc, I, S)
        combine_phase(nc, I, S)
        attention_phase(nc, I, S)
        s5_phase(nc, I, S)
        output_phase(nc, I, S)


def kernel(**inputs):
    import numpy as _np
    import concourse.bacc as _bacc
    from concourse import mybir as _mybir
    from concourse.bass_utils import run_bass_kernel_spmd as _run

    nc = _bacc.Bacc("TRN2", target_bir_lowering=False, num_devices=1)
    arrays, args = {}, {}
    for name, value in inputs.items():
        a = _np.ascontiguousarray(value)
        arrays[f"in_{name}_dram"] = a
        args[name] = nc.dram_tensor(f"in_{name}_dram", a.shape, _mybir.dt.from_np(a.dtype), kind="ExternalInput").ap()
    out = nc.dram_tensor("out_dram", (1, SEQ, D), _mybir.dt.float32, kind="ExternalOutput").ap()
    two_blocks(nc, args, out)
    r = _run(nc, [arrays], core_ids=[0])
    return r.results[0]["out_dram"]
```
